# Optimizing a Trainium2 kernel written in Bass

```python
import jax, jax.numpy as jnp
from jax import lax
import numpy as np

D_MODEL = 1024
BATCH = 1
SEQ = 512
DEPTH = 1

D_MIX = D_MODEL
RET_HEADS = 4
RET_WIDTH = D_MIX // 2
RET_HEAD_DIM = RET_WIDTH // RET_HEADS
RET_CHUNK = 128
ROPE_BASE = 10000.0
SGU_GROUPS = 4
SGU_WIDTH = D_MIX - RET_WIDTH
SGU_GROUP_DIM = SGU_WIDTH // SGU_GROUPS
SGU_CHUNK = 128
IN_COLS = 4 * RET_WIDTH + 2 * SGU_WIDTH
N_EXPERT_GROUPS = 4
EXPERTS_PER_GROUP = 8
TOP_K = 2
EXPERT_FF = D_MODEL // 4
ROUTER_BIAS_SCALE = 0.01
EPS = 1e-6

kernel_name = 'hybrid_retention_sgu_hmoe_block'

def rmsnorm(x, gain):
    x32 = x.astype(jnp.float32)
    y = x32 * lax.rsqrt(jnp.mean(x32 * x32, axis=-1, keepdims=True) + EPS)
    return (y * gain.astype(jnp.float32)).astype(x.dtype)

def rotary(x, positions):
    d = x.shape[-1]
    half = d // 2
    inv_freq = ROPE_BASE ** (-jnp.arange(half, dtype=jnp.float32) * 2.0 / d)
    ang = positions.astype(jnp.float32)[:, :, None, None] * inv_freq
    cos, sin = jnp.cos(ang), jnp.sin(ang)
    x32 = x.astype(jnp.float32)
    x1, x2 = x32[..., :half], x32[..., half:]
    return jnp.concatenate([x1 * cos - x2 * sin, x1 * sin + x2 * cos], axis=-1)

def retention(q, k, v, gate, positions, gn_gain):
    out_dtype = gate.dtype
    B, S, _ = q.shape
    H, dh, C = RET_HEADS, RET_HEAD_DIM, RET_CHUNK
    N = S // C
    q = rotary(q.reshape(B, S, H, dh), positions)
    k = rotary(k.reshape(B, S, H, dh), positions) * (dh ** -0.5)
    v = v.reshape(B, S, H, dh).astype(jnp.float32)
    log_gamma = jnp.log(1.0 - 2.0 ** (-5.0 - jnp.arange(H, dtype=jnp.float32)))
    idx = jnp.arange(C, dtype=jnp.float32)
    diff = idx[:, None] - idx[None, :]
    decay_intra = jnp.where(diff >= 0.0,
                            jnp.exp(log_gamma[:, None, None] * jnp.maximum(diff, 0.0)), 0.0)
    qc = q.reshape(B, N, C, H, dh)
    kc = k.reshape(B, N, C, H, dh)
    vc = v.reshape(B, N, C, H, dh)
    scores = jnp.einsum('bnihd,bnjhd->bnhij', qc, kc) * decay_intra
    intra = jnp.einsum('bnhij,bnjhe->bnihe', scores, vc)
    k_decay = jnp.exp(log_gamma[:, None] * (C - 1.0 - idx))
    kv = jnp.einsum('bnjhd,hj,bnjhe->nbhde', kc, k_decay, vc)
    chunk_decay = jnp.exp(log_gamma * C)[None, :, None, None]

    def step(state, kv_n):
        return state * chunk_decay + kv_n, state

    _, state_prev = lax.scan(step, jnp.zeros((B, H, dh, dh), jnp.float32), kv)
    q_decay = jnp.exp(log_gamma[:, None] * (idx + 1.0))
    cross = jnp.einsum('bnihd,nbhde,hi->bnihe', qc, state_prev, q_decay)
    o = (intra + cross).reshape(B, S, H, dh)
    mu = jnp.mean(o, axis=-1, keepdims=True)
    var = jnp.mean(jnp.square(o - mu), axis=-1, keepdims=True)
    o = ((o - mu) * lax.rsqrt(var + EPS)).reshape(B, S, RET_WIDTH) * gn_gain.astype(jnp.float32)
    return (jax.nn.silu(gate.astype(jnp.float32)) * o).astype(out_dtype)

def spatial_gating(u, v, w_s, b_s, norm_gain):
    B, S, _ = u.shape
    G, dg, C = SGU_GROUPS, SGU_GROUP_DIM, SGU_CHUNK
    N = S // C
    v32 = v.astype(jnp.float32).reshape(B, N, C, G, dg)
    v32 = v32 * lax.rsqrt(jnp.mean(v32 * v32, axis=-1, keepdims=True) + EPS)
    v32 = v32 * norm_gain.astype(jnp.float32).reshape(G, dg)
    causal = jnp.tril(jnp.ones((C, C), jnp.float32))
    w = w_s.astype(jnp.float32) * causal
    s = jnp.einsum('gij,bnjgc->bnigc', w, v32) + b_s.astype(jnp.float32).T[None, None, :, :, None]
    out = u.astype(jnp.float32).reshape(B, N, C, G, dg) * s
    return out.reshape(B, S, SGU_WIDTH).astype(u.dtype)

def hierarchical_moe(h, w_rg, b_rg, w_re, b_re, w_gate_up, w_up, w_down):
    B, S, D = h.shape
    T = B * S
    G, E = N_EXPERT_GROUPS, EXPERTS_PER_GROUP
    t = h.reshape(T, D)
    t32 = t.astype(jnp.float32)
    group_logits = t32 @ w_rg.astype(jnp.float32) + b_rg.astype(jnp.float32)
    group_prob = jax.nn.softmax(group_logits, axis=-1)
    gsel = jax.nn.one_hot(jnp.argmax(group_logits, axis=-1), G, dtype=jnp.float32)
    gweight = jnp.sum(group_prob * gsel, axis=-1)
    exp_logits = jnp.einsum('td,gde->tge', t32, w_re.astype(jnp.float32)) + b_re.astype(jnp.float32)
    sel_logits = jnp.sum(exp_logits * gsel[:, :, None], axis=1)
    top_v, top_i = lax.top_k(sel_logits, TOP_K)
    top_w = jax.nn.softmax(top_v, axis=-1)
    ew = jnp.sum(jax.nn.one_hot(top_i, E, dtype=jnp.float32) * top_w[..., None], axis=1)
    gates = (gweight[:, None] * gsel)[:, :, None] * ew[:, None, :]
    y = jnp.zeros((T, D), jnp.float32)
    for g in range(G):
        a = jnp.einsum('td,edf->tef', t, w_gate_up[g])
        b = jnp.einsum('td,edf->tef', t, w_up[g])
        act = jax.nn.silu(a) * b * gates[:, g, :, None].astype(a.dtype)
        y = y + jnp.einsum('tef,efd->td', act, w_down[g]).astype(jnp.float32)
    return y.reshape(B, S, D).astype(h.dtype)

def setup_inputs(seed: int = 0) -> dict:
    key = jax.random.key(seed)
    ks = jax.random.split(key, 17)
    G, E, F = N_EXPERT_GROUPS, EXPERTS_PER_GROUP, EXPERT_FF
    nrm = jax.random.normal
    return {
        'x': nrm(ks[0], (BATCH, SEQ, D_MODEL), jnp.float32),
        'positions': jnp.broadcast_to(jnp.arange(SEQ, dtype=jnp.int32), (BATCH, SEQ)),
        'norm_mix_gain': 1.0 + 0.02 * nrm(ks[1], (DEPTH, D_MODEL), jnp.float32),
        'w_in': nrm(ks[2], (DEPTH, D_MODEL, IN_COLS), jnp.float32) * D_MODEL ** -0.5,
        'ret_gn_gain': 1.0 + 0.02 * nrm(ks[3], (DEPTH, RET_WIDTH), jnp.float32),
        'sgu_norm_gain': 1.0 + 0.02 * nrm(ks[4], (DEPTH, SGU_WIDTH), jnp.float32),
        'sgu_w': nrm(ks[5], (DEPTH, SGU_GROUPS, SGU_CHUNK, SGU_CHUNK), jnp.float32) * SGU_CHUNK ** -0.5,
        'sgu_b': 1.0 + 0.1 * nrm(ks[6], (DEPTH, SGU_GROUPS, SGU_CHUNK), jnp.float32),
        'w_out': nrm(ks[7], (DEPTH, D_MIX, D_MODEL), jnp.float32) * D_MIX ** -0.5,
        'norm_ffn_gain': 1.0 + 0.02 * nrm(ks[8], (DEPTH, D_MODEL), jnp.float32),
        'w_router_group': nrm(ks[9], (DEPTH, D_MODEL, G), jnp.float32) * D_MODEL ** -0.5,
        'b_router_group': ROUTER_BIAS_SCALE * nrm(ks[10], (DEPTH, G), jnp.float32),
        'w_router_expert': nrm(ks[11], (DEPTH, G, D_MODEL, E), jnp.float32) * D_MODEL ** -0.5,
        'b_router_expert': ROUTER_BIAS_SCALE * nrm(ks[12], (DEPTH, G, E), jnp.float32),
        'w_expert_gate_up': nrm(ks[13], (DEPTH, G, E, D_MODEL, F), jnp.float32) * D_MODEL ** -0.5,
        'w_expert_up': nrm(ks[14], (DEPTH, G, E, D_MODEL, F), jnp.float32) * D_MODEL ** -0.5,
        'w_expert_down': nrm(ks[15], (DEPTH, G, E, F, D_MODEL), jnp.float32) * F ** -0.5,
        'final_norm_gain': 1.0 + 0.02 * nrm(ks[16], (D_MODEL,), jnp.float32),
    }

def reference(x, positions, norm_mix_gain, w_in, ret_gn_gain, sgu_norm_gain, sgu_w, sgu_b, w_out,
              norm_ffn_gain, w_router_group, b_router_group, w_router_expert, b_router_expert,
              w_expert_gate_up, w_expert_up, w_expert_down, final_norm_gain):
    R, U = RET_WIDTH, SGU_WIDTH
    splits = [R, 2 * R, 3 * R, 4 * R, 4 * R + U]
    for l in range(DEPTH):
        h = rmsnorm(x, norm_mix_gain[l])
        proj = h @ w_in[l]
        q, k, v, gate, u, vs = jnp.split(proj, splits, axis=-1)
        ret = retention(q, k, v, gate, positions, ret_gn_gain[l])
        sgu = spatial_gating(jax.nn.gelu(u, approximate=False), jax.nn.gelu(vs, approximate=False),
                             sgu_w[l], sgu_b[l], sgu_norm_gain[l])
        x = x + jnp.concatenate([ret, sgu], axis=-1) @ w_out[l]
        x = x + hierarchical_moe(rmsnorm(x, norm_ffn_gain[l]), w_router_group[l], b_router_group[l],
                                 w_router_expert[l], b_router_expert[l], w_expert_gate_up[l],
                                 w_expert_up[l], w_expert_down[l])
    return rmsnorm(x, final_norm_gain)


_drawn_inputs = setup_inputs


def setup_inputs(seed=0):
    import zlib

    import numpy as np

    out = dict(_drawn_inputs(seed))
    spreads = {}
    factors = {'ret_gn_gain': 8.933,
     'sgu_norm_gain': 11.403,
     'b_router_group': 11.735,
     'b_router_expert': 18.801,
     'final_norm_gain': 8.176,
     'norm_ffn_gain': 2.748}
    for name, (base, spread) in spreads.items():
        noise = np.random.default_rng([zlib.crc32(name.encode()), seed]).standard_normal(out[name].shape)
        drawn = base * np.exp(spread * noise) if base else spread * noise
        out[name] = __import__('jax').numpy.asarray(drawn.astype(out[name].dtype))
    for name, factor in factors.items():
        out[name] = (out[name] * factor).astype(out[name].dtype)
    return out
```

```python
from contextlib import ExitStack

import numpy as np

import concourse.bass as bass
from concourse import mybir

P = 128
F32 = mybir.dt.float32
F32R = mybir.dt.float32r
F16 = mybir.dt.float16
I32 = mybir.dt.int32
U32 = mybir.dt.uint32
ALU = mybir.AluOpType
ACT = mybir.ActivationFunctionType
AX = mybir.AxisListType.X

D = 1024
S = 512
NT = S // P
ND = D // P
H = 4
DH = 128
HALF = DH // 2
R = H * DH
NB_IN = 6
NB = NB_IN + 2
G = 4
EPG = 8
NE = G * EPG
FF = 256
NF = FF // P
TOPK = 2
WIN = 64
SLOTS = TOPK * S
NS = SLOTS // P
TRASH = SLOTS + WIN
NWIN = S // WIN
EPS = 1e-6
ROPE_BASE = 10000.0
NEG = -3.0e38
MAGIC = 1.5 * 2.0 ** 23
PI_BELOW = 3.1415925
TWO_PI = (6.28125, 4059 * 2.0 ** -21, 2 * np.pi - 6.28125 - 4059 * 2.0 ** -21)

RAW = 4
RING = 4
XS = 4
SMALL = 16 * 13

BLOCK_COL = [1, 0, 2, 5, 4, 3]
KB, QB, VB, VSB, UB, GB = range(6)
STEPS = [(b, k) for b in range(NB_IN) for k in range(ND)] + \
        [(NB_IN + c, k) for c in range(2) for k in (4, 5, 6, 7, 0, 1, 2, 3)]
NSTEP = len(STEPS)

C_ID, C_CAUSAL, C_BEFORE, C_ONES = 0, 128, 256, 384
C_QD, C_KD, C_CD, C_FREQ, C_I32, C_TOK, C_EPS = 512, 516, 520, 524, 588, 620, 624
C_N = 640


def constants():
    c = np.zeros((P, C_N), np.float32)
    i = np.arange(P, dtype=np.float64)
    c[:, C_ID:C_ID + P] = np.eye(P)
    c[:, C_CAUSAL:C_CAUSAL + P] = i[:, None] <= i[None, :]
    c[:, C_BEFORE:C_BEFORE + P] = i[:, None] < i[None, :]
    c[:, C_ONES:C_ONES + P] = 1.0
    gamma = 1.0 - 2.0 ** (-5.0 - np.arange(H))
    c[:, C_QD:C_QD + H] = gamma[None, :] ** (i[:, None] + 1)
    c[:, C_KD:C_KD + H] = gamma[None, :] ** -(i[:, None] + 1) * DH ** -0.5
    c[:, C_CD:C_CD + H] = gamma[None, :] ** P
    c[:, C_FREQ:C_FREQ + HALF] = ROPE_BASE ** (-np.arange(HALF) * 2.0 / DH)
    c[:, C_I32:C_I32 + NE] = np.arange(NE)
    c[:, C_TOK:C_TOK + NT] = i[:, None] + P * np.arange(NT)
    c[:, C_EPS] = EPS
    h = np.zeros((P, SLOTS + NT), np.float16)
    h[:, :SLOTS] = np.arange(SLOTS)
    h[:, SLOTS:] = i[:, None] + P * np.arange(NT)
    return c, h



class Banks:

    def __init__(self, banks, full, read):
        self.banks, self.full, self.read, self.order = banks, full, read, {}

    def add(self, item):
        self.order[item] = len(self.order)

    def turn(self, item):
        return self.order[item] % len(self.banks), self.order[item] // len(self.banks)

    def bank(self, item):
        return self.banks[self.turn(item)[0]]

    def filled(self, item):
        return self.full[self.turn(item)[0]]

    def done(self, item):
        return self.read[self.turn(item)[0]]

    def wait_free(self, eng, item):
        i, before = self.turn(item)
        if before:
            eng.wait_ge(self.read[i], before)

    def wait_full(self, eng, item):
        i, before = self.turn(item)
        eng.wait_ge(self.full[i], before + 1)

    def wait_read(self, eng, item):
        i, before = self.turn(item)
        eng.wait_ge(self.read[i], before + 1)


class Chain:

    def __init__(self, eng, sem):
        self.eng, self.sem, self.n = eng, sem, 0

    def __call__(self, ins):
        ins.then_inc(self.sem, 1)
        self.n += 1

    def settle(self):
        self.eng.wait_ge(self.sem, self.n)


INPUTS = ["x", "positions", "norm_mix_gain", "w_in", "ret_gn_gain", "sgu_norm_gain", "sgu_w", "sgu_b",
          "w_out", "norm_ffn_gain", "w_router_group", "b_router_group", "w_router_expert",
          "b_router_expert", "w_expert_gate_up", "w_expert_up", "w_expert_down", "final_norm_gain"]


def one_of(e, j):
    return slice(e + j, e + j + 1) if isinstance(e, int) else bass.ds(e + j, 1)


def flat(ap):
    return ap.rearrange("p a b c -> p (a b c)")


def build(nc, A, out):
    ctx = ExitStack()
    with ctx:
        at = {"next": 0}
        base = (nc.sbuf_base + 63) // 64 * 64

        def place(name, shape, dt, offset):
            return nc.alloc_sbuf_tensor_at("sb_" + name, list(shape), dt, offset=base + offset)

        def sb(name, shape, dt=F32):
            size = int(np.prod(shape[1:])) * (2 if dt == F16 else 4)
            t = place(name, shape, dt, at["next"])
            at["next"] += (size + 31) // 32 * 32
            return t

        def psum(name):
            return ctx.enter_context(nc.psum_tensor("ps_" + name, [P, 512], F32))

        def sem(name):
            return ctx.enter_context(nc.semaphore(name))

        KiB = 1024
        const = sb("const", [P, C_N])
        consth = sb("consth", [P, SLOTS + NT], F16)
        gmix = sb("gmix", [P, ND])
        bsgu = sb("bsgu", [P, G])
        brt = sb("brt", [P, G + NE])
        wrt = sb("wrt", [P, ND, G + NE])
        pos_i = sb("pos_i", [P, NT], I32)
        pos_f = sb("pos_f", [P, NT])
        stat = sb("stat", [P, 12, NT])
        gnstat = sb("gnstat", [P, NT, H, 6])
        gnaggr = sb("gnaggr", [P, NT, H, 2])
        gnrs = sb("gnrs", [P, 2, NT, H])
        vss = sb("vss", [P, 3, NT, G])
        actT = sb("actT", [P, 2, NF, WIN])
        silu_g = sb("silu_g", [P, 2, NF, WIN])
        offi = sb("offi", [P, NE + 1], I32)
        rd_i = sb("rd_i", [P, NE * NWIN], I32)
        wr_i = sb("wr_i", [P, NE * NWIN], I32)
        gsub = sb("gsub", [P, NT, G])
        esub = sb("esub", [P, NT])
        e2 = sb("e2", [P, NT])
        gden = sb("gden", [P, NT])
        eden = sb("eden", [P, NT])
        slot_of = sb("slot_of", [P, TOPK, NT], I32)
        tok_of = sb("tok_of", [P, NS], I32)
        gates = sb("gates", [P, TOPK, NT])
        wT = sb("wT", [P, G, P])
        gain_row = sb("gain_row", [P, D])
        trig = sb("trig", [P, 2, NT, HALF])
        sg_row = sb("sg_row", [P, R])
        gn_row = sb("gn_row", [P, R])
        wide = place("wide", [P, D], F32, at["next"] - 4 * KiB)
        kvt = sb("kvt", [P, H, DH])
        x = sb("x", [P, NT, D])

        arena = at["next"]
        hT_hi = place("hT_hi", [P, ND, S], F32R, arena)
        hT_lo = place("hT_lo", [P, ND, S], F32R, arena + 16 * KiB)
        mT_hi = place("mT_hi", [P, ND, S], F32R, arena)
        mT_lo = place("mT_lo", [P, ND, S], F32R, arena + 16 * KiB)
        w_raw = place("w_raw", [P, RAW, R], F32, arena + 32 * KiB)
        w_hi = place("w_hi", [P, RAW, R], F32R, arena + 40 * KiB)
        w_lo = place("w_lo", [P, RAW, R], F32R, arena + 48 * KiB)
        h2T = place("h2T", [P, ND, S], F32, arena)
        xs = place("xs", [P, XS, D], F32, arena)
        ysb = place("ysb", [WIN, 2, D], F32, arena + 8 * KiB)
        xsT_at = arena + 16 * KiB
        xsT = place("xsT", [P, ND, SLOTS + WIN], F32, xsT_at)
        onehot = place("onehot", [P, NT, SLOTS], F16, xsT_at)
        rt = xsT_at + 8 * KiB
        glog = place("glog", [P, NT, 8], F32, rt)
        gtop = place("gtop", [P, NT, 8], F32, rt + 128)
        gidx = place("gidx", [P, NT, 8], U32, rt + 256)
        elog = place("elog", [P, NT, G, EPG], F32, rt + 384)
        emul = place("emul", [P, NT, G, EPG], F32, rt + 896)
        slog = place("slog", [P, NT, EPG], F32, rt + 1408)
        etop = place("etop", [P, NT, 8], F32, rt + 1536)
        eidx = place("eidx", [P, NT, 8], U32, rt + 1664)
        gid = place("gid", [P, NT], F32, rt + 1792)
        gsel = place("gsel", [P, NT, G], F32, rt + 1824)
        gexp = place("gexp", [P, NT, G], F32, rt + 1888)
        eid = place("eid", [P, TOPK, NT], F32, rt + 1952)
        pairs = place("pairs", [P, TOPK, NT, NE], F32, rt + 1984)
        picked = place("picked", [P, NT, NE], F32, rt + 3008)
        slots = place("slots", [P, NT, NE], F32, rt + 3520)
        spick = place("spick", [P, TOPK, NT, NE], F32, rt + 4032)
        slot_f = place("slot_f", [P, TOPK, NT], F32, rt + 5056)
        cnt = place("cnt", [P, 4, NE], F32, rt + 5088)
        wtab = place("wtab", [P, 3, NE, NWIN], F32, rt + 5632)
        h2 = place("h2", [P, NT, D], F32, xsT_at + 34 * KiB)
        at["next"] = arena + 66 * KiB
        ring = at["next"]
        slot_size = 24 * KiB
        wg = [place(f"wg{i}", [P, ND, FF], F32, ring + slot_size * i) for i in range(RING)]
        wu = [place(f"wu{i}", [P, ND, FF], F32, ring + slot_size * i + 8 * KiB) for i in range(RING)]
        wd = [place(f"wd{i}", [P, NF, D], F32, ring + slot_size * i + 16 * KiB) for i in range(RING)]
        rows = ring + slot_size
        krow = place("krow", [P, NT, H, DH], F32, rows)
        vrow = place("vrow", [P, NT, H, DH], F32, rows + 8 * KiB)
        kT = place("kT", [P, H, S], F32, rows + 16 * KiB)
        qT = place("qT", [P, H, S], F32, rows + 24 * KiB)
        orow = place("orow", [P, NT, H, DH], F32, rows + 32 * KiB)
        grow = place("grow", [P, NT, R], F32, rows + 40 * KiB)
        urow = place("urow", [P, NT, R], F32, rows + 48 * KiB)
        vsrow = place("vsrow", [P, NT, R], F32, rows + 56 * KiB)
        state = place("state", [P, 2, H, DH], F32, rows + 64 * KiB)
        scT = place("scT", [P, 2, H, DH], F32, rows + 68 * KiB)
        hrow = place("hrow", [P, 2, D], F32, rows + 32 * KiB)
        rot = place("rot", [P, 2, 2, H, DH], F32, rows + 40 * KiB)
        qrow = place("qrow", [P, NT, H, DH], F32, rows + 48 * KiB)
        vsq = place("vsq", [P, NT, G, P], F32, rows + 48 * KiB)
        junk = place("junk", [P, D], F32, rows + 56 * KiB)
        wsraw = place("wsraw", [P, G, P], F32, rows + 60 * KiB)
        ang = place("ang", [P, 2, 2, NT, HALF], F32, rows)
        gy = place("gy", [P, TOPK, NT, D], F32, ring)
        outrow = place("outrow", [P, NT, D], F32, ring + 48 * KiB)
        junk2 = place("junk2", [P, D], F32, ring + 64 * KiB)
        at["next"] = ring + RING * slot_size
        assert base + at["next"] <= nc.sbuf_usable_end, (base + at["next"], nc.sbuf_usable_end)

        orow_flat = orow[:].rearrange("p t h d -> p t (h d)")
        vsrow4 = vsrow[:].rearrange("p t (g c) -> p t g c", g=G)
        bk = [psum(f"bank{i}") for i in range(8)]

        h2_rows = nc.dram_tensor("h2_rows", [S, D], F32).ap()
        y_rows = nc.dram_tensor("y_rows", [TRASH + WIN, D], F32).ap()

        s_x = [sem(f"x_loaded{t}") for t in range(NT)]
        s_const = sem("constants_loaded")
        s_small = sem("small_inputs_loaded")
        s_sgw = sem("sgu_w_loaded")
        s_gain = sem("row_gain_loaded")
        s_raw = [sem(f"w_raw_loaded{i}") for i in range(RAW)]
        s_whi = sem("w_high_made")
        s_wlo = sem("w_low_made")
        s_step = sem("dense_step_done")
        s_ss = sem("squares_summed")
        s_sd = sem("deviation_made")
        s_h = sem("normalised_rows_made")
        s_thi = sem("transposed_high_made")
        s_ang = sem("angles_reduced")
        s_trig = sem("sin_cos_made")
        s_rot = sem("rotated_rows_made")
        s_vsq = sem("gating_squares_made")
        s_vss = sem("gating_sums_made")
        s_vsd = sem("gating_deviation_made")
        s_vn = sem("gating_v_scaled")
        s_vg = sem("gating_v_normalised")
        s_gnv = sem("retention_variance_made")
        s_gnd = sem("retention_deviation_made")
        s_on = sem("retention_normalised")
        s_og = sem("retention_gained")
        s_mix = sem("retention_mix_made")
        s_h2 = sem("ffn_rows_made")
        s_h2out = sem("ffn_rows_stored")
        s_arg = sem("softmax_arguments_made")
        s_exp = sem("softmax_exponentials_made")
        s_pick = sem("pairs_picked")
        s_tabs = sem("window_tables_made")
        s_slot = sem("slots_made")
        s_hot = sem("slot_one_hots_made")
        s_xs = [sem(f"sorted_rows_gathered{i}") for i in range(XS)]
        s_pad = sem("window_padding_cleared")
        s_auxf = [sem(f"aux_bank_full{i}") for i in range(2)]
        s_auxr = [sem(f"aux_bank_read{i}") for i in range(2)]
        s_mainf = [sem(f"main_bank_full{i}") for i in range(6)]
        s_mainr = [sem(f"main_bank_read{i}") for i in range(6)]
        s_wgu = [sem(f"gate_up_weights_loaded{i}") for i in range(RING)]
        s_wd = [sem(f"down_weights_loaded{i}") for i in range(RING)]
        s_gu = sem("gate_up_done")
        s_silu = sem("silu_made")
        s_act = sem("activation_made")
        s_down = sem("down_done")
        s_yl = sem("expert_rows_left_half_made")
        s_yr = sem("expert_rows_right_half_made")
        s_yout = sem("expert_rows_stored")
        g_w = sem("general_weights_loaded")
        g_gu = sem("general_gate_up_done")
        g_silu = sem("general_silu_made")
        g_act = sem("general_activation_made")
        g_down = sem("general_down_done")
        g_yl = sem("general_rows_left_half_made")
        g_yr = sem("general_rows_right_half_made")
        g_yout = sem("general_rows_stored")
        s_gy = [sem(f"pair_rows_gathered{i}") for i in range(NT)]
        s_x2 = sem("experts_added")
        s_out = sem("rows_finished")
        s_stored = sem("output_stored")
        c_act = sem("scalar_own_results")
        c_dve = sem("vector_own_results")
        c_pool = sem("pool_own_results")

        main = Banks(bk[:6], s_mainf, s_mainr)
        for b in range(NB):
            for t in range(NT):
                main.add((b, t))
        beside = [(-1, ("hT", t, half)) for t in range(NT) for half in range(2)]
        beside += [(2, ("wT",))]
        beside += [(12 + t, ("kT", t)) for t in range(NT)]
        beside += [(20 + t, ("qT", t)) for t in range(NT)]
        for n in range(NT):
            beside += [(28 + 3 * n, ("scores", n)), (30 + 3 * n, ("o", n))]
            if n < NT - 1:
                beside += [(28 + 3 * n, ("kv", n))]
        beside += [(41 + t, ("gating", t)) for t in range(NT)]
        beside += [(47, ("mT", t, 1)) for t in range(NT)]
        beside += [(49, ("mT", t, 0)) for t in range(NT)]
        beside += [(NSTEP, ("h2T", t, half)) for t in range(NT) for half in range(2)]
        beside += [(NSTEP, ("logits",)), (NSTEP, ("ranks",)), (NSTEP, ("tokens",))]
        beside += [(NSTEP, ("xsT", s, half)) for s in range(NS) for half in range(2)]
        beside.sort(key=lambda entry: entry[0])
        aux = Banks(bk[6:], s_auxf, s_auxr)
        for _, item in beside:
            aux.add(item)

        def heads(bank):
            return bank[:, :].rearrange("p (h d) -> p h d", h=H)

        ident = const[:, C_ID:C_ID + P]
        causal = const[:, C_CAUSAL:C_CAUSAL + P]
        before = const[:, C_BEFORE:C_BEFORE + P]
        ones = const[:, C_ONES:C_ONES + P]
        pad = xsT[:, :, SLOTS:]

        def along(ap, n):
            return ap.unsqueeze(1).broadcast_to([P, n, ap.shape[1]])

        def spread(ap, n):
            return ap.unsqueeze(len(ap.shape)).broadcast_to([*ap.shape, n])

        w_gate = A["w_expert_gate_up"].rearrange("l g e (p k) f -> (l g e) p k f", p=P)
        w_up = A["w_expert_up"].rearrange("l g e (p k) f -> (l g e) p k f", p=P)
        w_down = A["w_expert_down"].rearrange("l g e (p j) n -> (l g e) p j n", p=P)

        def one(ap, e):
            return ap[bass.ds(e, 1)].squeeze(0) if not isinstance(e, int) else ap[e]

        block = ctx.enter_context(nc.Block())

        def at_least(eng, sem, i, mul, add):
            if isinstance(i, int):
                if mul * i + add > 0:
                    eng.wait_ge(sem, mul * i + add)
            else:
                eng.wait_ge(sem, i * mul + add)

        def group_loop(eng, group):
            group(0)
            with eng.Fori(1, NE // RING - 1) as r:
                group(r * RING)
            group(NE - RING)

        def if_crowded(eng):
            eng.wait_ge(s_tabs, 1)
            return eng.If(eng.value_load(offi[0:1, NE:NE + 1], min_val=0, max_val=1) >= 1)

        def gate_up_bank(j):
            return bk[j % 2][:, 0:2 * NF * WIN].rearrange("p (c w) -> p c w", w=WIN)

        def down_bank(j, c):
            return bk[2 + 2 * (j % 2) + c]

        def wait_step(eng, g):
            if g % ND == ND - 1:
                main.wait_full(eng, (STEPS[g][0], NT - 1))
            else:
                eng.wait_ge(s_step, g + 1 - g // ND)

        def tokens(t):
            return slice(t * P, (t + 1) * P)

        def half_rows(half):
            return slice(4 * half, 4 * half + 4)

        @block.sync
        def _(sp):
            for t in range(NT):
                sp.dma_start(x[:, t, :], A["x"][0, tokens(t), :]).then_inc(s_x[t], 16)

            def gate_up(slot, e, *sems):
                sp.dma_start(wg[slot][:], one(w_gate, e)).then_inc(sems[0], 16)
                sp.dma_start(wu[slot][:], one(w_up, e)).then_inc(sems[0], 16)

            def down(slot, e, sem):
                sp.dma_start(wd[slot][:], one(w_down, e)).then_inc(sem, 16)

            for g, (b, k) in enumerate(STEPS):
                if g >= RAW:
                    sp.wait_ge(s_whi, g - RAW + 1)
                    sp.wait_ge(s_wlo, g - RAW + 1)
                if b < NB_IN:
                    src = A["w_in"][0, tokens(k), BLOCK_COL[b] * R:(BLOCK_COL[b] + 1) * R]
                else:
                    src = A["w_out"][0, tokens(k), (b - NB_IN) * R:(b - NB_IN + 1) * R]
                sp.dma_start(w_raw[:, g % RAW, :], src).then_inc(s_raw[g % RAW], 16)
                if g == 8:
                    gate_up(0, 0, s_wgu[0])
                    down(0, 0, s_wd[0])
                if g == 57:
                    aux.wait_read(sp, ("mT", NT - 2, 0))
                    aux.wait_read(sp, ("mT", NT - 1, 0))
                    for slot in range(1, RING):
                        gate_up(slot, slot, s_wgu[slot])
                        down(slot, slot, s_wd[slot])
            for t in range(NT):
                sp.wait_ge(s_h2, t + 1)
                sp.dma_start(h2_rows[tokens(t), :], h2[:, t, :]).then_inc(s_h2out, 16)
            sp.dma_start(gain_row[:], A["final_norm_gain"].partition_broadcast(P)).then_inc(s_gain, 16)

            def group(i):
                for slot in range(RING):
                    at_least(sp, s_gu, i, 1, slot + 1)
                    gate_up(slot, i + (slot + RING), s_wgu[slot])
                    at_least(sp, s_down, i, 1, slot + 1)
                    down(slot, i + (slot + RING), s_wd[slot])

            group(0)
            with sp.Fori(1, NE // RING - 1) as r:
                group(r * RING)
            sp.wait_ge(s_down, NE)
            with if_crowded(sp):
                gate_up(0, 0, g_w)
                down(0, 0, g_w)
                with sp.Fori(1, NE) as e:
                    sp.wait_ge(g_down, e * NWIN)
                    gate_up(0, e, g_w)
                    down(0, e, g_w)
            for t in range(NT):
                sp.wait_ge(s_out, t + 1)
                sp.dma_start(out[0, tokens(t), :], outrow[:, t, :]).then_inc(s_stored, 16)
            sp.wait_ge(s_stored, 16 * NT)

        @block.scalar
        def _(act):
            small = [0]

            def load(dst, src, slow=False):
                act.dma_start(dst, src, allow_slow_non_contiguous=slow).then_inc(s_small, 16)
                small[0] += 16

            act.dma_start(const[:], A["constants"]).then_inc(s_const, 16)
            load(gmix[:], A["norm_mix_gain"].rearrange("a (k p) -> p (a k)", p=P), slow=True)
            act.dma_start(wsraw[:], A["sgu_w"].rearrange("a g i j -> i (a g) j")).then_inc(s_sgw, 16)
            load(pos_i[:], A["positions"].rearrange("a (t p) -> p (a t)", p=P), slow=True)
            load(bsgu[:], A["sgu_b"].rearrange("a g i -> i (a g)"), slow=True)
            load(sg_row[:], A["sgu_norm_gain"][0].partition_broadcast(P))
            load(gn_row[:], A["ret_gn_gain"][0].partition_broadcast(P))
            load(brt[:, 0:G], A["b_router_group"][0].partition_broadcast(P))
            load(brt[:, G:], A["b_router_expert"][0].rearrange("g e -> (g e)").partition_broadcast(P))
            load(wrt[:, :, 0:G], A["w_router_group"][0].rearrange("(p k) g -> p k g", p=P))
            for g in range(G):
                load(wrt[:, :, G + g * EPG:G + (g + 1) * EPG],
                     A["w_router_expert"][0, g].rearrange("(p k) e -> p k e", p=P))
            load(consth[:], A["constants_half"])
            act.dma_start(gain_row[:], A["norm_ffn_gain"][0].partition_broadcast(P)).then_inc(s_gain, 16)

            def sum_squares(t, kind, scratch):
                if NT * kind + t:
                    act.wait_ge(s_ss, NT * kind + t)
                act.activation(scratch, x[:, t, :], ACT.Square,
                               accum_out=stat[:, 3 * kind, t:t + 1]).then_inc(s_ss, 1)

            def deviation(kind):
                act.wait_ge(s_ss, NT * (kind + 1))
                act.activation(stat[:, 3 * kind + 1, :], stat[:, 3 * kind, :], ACT.Sqrt, scale=1.0 / D,
                               bias=const[:, C_EPS:C_EPS + 1]).then_inc(s_sd, 1)

            def w_high(g):
                b, k = STEPS[g]
                act.wait_ge(s_raw[g % RAW], 16 * (g // RAW + 1))
                if g >= RAW:
                    wait_step(act, g - RAW)
                    act.wait_ge(s_wlo, g - RAW + 1)
                act.activation(w_hi[:, g % RAW, :], w_raw[:, g % RAW, :], ACT.Copy,
                               scale=gmix[:, k:k + 1] if b < NB_IN else 1.0).then_inc(s_whi, 1)

            def read_aux(item, dst):
                aux.wait_full(act, item)
                act.activation(dst, heads(aux.bank(item)), ACT.Copy).then_inc(aux.done(item), 1)

            def transposed_high(name, dst, t, half):
                item = (name, t, half)
                aux.wait_full(act, item)
                act.activation(dst[:, half_rows(half), tokens(t)], heads(aux.bank(item)),
                               ACT.Copy).then_inc(s_thi, 1)

            def rows(b, dst, func):
                for t in range(NT):
                    main.wait_full(act, (b, t))
                    act.activation(dst[:, t, :], main.bank((b, t))[:, :], func
                                   ).then_inc(main.done((b, t)), 1)

            for t in range(NT):
                act.wait_ge(s_x[t], 16)
                sum_squares(t, 0, junk[:])
            act.wait_ge(s_const, 16)
            deviation(0)
            act.wait_ge(s_small, small[0])
            w_high(0)
            w_high(1)
            for t in range(NT):
                for half in range(2):
                    transposed_high("hT", hT_hi, t, half)
            act.wait_ge(s_ang, 1)
            act.activation(trig[:], ang[:, 0], ACT.Sin).then_inc(s_trig, 1)

            for g in range(2, NSTEP):
                w_high(g)
                if 16 <= g < 16 + NT:
                    read_aux(("kT", g - 16), kT[:, :, tokens(g - 16)])
                if 24 <= g < 24 + NT:
                    read_aux(("qT", g - 24), qT[:, :, tokens(g - 24)])
                if g == 27:
                    rows(VB, vrow[:].rearrange("p t h d -> p t (h d)"), ACT.Copy)
                if g >= 34 and (g - 34) % 3 == 0 and (g - 34) // 3 < NT:
                    n = (g - 34) // 3
                    read_aux(("o", n), orow[:, n])
                if g == 35:
                    rows(VSB, vsrow, ACT.Gelu)
                if g == 38:
                    act.wait_ge(s_vss, 1)
                    act.activation(vss[:, 1], vss[:, 0], ACT.Sqrt, scale=1.0 / P,
                                   bias=const[:, C_EPS:C_EPS + 1]).then_inc(s_vsd, 1)
                if g == 43:
                    rows(UB, urow, ACT.Gelu)
                if g == 46:
                    act.wait_ge(s_gnv, 1)
                    act.activation(gnrs[:, 0], gnaggr[:, :, :, 1], ACT.Sqrt,
                                   bias=const[:, C_EPS:C_EPS + 1]).then_inc(s_gnd, 1)
                if g == 51:
                    for t in range(NT):
                        transposed_high("mT", mT_hi, t, 1)
                    rows(GB, grow, ACT.Silu)
                if g == 52:
                    for t in range(NT):
                        transposed_high("mT", mT_hi, t, 0)

            for t in range(NT):
                main.wait_read(act, (NB - 1, t))
                sum_squares(t, 1, wide[:])
            deviation(1)
            for t in range(NT):
                read_aux(("h2T", t, 0), h2T[:, half_rows(0), tokens(t)])
            act.wait_ge(s_arg, 1)
            act.activation(gexp[:], gsub[:], ACT.Exp).then_inc(s_exp, 1)
            act.wait_ge(s_arg, 2)
            act.activation(e2[:], esub[:], ACT.Exp).then_inc(s_exp, 1)
            for s in range(NS):
                read_aux(("xsT", s, 0), xsT[:, half_rows(0), tokens(s)])

            def silu(e, j):
                at_least(act, s_gu, e, 1, j + 1)
                at_least(act, s_act, e, 1, j - 1)
                act.activation(silu_g[:, j % 2], gate_up_bank(j)[:, 0:NF, :], ACT.Silu
                               ).then_inc(s_silu, 1)

            def y_left(e, j):
                at_least(act, s_down, e, 1, j + 1)
                at_least(act, s_yout, e, 16, 16 * (j - 1))
                act.activation(ysb[:, j % 2, 0:R], down_bank(j, 0)[0:WIN, :], ACT.Copy
                               ).then_inc(s_yl, 1)

            def group(i):
                for j in range(RING):
                    if not (isinstance(i, int) and i + j + 1 >= NE):
                        silu(i, j + 1)
                    y_left(i, j)

            silu(0, 0)
            group_loop(act, group)
            with if_crowded(act):
                act.wait_ge(s_yout, 16 * NE)
                with act.Fori(0, NE * NWIN) as n:
                    act.wait_ge(g_gu, n + 1)
                    act.activation(silu_g[:, 0], gate_up_bank(0)[:, 0:NF, :], ACT.Silu
                                   ).then_inc(g_silu, 1)
                    act.wait_ge(g_down, n + 1)
                    act.activation(ysb[:, 0, 0:R], down_bank(0, 0)[0:WIN, :], ACT.Copy
                                   ).then_inc(g_yl, 1)
                    act.wait_ge(g_yout, n * 16 + 16)

            for t in range(NT):
                act.wait_ge(s_x2, t + 1)
                sum_squares(t, 2, wide[:])
            deviation(2)

        @block.gpsimd
        def _(pool):
            own = Chain(pool, c_pool)
            pool.wait_ge(s_const, 16)
            pool.wait_ge(s_small, SMALL)
            for n in range(2 * NT):
                b, t = divmod(n, NT)
                dst, decay = ((krow, C_KD), (qrow, C_QD))[b]
                main.wait_read(pool, (b, t))
                own(pool.tensor_tensor(rot[:, n % 2, 0], rot[:, n % 2, 0], rot[:, n % 2, 1], ALU.add))
                own.settle()
                pool.tensor_tensor(dst[:, t], rot[:, n % 2, 0], spread(const[:, decay:decay + H], DH),
                                   ALU.mult).then_inc(s_rot, 1)
            for t in range(NT):
                main.wait_read(pool, (VSB, t))
                pool.tensor_tensor(vsq[:, t], vsrow4[:, t], vsrow4[:, t], ALU.mult).then_inc(s_vsq, 1)
            for t in range(NT):
                pool.wait_ge(s_vn, t + 1)
                pool.tensor_tensor(vsrow[:, t, :], vsrow[:, t, :], sg_row[:], ALU.mult
                                   ).then_inc(s_vg, 1)
            for n in range(NT):
                pool.wait_ge(s_on, n + 1)
                pool.tensor_tensor(orow_flat[:, n, :], orow_flat[:, n, :], gn_row[:], ALU.mult
                                   ).then_inc(s_og, 1)
            pool.wait_ge(s_h2out, 16 * NT)
            aux.wait_read(pool, ("tokens",))
            for s in range(NS):
                if s >= XS:
                    aux.wait_full(pool, ("xsT", s - XS, 0))
                    aux.wait_full(pool, ("xsT", s - XS, 1))
                pool.indirect_dma_start(
                    out=xs[:, s % XS, :], out_offset=None, in_=h2_rows[:, :],
                    in_offset=bass.IndirectOffsetOnAxis(ap=tok_of[:, s:s + 1], axis=0)
                ).then_inc(s_xs[s % XS], 16)
            pool.wait_ge(s_tabs, 1)

            def store(e, j):
                first = pool.value_load(offi[0:1, one_of(e, j)], min_val=0, max_val=SLOTS)
                at_least(pool, s_yl, e, 1, j + 1)
                at_least(pool, s_yr, e, 1, j + 1)
                at_least(pool, s_yout, e, 16, 16 * j)
                pool.dma_start(y_rows[bass.ds(first, WIN), :], ysb[:, j % 2, :]).then_inc(s_yout, 16)

            def group(i):
                for j in range(RING):
                    store(i, j)

            group_loop(pool, group)
            pool.wait_ge(s_yout, 16 * NE)
            with if_crowded(pool):
                with pool.Fori(0, NE * NWIN) as n:
                    first = pool.value_load(wr_i[0:1, bass.ds(n, 1)], min_val=0, max_val=TRASH)
                    pool.wait_ge(g_yl, n + 1)
                    pool.wait_ge(g_yr, n + 1)
                    pool.dma_start(y_rows[bass.ds(first, WIN), :], ysb[:, 0, :]).then_inc(g_yout, 16)
                    pool.wait_ge(g_yout, n * 16 + 16)
            for t in range(NT):
                for pick in range(TOPK):
                    pool.indirect_dma_start(
                        out=gy[:, pick, t, :], out_offset=None, in_=y_rows[0:SLOTS, :],
                        in_offset=bass.IndirectOffsetOnAxis(ap=slot_of[:, pick, t:t + 1], axis=0)
                    ).then_inc(s_gy[t], 16)

        @block.vector
        def _(dve):
            own = Chain(dve, c_dve)

            def rstd(kind):
                dve.wait_ge(s_sd, kind + 1)
                own(dve.reciprocal(stat[:, 3 * kind + 2, :], stat[:, 3 * kind + 1, :]))
                own.settle()

            def rstd_of(kind, t):
                return stat[:, 3 * kind + 2, t:t + 1]

            def w_low(g):
                b, k = STEPS[g]
                dve.wait_ge(s_whi, g + 1)
                dst, raw, high = w_lo[:, g % RAW, :], w_raw[:, g % RAW, :], w_hi[:, g % RAW, :]
                if b < NB_IN:
                    ins = dve.scalar_tensor_tensor(dst, raw, gmix[:, k:k + 1], high.bitcast(F32),
                                                   ALU.mult, ALU.subtract)
                else:
                    ins = dve.tensor_tensor(dst, raw, high.bitcast(F32), ALU.subtract)
                ins.then_inc(s_wlo, 1)

            made = [0]

            def transposed_low(name, hi, lo, t, half):
                item = (name, t, half)
                made[0] += 1
                dve.wait_ge(s_thi, made[0])
                at = (slice(None), half_rows(half), tokens(t))
                dve.tensor_tensor(lo[at], heads(aux.bank(item)), hi[at].bitcast(F32), ALU.subtract
                                  ).then_inc(aux.done(item), 1)

            def normalise(t):
                dve.tensor_scalar(hrow[:, t % 2, :], x[:, t, :], rstd_of(0, t), None, ALU.mult
                                  ).then_inc(s_h, 1)

            dve.wait_ge(s_small, SMALL)
            rstd(0)
            normalise(0)
            normalise(1)
            w_low(0)
            w_low(1)
            for t in range(NT):
                for half in range(2):
                    transposed_low("hT", hT_hi, hT_lo, t, half)
                if t + 2 < NT:
                    normalise(t + 2)

            own(dve.tensor_copy(pos_f[:], pos_i[:]))
            own.settle()
            for c in range(2):
                for t in range(NT):
                    own(dve.tensor_scalar(ang[:, 0, c, t, :], const[:, C_FREQ:C_FREQ + HALF],
                                          pos_f[:, t:t + 1], None, ALU.mult))
            own.settle()
            for c in range(2):
                own(dve.tensor_scalar(ang[:, 1, c], ang[:, 0, c], 1 / (2 * np.pi), 0.25 * c,
                                      ALU.mult, ALU.add))
            own.settle()
            own(dve.tensor_scalar(ang[:, 1], ang[:, 1], MAGIC, MAGIC, ALU.add, ALU.subtract))
            for part in TWO_PI:
                own.settle()
                own(dve.scalar_tensor_tensor(flat(ang[:, 0]), flat(ang[:, 1]), -part, flat(ang[:, 0]),
                                             ALU.mult, ALU.add))
            own.settle()
            own(dve.tensor_scalar(ang[:, 0, 1], ang[:, 0, 1], np.pi / 2, None, ALU.add))
            own.settle()
            dve.tensor_scalar(ang[:, 0], ang[:, 0], PI_BELOW, -PI_BELOW, ALU.min, ALU.max
                              ).then_inc(s_ang, 1)

            def rotate(b, t):
                n = NT * b + t
                main.wait_full(dve, (b, t))
                if n >= 2:
                    dve.wait_ge(s_rot, n - 1)
                ps = main.bank((b, t))[:, :].rearrange("p (x c) -> p x c", c=HALF)
                row = main.bank((b, t))[:, :].rearrange("p (h two c) -> p h two c", two=2, c=HALF)
                a = rot[:, n % 2, 0].rearrange("p h (two c) -> p (h two) c", two=2)
                z = rot[:, n % 2, 1].rearrange("p h (two c) -> p h two c", two=2)
                sin, cos = trig[:, 0, t, :], trig[:, 1, t, :]
                dve.tensor_tensor(a, ps, along(cos, 2 * H), ALU.mult)
                dve.scalar_tensor_tensor(z[:, :, 0, :], row[:, :, 1, :], -1.0, along(sin, H),
                                         ALU.mult, ALU.mult)
                dve.tensor_tensor(z[:, :, 1, :], row[:, :, 0, :], along(sin, H), ALU.mult
                                  ).then_inc(main.done((b, t)), 1)

            def mask(n):
                aux.wait_full(dve, ("scores", n))
                dve.tensor_tensor(scT[:, n % 2], heads(aux.bank(("scores", n))), along(causal, H),
                                  ALU.mult).then_inc(aux.done(("scores", n)), 1)

            def next_state(n):
                aux.wait_full(dve, ("kv", n))
                kv, decay = heads(aux.bank(("kv", n))), spread(const[:, C_CD:C_CD + H], DH)
                if n:
                    own(dve.tensor_tensor(kvt[:], kv, state[:, n % 2], ALU.add))
                    own.settle()
                    kv = kvt[:]
                dve.tensor_tensor(state[:, (n + 1) % 2], kv, decay, ALU.mult
                                  ).then_inc(aux.done(("kv", n)), 1)

            def variance(n):
                aux.wait_read(dve, ("o", n))
                for h in range(H):
                    own(dve.bn_stats(gnstat[:, n, h, :], orow[:, n, h, :]))
                own.settle()
                for h in range(H):
                    ins = dve.bn_aggr(gnaggr[:, n, h, :], gnstat[:, n, h, :])
                    if n == NT - 1 and h == H - 1:
                        ins.then_inc(s_gnv, 1)

            def gate_tokens(t):
                item = ("gating", t)
                aux.wait_full(dve, item)
                main.wait_read(dve, (UB, t))
                for g in range(G):
                    u = urow[:, t, g * P:(g + 1) * P]
                    ins = dve.scalar_tensor_tensor(u, aux.bank(item)[:, g * P:(g + 1) * P],
                                                   bsgu[:, g:g + 1], u, ALU.add, ALU.mult)
                ins.then_inc(aux.done(item), 1)

            def residual(c):
                for t in range(NT):
                    item = (NB_IN + c, t)
                    main.wait_full(dve, item)
                    part = x[:, t, c * R:(c + 1) * R]
                    dve.tensor_tensor(part, main.bank(item)[:, :], part, ALU.add
                                      ).then_inc(main.done(item), 1)

            for g in range(2, NSTEP):
                w_low(g)
                if g == 6:
                    aux.wait_full(dve, ("wT",))
                    dve.tensor_tensor(wT[:], heads(aux.bank(("wT",))), along(causal, G), ALU.mult
                                      ).then_inc(aux.done(("wT",)), 1)
                if g in (11, 12, 19, 20):
                    if g == 11:
                        dve.wait_ge(s_trig, 1)
                    b, first = (g - 11) // 8, 2 * ((g - 11) % 8)
                    rotate(b, first)
                    rotate(b, first + 1)
                for n in range(NT):
                    if g == 32 + 3 * n:
                        mask(n)
                        if n < NT - 1:
                            next_state(n)
                    if g == 35 + 3 * n:
                        variance(n)
                if g == 37:
                    dve.wait_ge(s_vsq, NT)
                    dve.tensor_reduce(vss[:, 0], vsq[:], AX, ALU.add).then_inc(s_vss, 1)
                if g == 39:
                    dve.wait_ge(s_vsd, 1)
                    own(dve.reciprocal(vss[:, 2], vss[:, 1]))
                    own.settle()
                    for t in range(NT):
                        dve.tensor_tensor(vsrow4[:, t], vsrow4[:, t], spread(vss[:, 2, t, :], P),
                                          ALU.mult).then_inc(s_vn, 1)
                for t, step in enumerate((45, 46, 47, 48)):
                    if g == step:
                        gate_tokens(t)
                if g == 49:
                    dve.wait_ge(s_gnd, 1)
                    own(dve.reciprocal(gnrs[:, 1], gnrs[:, 0]))
                    own.settle()
                    for n in range(NT):
                        for h in range(H):
                            row = orow[:, n, h, :]
                            ins = dve.tensor_scalar(row, row, gnaggr[:, n, h, 0:1],
                                                    gnrs[:, 1, n, h:h + 1], ALU.subtract, ALU.mult)
                        ins.then_inc(s_on, 1)
                if g == 51:
                    for t in range(NT):
                        transposed_low("mT", mT_hi, mT_lo, t, 1)
                    for t in range(NT):
                        main.wait_read(dve, (GB, t))
                        dve.wait_ge(s_og, t + 1)
                        dve.tensor_tensor(grow[:, t, :], grow[:, t, :], orow_flat[:, t, :], ALU.mult
                                          ).then_inc(s_mix, 1)
                if g == 52:
                    for t in range(NT):
                        transposed_low("mT", mT_hi, mT_lo, t, 0)
                if g == 59:
                    residual(0)
            residual(1)
            rstd(1)
            dve.wait_ge(s_gain, 16)
            for t in range(NT):
                dve.scalar_tensor_tensor(h2[:, t, :], x[:, t, :], rstd_of(1, t), gain_row[:],
                                         ALU.mult, ALU.mult).then_inc(s_h2, 1)

            def read_aux(item, dst):
                aux.wait_full(dve, item)
                dve.tensor_copy(dst, heads(aux.bank(item))).then_inc(aux.done(item), 1)

            for t in range(NT):
                read_aux(("h2T", t, 1), h2T[:, half_rows(1), tokens(t)])

            aux.wait_full(dve, ("logits",))
            logits = aux.bank(("logits",))[:, 0:NT * (G + NE)].rearrange("p (t c) -> p t c", t=NT)
            own(dve.memset(glog[:], NEG))
            own.settle()
            own(dve.tensor_tensor(glog[:, :, 0:G], logits[:, :, 0:G], along(brt[:, 0:G], NT), ALU.add))
            dve.tensor_tensor(elog[:].rearrange("p t g e -> p t (g e)"), logits[:, :, G:],
                              along(brt[:, G:], NT), ALU.add).then_inc(aux.done(("logits",)), 1)
            own.settle()
            for t in range(NT):
                own(dve.max(gtop[:, t, :], glog[:, t, :]))
            own.settle()
            dve.tensor_tensor(gsub[:], glog[:, :, 0:G], spread(gtop[:, :, 0], G), ALU.subtract
                              ).then_inc(s_arg, 1)
            for t in range(NT):
                own(dve.max_index(gidx[:, t, :], gtop[:, t, :], glog[:, t, :]))
            own.settle()
            own(dve.tensor_copy(gid[:], gidx[:, :, 0]))
            own.settle()
            own(dve.tensor_tensor(gsel[:], along(const[:, C_I32:C_I32 + G], NT), spread(gid[:], G),
                                  ALU.is_equal))
            own.settle()
            aux.wait_read(dve, ("logits",))
            own(dve.tensor_tensor(emul[:], elog[:], spread(gsel[:], EPG), ALU.mult))
            own.settle()
            own(dve.tensor_reduce(slog[:], emul[:].rearrange("p t g e -> p t e g"), AX, ALU.add))
            own.settle()
            for t in range(NT):
                own(dve.max(etop[:, t, :], slog[:, t, :]))
            own.settle()
            dve.tensor_tensor(esub[:], etop[:, :, 1], etop[:, :, 0], ALU.subtract).then_inc(s_arg, 1)
            for t in range(NT):
                own(dve.max_index(eidx[:, t, :], etop[:, t, :], slog[:, t, :]))
            own.settle()
            for pick in range(TOPK):
                own(dve.tensor_copy(eid[:, pick, :], eidx[:, :, pick]))
            own.settle()
            for pick in range(TOPK):
                own(dve.scalar_tensor_tensor(eid[:, pick, :], gid[:], float(EPG), eid[:, pick, :],
                                             ALU.mult, ALU.add))
            own.settle()
            for pick in range(TOPK):
                own(dve.tensor_tensor(pairs[:, pick], along(const[:, C_I32:C_I32 + NE], NT),
                                      spread(eid[:, pick, :], NE), ALU.is_equal))
            own.settle()
            dve.tensor_tensor(picked[:], pairs[:, 0], pairs[:, 1], ALU.add).then_inc(s_pick, 1)

            dve.wait_ge(s_exp, 2)
            own(dve.tensor_reduce(gden[:], gexp[:], AX, ALU.add))
            own(dve.tensor_scalar(eden[:], e2[:], 1.0, None, ALU.add))
            own.settle()
            own(dve.tensor_tensor(eden[:], eden[:], gden[:], ALU.mult))
            own.settle()
            own(dve.reciprocal(gates[:, 0, :], eden[:]))
            own.settle()
            own(dve.tensor_tensor(gates[:, 1, :], gates[:, 0, :], e2[:], ALU.mult))

            ranks = ("ranks",)
            aux.wait_full(dve, ranks)
            rank = aux.bank(ranks)[:, 0:NT * NE].rearrange("p (t e) -> p t e", t=NT)
            total = aux.bank(ranks)[:, NT * NE:(NT + 1) * NE]
            own(dve.tensor_copy(cnt[:, 0], total))
            own(dve.memset(cnt[:, 3], 0.0))
            own.settle()
            own(dve.tensor_tensor_scan(cnt[:, 1], cnt[:, 0], cnt[:, 3], 0.0, ALU.add, ALU.add))
            own.settle()
            own(dve.tensor_tensor(cnt[:, 2], cnt[:, 1], cnt[:, 0], ALU.subtract))
            own.settle()
            dve.tensor_tensor(slots[:], rank, along(cnt[:, 2], NT), ALU.add
                              ).then_inc(aux.done(ranks), 1)
            aux.wait_read(dve, ranks)
            for pick in range(TOPK):
                own(dve.tensor_tensor(spick[:, pick], pairs[:, pick], slots[:], ALU.mult))
            own.settle()
            own(dve.tensor_reduce(slot_f[:], spick[:], AX, ALU.add))
            own.settle()
            for t in range(NT):
                own(dve.tensor_scalar(onehot[:, t, :], consth[:, 0:SLOTS], slot_f[:, 0, t:t + 1], None,
                                      ALU.is_equal))
            own.settle()
            for t in range(NT):
                dve.scalar_tensor_tensor(onehot[:, t, :], consth[:, 0:SLOTS], slot_f[:, 1, t:t + 1],
                                         onehot[:, t, :], ALU.is_equal, ALU.add).then_inc(s_hot, 1)
            own(dve.tensor_copy(slot_of[:], slot_f[:]))

            own(dve.tensor_copy(offi[:, 0:NE], cnt[:, 2]))
            own(dve.tensor_reduce(gden[:, 0:1], cnt[:, 0], AX, ALU.max))
            own.settle()
            own(dve.tensor_scalar(offi[:, NE:NE + 1], gden[:, 0:1], float(WIN), None, ALU.is_gt))
            w64, used, start = wtab[:, 0], wtab[:, 1], wtab[:, 2]
            own(dve.tensor_scalar(w64, along(const[:, C_I32:C_I32 + NWIN], NE), float(WIN), None,
                                  ALU.mult))
            own.settle()
            own(dve.tensor_tensor(used, spread(cnt[:, 0], NWIN), w64, ALU.is_gt))
            own(dve.tensor_tensor(start, spread(cnt[:, 2], NWIN), w64, ALU.add))
            for unused, table in ((SLOTS, rd_i), (TRASH, wr_i)):
                own.settle()
                own(dve.scalar_tensor_tensor(w64, start, -float(unused), used, ALU.add, ALU.mult))
                own.settle()
                own(dve.tensor_scalar(table[:].rearrange("p (e w) -> p e w", w=NWIN), w64,
                                      float(unused), None, ALU.add))
            own.settle()
            dve.engine_nop().then_inc(s_tabs, 1)

            tok = ("tokens",)
            aux.wait_full(dve, tok)
            dve.tensor_copy(tok_of[:], aux.bank(tok)[:, 0:NS]).then_inc(aux.done(tok), 1)
            dve.memset(pad, 0.0).then_inc(s_pad, 1)
            for s in range(NS):
                read_aux(("xsT", s, 1), xsT[:, half_rows(1), tokens(s)])

            def multiply(e, j):
                at_least(dve, s_silu, e, 1, j + 1)
                at_least(dve, s_down, e, 1, j - 1)
                dve.tensor_tensor(actT[:, j % 2], silu_g[:, j % 2], gate_up_bank(j)[:, NF:2 * NF, :],
                                  ALU.mult).then_inc(s_act, 1)

            def y_right(e, j):
                at_least(dve, s_down, e, 1, j + 1)
                at_least(dve, s_yout, e, 16, 16 * (j - 1))
                dve.tensor_copy(ysb[:, j % 2, R:D], down_bank(j, 1)[0:WIN, :]).then_inc(s_yr, 1)

            def group(i):
                for j in range(RING):
                    if not (isinstance(i, int) and i + j + 1 >= NE):
                        multiply(i, j + 1)
                    y_right(i, j)

            multiply(0, 0)
            group_loop(dve, group)
            with if_crowded(dve):
                dve.wait_ge(s_yout, 16 * NE)
                with dve.Fori(0, NE * NWIN) as n:
                    dve.wait_ge(g_silu, n + 1)
                    dve.tensor_tensor(actT[:, 0], silu_g[:, 0], gate_up_bank(0)[:, NF:2 * NF, :],
                                      ALU.mult).then_inc(g_act, 1)
                    dve.wait_ge(g_down, n + 1)
                    dve.tensor_copy(ysb[:, 0, R:D], down_bank(0, 1)[0:WIN, :]).then_inc(g_yr, 1)
                    dve.wait_ge(g_yout, n * 16 + 16)

            for t in range(NT):
                dve.wait_ge(s_gy[t], 16 * TOPK)
                own(dve.scalar_tensor_tensor(x[:, t, :], gy[:, 0, t, :], gates[:, 0, t:t + 1],
                                             x[:, t, :], ALU.mult, ALU.add))
                own.settle()
                dve.scalar_tensor_tensor(x[:, t, :], gy[:, 1, t, :], gates[:, 1, t:t + 1], x[:, t, :],
                                         ALU.mult, ALU.add).then_inc(s_x2, 1)
            rstd(2)
            dve.wait_ge(s_gain, 32)
            for t in range(NT):
                dve.scalar_tensor_tensor(outrow[:, t, :], x[:, t, :], rstd_of(2, t), gain_row[:],
                                         ALU.mult, ALU.mult).then_inc(s_out, 1)

        @block.tensor
        def _(pe):
            def transposes(item, chunks, last=None):
                for i, chunk in enumerate(chunks):
                    ins = pe.transpose(aux.bank(item)[:, i * P:(i + 1) * P], chunk, ident)
                ins.then_inc(aux.filled(item), 1)

            def every_kth(row, half):
                cols = row.rearrange("p (q k) -> p k q", k=ND)
                return [cols[:, 4 * half + i, :] for i in range(4)]

            def head_products(item, left, right):
                for h in range(H):
                    ins = pe.matmul(aux.bank(item)[:, h * P:(h + 1) * P], left(h), right(h),
                                    start=True, stop=True)
                ins.then_inc(aux.filled(item), 1)

            def do(item):
                name, *at = item
                aux.wait_free(pe, item)
                if name == "hT":
                    t, half = at
                    pe.wait_ge(s_h, t + 1)
                    transposes(item, [hrow[:, t % 2, (4 * half + i) * P:(4 * half + i + 1) * P]
                                      for i in range(4)])
                elif name == "wT":
                    pe.wait_ge(s_sgw, 16)
                    transposes(item, [wsraw[:, g, :] for g in range(G)])
                elif name in ("kT", "qT"):
                    t, = at
                    src, b = (krow, 0) if name == "kT" else (qrow, 1)
                    pe.wait_ge(s_rot, NT * b + t + 1)
                    transposes(item, [src[:, t, h, :] for h in range(H)])
                elif name == "scores":
                    n, = at
                    aux.wait_read(pe, ("kT", n))
                    aux.wait_read(pe, ("qT", n))
                    head_products(item, lambda h: kT[:, h, tokens(n)], lambda h: qT[:, h, tokens(n)])
                elif name == "kv":
                    n, = at
                    main.wait_read(pe, (VB, n))
                    head_products(item, lambda h: krow[:, n, h, :], lambda h: vrow[:, n, h, :])
                elif name == "o":
                    n, = at
                    main.wait_read(pe, (VB, n))
                    aux.wait_read(pe, ("scores", n))
                    if n:
                        aux.wait_read(pe, ("kv", n - 1))
                    for h in range(H):
                        dst = aux.bank(item)[:, h * P:(h + 1) * P]
                        ins = pe.matmul(dst, scT[:, n % 2, h, :], vrow[:, n, h, :],
                                        start=True, stop=(n == 0))
                        if n:
                            ins = pe.matmul(dst, qT[:, h, tokens(n)], state[:, n % 2, h, :],
                                            start=False, stop=True)
                    ins.then_inc(aux.filled(item), 1)
                elif name == "gating":
                    t, = at
                    aux.wait_read(pe, ("wT",))
                    pe.wait_ge(s_vg, t + 1)
                    head_products(item, lambda g: wT[:, g, :],
                                  lambda g: vsrow[:, t, g * P:(g + 1) * P])
                elif name == "mT":
                    t, half = at
                    if half:
                        aux.wait_read(pe, ("gating", t))
                    else:
                        pe.wait_ge(s_mix, t + 1)
                    src = urow if half else grow
                    transposes(item, [src[:, t, i * P:(i + 1) * P] for i in range(4)])
                elif name == "h2T":
                    t, half = at
                    pe.wait_ge(s_h2, t + 1)
                    transposes(item, every_kth(h2[:, t, :], half))
                elif name == "logits":
                    aux.wait_read(pe, ("h2T", NT - 1, 0))
                    aux.wait_read(pe, ("h2T", NT - 1, 1))
                    for t in range(NT):
                        dst = aux.bank(item)[:, t * (G + NE):(t + 1) * (G + NE)]
                        for k in range(ND):
                            ins = pe.matmul(dst, h2T[:, k, tokens(t)], wrt[:, k, :],
                                            start=(k == 0), stop=(k == ND - 1))
                    ins.then_inc(aux.filled(item), 1)
                elif name == "ranks":
                    pe.wait_ge(s_pick, 1)
                    for t in range(NT + 1):
                        dst = aux.bank(item)[:, t * NE:(t + 1) * NE]
                        for c in range(min(t + 1, NT)):
                            ins = pe.matmul(dst, before if c == t else ones, picked[:, c, :],
                                            start=(c == 0), stop=(c == min(t, NT - 1)))
                    ins.then_inc(aux.filled(item), 1)
                elif name == "tokens":
                    pe.wait_ge(s_hot, NT)
                    for s in range(NS):
                        for t in range(NT):
                            ins = pe.matmul(aux.bank(item)[:, s:s + 1], onehot[:, t, tokens(s)],
                                            consth[:, SLOTS + t:SLOTS + t + 1],
                                            start=(t == 0), stop=(t == NT - 1))
                    ins.then_inc(aux.filled(item), 1)
                elif name == "xsT":
                    s, half = at
                    pe.wait_ge(s_xs[s % XS], 16 * (s // XS + 1))
                    transposes(item, every_kth(xs[:, s % XS, :], half))

            def step(g):
                b, k = STEPS[g]
                high, low = (hT_hi, hT_lo) if b < NB_IN else (mT_hi, mT_lo)
                first, last = g % ND == 0, g % ND == ND - 1
                pe.wait_ge(s_wlo, g + 1)
                for t in range(NT):
                    if g == NB_IN * ND or g == NB_IN * ND + 4:
                        aux.wait_read(pe, ("mT", t, int(g == NB_IN * ND)))
                    if first:
                        main.wait_free(pe, (b, t))
                    dst = main.bank((b, t))[:, :]
                    slot = g % RAW
                    pe.matmul(dst, high[:, k, tokens(t)], w_hi[:, slot, :], start=first, stop=False)
                    pe.matmul(dst, high[:, k, tokens(t)], w_lo[:, slot, :], start=False, stop=False)
                    ins = pe.matmul(dst, low[:, k, tokens(t)], w_hi[:, slot, :],
                                    start=False, stop=last)
                    if last:
                        ins.then_inc(main.filled((b, t)), 1)
                    elif t == NT - 1:
                        ins.then_inc(s_step, 1)

            pe.wait_ge(s_const, 16)
            todo = list(beside)
            for g in range(-1, NSTEP + 1):
                if g == 0:
                    aux.wait_read(pe, ("hT", NT - 1, 0))
                    aux.wait_read(pe, ("hT", NT - 1, 1))
                if 0 <= g < NSTEP:
                    step(g)
                while todo and todo[0][0] == g:
                    do(todo.pop(0)[1])

            aux.wait_read(pe, ("xsT", NS - 1, 0))
            aux.wait_read(pe, ("xsT", NS - 1, 1))
            pe.wait_ge(s_pad, 1)
            for t in range(NT):
                main.wait_read(pe, (NB - 1, t))
            pe.wait_ge(s_tabs, 1)

            def gate_up(slot, first, bank):
                for w, c in ((wg[slot], 0), (wu[slot], NF)):
                    for f in range(NF):
                        for k in range(ND):
                            ins = pe.matmul(bank[:, c + f, :], w[:, k, f:FF:NF],
                                            xsT[:, k, bass.ds(first, WIN)],
                                            start=(k == 0), stop=(k == ND - 1))
                return ins

            def down(slot, acts, banks):
                for c in range(2):
                    for f in range(NF):
                        ins = pe.matmul(banks[c][0:WIN, :], acts[:, f, :],
                                        wd[slot][:, f, c * R:(c + 1) * R],
                                        start=(f == 0), stop=(f == NF - 1))
                return ins

            def expert_gate_up(e, j):
                slot = j % RING
                first = pe.value_load(offi[0:1, one_of(e, j)], min_val=0, max_val=SLOTS)
                at_least(pe, s_wgu[slot], e, 32 // RING, 32 * (j // RING + 1))
                at_least(pe, s_act, e, 1, j - 1)
                gate_up(slot, first, gate_up_bank(j)).then_inc(s_gu, 1)

            def expert_down(e, j):
                at_least(pe, s_wd[j], e, 16 // RING, 16)
                at_least(pe, s_act, e, 1, j + 1)
                at_least(pe, s_yl, e, 1, j - 1)
                at_least(pe, s_yr, e, 1, j - 1)
                down(j, actT[:, j % 2], [down_bank(j, 0), down_bank(j, 1)]).then_inc(s_down, 1)

            def group(i):
                for j in range(RING):
                    if not (isinstance(i, int) and i + j + 1 >= NE):
                        expert_gate_up(i, j + 1)
                    expert_down(i, j)

            expert_gate_up(0, 0)
            group_loop(pe, group)
            with if_crowded(pe):
                pe.wait_ge(s_yl, NE)
                pe.wait_ge(s_yr, NE)
                with pe.Fori(0, NE) as e:
                    with pe.Fori(0, NWIN) as w:
                        n = e * NWIN + w
                        first = pe.value_load(rd_i[0:1, bass.ds(n, 1)], min_val=0, max_val=SLOTS)
                        pe.wait_ge(g_w, e * 48 + 48)
                        gate_up(0, first, gate_up_bank(0)).then_inc(g_gu, 1)
                        pe.wait_ge(g_act, n + 1)
                        down(0, actT[:, 0], [down_bank(0, 0), down_bank(0, 1)]).then_inc(g_down, 1)
                        pe.wait_ge(g_yl, n + 1)
                        pe.wait_ge(g_yr, n + 1)


def kernel(**inputs):
    from concourse import bacc
    from concourse.bass_utils import run_bass_kernel_spmd

    nc = bacc.Bacc("TRN2", target_bir_lowering=False, num_devices=1)
    wide, half = constants()
    arrays = {"in_" + n: np.ascontiguousarray(inputs[n]) for n in INPUTS}
    arrays["in_constants"], arrays["in_constants_half"] = wide, half
    A = {n[3:]: nc.dram_tensor(n, a.shape, mybir.dt.from_np(a.dtype), kind="ExternalInput").ap()
         for n, a in arrays.items()}
    out = nc.dram_tensor("out", (1, S, D), F32, kind="ExternalOutput").ap()
    build(nc, A, out)
    r = run_bass_kernel_spmd(nc, [arrays], core_ids=[0])
    return r.results[0]["out"]
```

```python
from contextlib import ExitStack

import numpy as np

import concourse.bass as bass
from concourse import mybir

P = 128
F32 = mybir.dt.float32
F32R = mybir.dt.float32r
F16 = mybir.dt.float16
I32 = mybir.dt.int32
U32 = mybir.dt.uint32
ALU = mybir.AluOpType
ACT = mybir.ActivationFunctionType
AX = mybir.AxisListType.X

D = 1024
S = 512
NT = S // P
ND = D // P
H = 4
DH = 128
HALF = DH // 2
R = H * DH
NB_IN = 6
NB = NB_IN + 2
G = 4
EPG = 8
NE = G * EPG
FF = 256
NF = FF // P
TOPK = 2
WIN = 64
RANKS = S
NWIN = RANKS // WIN
UNUSED = 2048
NPAIR = NE // 2
EPS = 1e-6
ROPE_BASE = 10000.0
NEG = -3.0e38
MAGIC = 1.5 * 2.0 ** 23
PI_BELOW = 3.1415925
TWO_PI = (6.28125, 4059 * 2.0 ** -21, 2 * np.pi - 6.28125 - 4059 * 2.0 ** -21)

RAW = 4
RING = 6
GP = RING // 2
NGROUP = NPAIR // GP
LAST = NPAIR - GP * (NGROUP - 1)
SMALL = 16 * 15

BLOCK_COL = [1, 0, 2, 5, 4, 3]
KB, QB, VB, VSB, UB, GB = range(6)
STEPS = [(b, k) for b in range(NB_IN) for k in range(ND)] + \
        [(NB_IN + c, k) for c in range(2) for k in (4, 5, 6, 7, 0, 1, 2, 3)]
NSTEP = len(STEPS)

C_ID, C_CAUSAL = 0, 128
C_QD, C_KD, C_CD, C_FREQ, C_I32, C_EPS = 256, 260, 264, 268, 332, 364
C_N = 368
H_BEFORE, H_ONES, H_PLACE, H_BASE, H_ROW = 0, 128, 256, 384, 416
H_N = H_ROW + TOPK * NT * 2


def constants():
    c = np.zeros((P, C_N), np.float32)
    i = np.arange(P, dtype=np.float64)
    c[:, C_ID:C_ID + P] = np.eye(P)
    c[:, C_CAUSAL:C_CAUSAL + P] = i[:, None] <= i[None, :]
    gamma = 1.0 - 2.0 ** (-5.0 - np.arange(H))
    c[:, C_QD:C_QD + H] = gamma[None, :] ** (i[:, None] + 1)
    c[:, C_KD:C_KD + H] = gamma[None, :] ** -(i[:, None] + 1) * DH ** -0.5
    c[:, C_CD:C_CD + H] = gamma[None, :] ** P
    c[:, C_FREQ:C_FREQ + HALF] = ROPE_BASE ** (-np.arange(HALF) * 2.0 / DH)
    c[:, C_I32:C_I32 + NE] = np.arange(NE)
    c[:, C_EPS] = EPS
    h = np.zeros((P, H_N), np.float16)
    h[:, H_BEFORE:H_BEFORE + P] = i[:, None] < i[None, :]
    h[:, H_ONES:H_ONES + P] = 1.0
    h[:, H_PLACE:H_PLACE + P] = np.arange(P) % WIN + RANKS * (np.arange(P) // WIN)
    h[:, H_BASE:H_BASE + NE] = np.arange(NE) * (RANKS // P)
    row = h[:, H_ROW:].reshape(P, TOPK, NT, 2)
    row[...] = (i[:, None] + P * np.arange(NT) - UNUSED)[:, None, :, None]
    row[:, 1, :, 1] += S
    return c, h



class Banks:

    def __init__(self, banks, full, read):
        self.banks, self.full, self.read, self.order = banks, full, read, {}

    def add(self, item):
        self.order[item] = len(self.order)

    def turn(self, item):
        return self.order[item] % len(self.banks), self.order[item] // len(self.banks)

    def bank(self, item):
        return self.banks[self.turn(item)[0]]

    def filled(self, item):
        return self.full[self.turn(item)[0]]

    def done(self, item):
        return self.read[self.turn(item)[0]]

    def wait_free(self, eng, item):
        i, before = self.turn(item)
        if before:
            eng.wait_ge(self.read[i], before)

    def wait_full(self, eng, item):
        i, before = self.turn(item)
        eng.wait_ge(self.full[i], before + 1)

    def wait_read(self, eng, item):
        i, before = self.turn(item)
        eng.wait_ge(self.read[i], before + 1)


class Chain:

    def __init__(self, eng, sem):
        self.eng, self.sem, self.n = eng, sem, 0

    def __call__(self, ins):
        ins.then_inc(self.sem, 1)
        self.n += 1

    def settle(self):
        self.eng.wait_ge(self.sem, self.n)


INPUTS = ["x", "positions", "norm_mix_gain", "w_in", "ret_gn_gain", "sgu_norm_gain", "sgu_w", "sgu_b",
          "w_out", "norm_ffn_gain", "w_router_group", "b_router_group", "w_router_expert",
          "b_router_expert", "w_expert_gate_up", "w_expert_up", "w_expert_down", "final_norm_gain"]


def flat(ap):
    return ap.rearrange("p a b c -> p (a b c)")


def build(nc, A, out):
    ctx = ExitStack()
    with ctx:
        at = {"next": 0}
        base = (nc.sbuf_base + 63) // 64 * 64

        def place(name, shape, dt, offset):
            return nc.alloc_sbuf_tensor_at("sb_" + name, list(shape), dt, offset=base + offset)

        def sb(name, shape, dt=F32):
            size = int(np.prod(shape[1:])) * (2 if dt == F16 else 4)
            t = place(name, shape, dt, at["next"])
            at["next"] += (size + 31) // 32 * 32
            return t

        def psum(name):
            return ctx.enter_context(nc.psum_tensor("ps_" + name, [P, 512], F32))

        def sem(name):
            return ctx.enter_context(nc.semaphore(name))

        KiB = 1024
        const = sb("const", [P, C_N])
        consth = sb("consth", [P, H_N], F16)
        gmix = sb("gmix", [P, ND])
        gffn = sb("gffn", [P, ND])
        gffn_s = sb("gffn_s", [P, ND])
        bsgu = sb("bsgu", [P, G])
        brt = sb("brt", [P, NE + G])
        wrt = sb("wrt", [P, ND, NE + G])
        pos_i = sb("pos_i", [P, NT], I32)
        pos_f = sb("pos_f", [P, NT])
        stat = sb("stat", [P, 3 * 3, NT])
        half_ss = sb("half_ss", [P, 3, NT])
        gnstat = sb("gnstat", [P, NT, H, 6])
        gnaggr = sb("gnaggr", [P, NT, H, 2])
        gnrs = sb("gnrs", [P, 2, NT, H])
        vss = sb("vss", [P, 3, NT, G])
        actT = sb("actT", [P, NF, P])
        silu_g = sb("silu_g", [P, FF])
        acts = sb("acts", [P, FF])
        crowded = sb("crowded", [P, 1], I32)
        most = sb("most", [P, 1])
        gsub = sb("gsub", [P, NT, G])
        esub = sb("esub", [P, NT])
        e2 = sb("e2", [P, NT])
        gden = sb("gden", [P, NT])
        eden = sb("eden", [P, NT])
        gates = sb("gates", [P, TOPK, NT])
        gain_row = sb("gain_row", [P, D])
        logit = sb("logit", [P, NT, NE + 8])
        gtop = sb("gtop", [P, NT, 8])
        gidx = sb("gidx", [P, NT, 8], U32)
        gsel = sb("gsel", [P, NT, G])
        emul = sb("emul", [P, NT, G, EPG])
        slog = sb("slog", [P, NT, EPG])
        etop = sb("etop", [P, NT, 8])
        eidx = sb("eidx", [P, NT, 8], U32)
        gexp = sb("gexp", [P, NT, G])
        eid = sb("eid", [P, NT, TOPK])
        pairs = sb("pairs", [P, NT, TOPK, NE], F16)
        picked = sb("picked", [P, NT, NE], F16)
        spick = sb("spick", [P, NT, TOPK, NE])
        place_of = sb("place_of", [P, NT, TOPK])
        place_on = sb("place_on", [P, NT, TOPK])
        onehot = sb("onehot", [P, TOPK, NT, P], F16)
        row_of = sb("row_of", [P, GP, 2], I32)
        x = sb("x", [P, NT, D])

        arena = at["next"]
        w_raw = place("w_raw", [P, RAW, R], F32, arena)
        w_hi = place("w_hi", [P, RAW, R], F32R, arena + 8 * KiB)
        w_lo = place("w_lo", [P, RAW, R], F32R, arena + 16 * KiB)
        xs = place("xs", [P, D], F32, arena)
        hx = place("hx", [P, NT, D], F32, arena + 4 * KiB)
        xsT = place("xsT", [P, ND, P], F32, arena + 4 * KiB)
        ysb = place("ysb", [P, D], F32, arena + 8 * KiB)
        at["next"] = arena + 24 * KiB
        ring = at["next"]
        slot_size = 24 * KiB
        wgu = [place(f"wgu{i}", [P, ND, 2, FF], F32, ring + slot_size * i) for i in range(RING)]
        wd = [place(f"wd{i}", [P, NF, D], F32, ring + slot_size * i + 16 * KiB) for i in range(RING)]
        rows = ring + slot_size
        krow = place("krow", [P, NT, H, DH], F32, rows)
        vrow = place("vrow", [P, NT, H, DH], F32, rows + 8 * KiB)
        kT = place("kT", [P, H, S], F32, rows + 16 * KiB)
        qT = place("qT", [P, H, S], F32, rows + 24 * KiB)
        orow = place("orow", [P, NT, H, DH], F32, rows + 32 * KiB)
        grow = place("grow", [P, NT, R], F32, rows + 40 * KiB)
        urow = place("urow", [P, NT, R], F32, rows + 48 * KiB)
        vsrow = place("vsrow", [P, NT, R], F32, rows + 56 * KiB)
        state = place("state", [P, 2, H, DH], F32, rows + 64 * KiB)
        scT = place("scT", [P, 2, H, DH], F32, rows + 68 * KiB)
        hrow = place("hrow", [P, 2, D], F32, rows + 32 * KiB)
        rot = place("rot", [P, 2, 2, H, DH], F32, rows + 40 * KiB)
        qrow = place("qrow", [P, NT, H, DH], F32, rows + 48 * KiB)
        vsq = place("vsq", [P, NT, G, P], F32, rows + 48 * KiB)
        junk = place("junk", [P, D], F32, rows + 56 * KiB)
        wsraw = place("wsraw", [P, G, P], F32, rows + 60 * KiB)
        ang = place("ang", [P, 2, 2, NT, HALF], F32, rows)
        xT = place("xT", [P, ND, S], F32, rows + 48 * KiB)
        wide = place("wide", [P, R], F32, rows + 64 * KiB)
        hT_hi = place("hT_hi", [P, ND, S], F32R, rows + 72 * KiB)
        hT_lo = place("hT_lo", [P, ND, S], F32R, rows + 88 * KiB)
        mT_hi = place("mT_hi", [P, ND, S], F32R, rows + 72 * KiB)
        mT_lo = place("mT_lo", [P, ND, S], F32R, rows + 88 * KiB)
        trig = place("trig", [P, 2, NT, HALF], F32, rows + 104 * KiB)
        sg_row = place("sg_row", [P, R], F32, rows + 106 * KiB)
        gn_row = place("gn_row", [P, R], F32, rows + 108 * KiB)
        wT = place("wT", [P, G, P], F32, rows + 110 * KiB)
        kvt = place("kvt", [P, H, DH], F32, rows + 112 * KiB)
        gy = place("gy", [P, NT, TOPK, D], F32, ring)
        outrow = place("outrow", [P, NT, D], F32, ring + 32 * KiB)
        junk2 = place("junk2", [P, D], F32, ring + 48 * KiB)
        at["next"] = ring + RING * slot_size
        assert base + at["next"] <= nc.sbuf_usable_end, (base + at["next"], nc.sbuf_usable_end)

        orow_flat = orow[:].rearrange("p t h d -> p t (h d)")
        vsrow4 = vsrow[:].rearrange("p t (g c) -> p t g c", g=G)
        bk = [psum(f"bank{i}") for i in range(8)]

        hx_rows = nc.dram_tensor("hx_rows", [S, D], F32).ap()
        y_rows = nc.dram_tensor("y_rows", [TOPK * S, D], F32).ap()

        s_x = [sem(f"x_loaded{t}") for t in range(NT)]
        s_const = sem("constants_loaded")
        s_small = sem("small_inputs_loaded")
        s_sgw = sem("sgu_w_loaded")
        s_gain = sem("row_gain_loaded")
        s_raw = [sem(f"w_raw_loaded{i}") for i in range(RAW)]
        s_whi = sem("w_high_made")
        s_wlo = sem("w_low_made")
        s_step = sem("dense_step_done")
        s_ss = sem("squares_summed")
        s_sd = sem("deviation_made")
        s_h = sem("normalised_rows_made")
        s_thi = sem("transposed_high_made")
        s_ang = sem("angles_reduced")
        s_trig = sem("sin_cos_made")
        s_rot = sem("rotated_rows_made")
        s_vsq = sem("gating_squares_made")
        s_vss = sem("gating_sums_made")
        s_vsd = sem("gating_deviation_made")
        s_vn = sem("gating_v_scaled")
        s_vg = sem("gating_v_normalised")
        s_gnv = sem("retention_variance_made")
        s_gnd = sem("retention_deviation_made")
        s_on = sem("retention_normalised")
        s_og = sem("retention_gained")
        s_mix = sem("retention_mix_made")
        s_wrt = sem("router_weights_scaled")
        s_hss = sem("half_squares_summed")
        s_hbias = sem("first_half_squares_biased")
        s_rstd = sem("ffn_scale_made")
        s_hx = sem("scaled_rows_made")
        s_hxout = sem("scaled_rows_stored")
        s_arg = sem("softmax_arguments_made")
        s_exp = sem("softmax_exponentials_made")
        s_pick = sem("pairs_picked")
        s_crowd = sem("crowding_known")
        s_hot = sem("place_one_hots_made")
        s_moved = sem("places_moved_on")
        s_ids = sem("row_numbers_summed")
        s_rowof = sem("row_numbers_made")
        s_xs = sem("window_rows_gathered")
        s_tr = sem("window_halves_transposed")
        s_xsT = sem("window_halves_ready")
        s_auxf = [sem(f"aux_bank_full{i}") for i in range(2)]
        s_auxr = [sem(f"aux_bank_read{i}") for i in range(2)]
        s_mainf = [sem(f"main_bank_full{i}") for i in range(6)]
        s_mainr = [sem(f"main_bank_read{i}") for i in range(6)]
        s_wgu = [sem(f"gate_up_weights_loaded{q}") for q in range(GP)]
        s_wd = [sem(f"down_weights_loaded{q}") for q in range(GP)]
        s_gu = sem("gate_up_done")
        s_silu = sem("silu_made")
        s_act = sem("activation_made")
        s_at = sem("activation_transposed")
        s_actT = sem("transposed_activation_ready")
        s_down = sem("down_done")
        s_yl = sem("expert_rows_left_half_made")
        s_yr = sem("expert_rows_right_half_made")
        s_yout = sem("expert_rows_stored")
        g_w = sem("general_weights_loaded")
        g_hot = sem("general_one_hots_made")
        g_moved = sem("general_places_moved_on")
        g_ids = sem("general_row_numbers_summed")
        g_rowof = sem("general_row_numbers_made")
        g_xs = sem("general_rows_gathered")
        g_tr = sem("general_halves_transposed")
        g_xsT = sem("general_halves_ready")
        g_gu = sem("general_gate_up_done")
        g_silu = sem("general_silu_made")
        g_act = sem("general_activation_made")
        g_at = sem("general_activation_transposed")
        g_actT = sem("general_transposed_activation_ready")
        g_down = sem("general_down_done")
        g_yl = sem("general_rows_left_half_made")
        g_yr = sem("general_rows_right_half_made")
        g_yout = sem("general_rows_stored")
        s_gy = [sem(f"pair_rows_loaded{i}") for i in range(NT)]
        s_x2 = sem("experts_added")
        s_out = sem("rows_finished")
        s_turn = sem("indirect_queue_turn")
        s_stored = sem("output_stored")
        c_act = sem("scalar_own_results")
        c_dve = sem("vector_own_results")
        c_pool = sem("pool_own_results")

        main = Banks(bk[:6], s_mainf, s_mainr)
        for b in range(NB):
            for t in range(NT):
                main.add((b, t))
        main.add(("logits",))
        main.add(("ranks",))
        beside = [(-1, ("hT", t, half)) for t in range(NT) for half in range(2)]
        beside += [(2, ("wT",))]
        beside += [(12 + t, ("kT", t)) for t in range(NT)]
        beside += [(20 + t, ("qT", t)) for t in range(NT)]
        for n in range(NT):
            beside += [(28 + 3 * n, ("scores", n)), (30 + 3 * n, ("o", n))]
            if n < NT - 1:
                beside += [(28 + 3 * n, ("kv", n))]
        beside += [(41 + t, ("gating", t)) for t in range(NT)]
        beside += [(47, ("mT", t, 1)) for t in range(NT)]
        beside += [(49, ("mT", t, 0)) for t in range(NT)]
        beside += [(58 + t, ("xT", t, 0)) for t in range(NT)]
        beside += [(NSTEP, ("xT", 0, 1))]
        for t in range(1, NT):
            beside += [(NSTEP, ("xT", t, 1)), (NSTEP, ("logits", t - 1))]
        beside += [(NSTEP, ("logits", NT - 1)), (NSTEP, ("ranks",))]
        beside.sort(key=lambda entry: entry[0])
        aux = Banks(bk[6:], s_auxf, s_auxr)
        for _, item in beside:
            if item[0] not in ("logits", "ranks"):
                aux.add(item)

        def heads(bank):
            return bank[:, :].rearrange("p (h d) -> p h d", h=H)

        ident = const[:, C_ID:C_ID + P]
        causal = const[:, C_CAUSAL:C_CAUSAL + P]
        before = consth[:, H_BEFORE:H_BEFORE + P]
        ones = consth[:, H_ONES:H_ONES + P]

        def along(ap, n):
            return ap.unsqueeze(1).broadcast_to([P, n, ap.shape[1]])

        def spread(ap, n):
            return ap.unsqueeze(len(ap.shape)).broadcast_to([*ap.shape, n])

        w_gate = A["w_expert_gate_up"].rearrange("l g e (p k) f -> (l g e) p k f", p=P)
        w_up = A["w_expert_up"].rearrange("l g e (p k) f -> (l g e) p k f", p=P)
        w_down = A["w_expert_down"].rearrange("l g e (p j) n -> (l g e) p j n", p=P)

        def one(ap, e):
            return ap[bass.ds(e, 1)].squeeze(0) if not isinstance(e, int) else ap[e]

        block = ctx.enter_context(nc.Block())

        def at_least(eng, sem, i, mul, add):
            if isinstance(i, int):
                if mul * i + add > 0:
                    eng.wait_ge(sem, mul * i + add)
            else:
                eng.wait_ge(sem, i * mul + add)

        def group_loop(eng, group):
            group(0, GP)
            with eng.Fori(1, NGROUP - 1) as r:
                group(r, GP)
            group(NGROUP - 1, LAST)

        def comes(r, q):
            return not isinstance(r, int) or GP * r + q < NPAIR

        def if_crowded(eng):
            eng.wait_ge(s_crowd, 1)
            return eng.If(eng.value_load(crowded[0:1, 0:1], min_val=0, max_val=1) >= 1)

        gate_up_bank, act_bank = bk[0], bk[1]
        down_bank = [bk[2], bk[3]]
        ids_bank = bk[4]
        half_bank = [bk[6], bk[7]]

        def wait_step(eng, g):
            if g % ND == ND - 1:
                main.wait_full(eng, (STEPS[g][0], NT - 1))
            else:
                eng.wait_ge(s_step, g + 1 - g // ND)

        def tokens(t):
            return slice(t * P, (t + 1) * P)

        def half_rows(half):
            return slice(4 * half, 4 * half + 4)

        @block.sync
        def _(sp):
            for t in range(NT):
                sp.dma_start(x[:, t, :], A["x"][0, tokens(t), :]).then_inc(s_x[t], 16)

            def gate(slot, e, sem):
                sp.dma_start(wgu[slot][:, :, 0, :], one(w_gate, e)).then_inc(sem, 16)

            def up(slot, e, sem):
                sp.dma_start(wgu[slot][:, :, 1, :], one(w_up, e)).then_inc(sem, 16)

            def gate_up(slot, e, sem):
                gate(slot, e, sem)
                up(slot, e, sem)

            def down(slot, e, sem):
                sp.dma_start(wd[slot][:], one(w_down, e)).then_inc(sem, 16)

            for g, (b, k) in enumerate(STEPS):
                if g >= RAW:
                    sp.wait_ge(s_whi, g - RAW + 1)
                    sp.wait_ge(s_wlo, g - RAW + 1)
                if b < NB_IN:
                    src = A["w_in"][0, tokens(k), BLOCK_COL[b] * R:(BLOCK_COL[b] + 1) * R]
                else:
                    src = A["w_out"][0, tokens(k), (b - NB_IN) * R:(b - NB_IN + 1) * R]
                sp.dma_start(w_raw[:, g % RAW, :], src).then_inc(s_raw[g % RAW], 16)
                if g == 8:
                    gate_up(0, 0, s_wgu[0])
                    down(0, 0, s_wd[0])
                if g == 57:
                    aux.wait_read(sp, ("mT", NT - 2, 0))
                    aux.wait_read(sp, ("mT", NT - 1, 0))
                    gate(1, 1, s_wgu[0])
                if g == 58:
                    up(1, 1, s_wgu[0])
                if g == 59:
                    down(1, 1, s_wd[0])
                if g == 60:
                    gate(2, 2, s_wgu[1])
                if g == 61:
                    up(2, 2, s_wgu[1])
            down(2, 2, s_wd[1])
            main.wait_full(sp, (NB - 1, NT - 1))
            gate_up(4, 4, s_wgu[2])
            for t in range(NT):
                sp.wait_ge(s_hx, t + 1)
                sp.dma_start(hx_rows[tokens(t), :], hx[:, t, :]).then_inc(s_hxout, 16)
            down(4, 4, s_wd[2])
            sp.wait_ge(s_xs, 16)
            main.wait_full(sp, ("logits",))
            for slot in (3, 5):
                gate_up(slot, slot, s_wgu[slot // 2])
                down(slot, slot, s_wd[slot // 2])

            def group(r, pairs):
                for q in range(pairs):
                    e = r * RING + (2 * q + RING)
                    at_least(sp, s_gu, r, GP, q + 1)
                    for i in range(2):
                        gate_up(2 * q + i, e + i, s_wgu[q])
                    at_least(sp, s_down, r, GP, q + 1)
                    for i in range(2):
                        down(2 * q + i, e + i, s_wd[q])

            group(0, GP)
            with sp.Fori(1, NGROUP - 1) as r:
                group(r, GP)
            group(NGROUP - 1, LAST - GP)
            sp.wait_ge(s_down, NPAIR)
            with if_crowded(sp):
                gate_up(0, 0, g_w)
                down(0, 0, g_w)
                with sp.Fori(1, NE) as e:
                    sp.wait_ge(g_down, e * NWIN)
                    gate_up(0, e, g_w)
                    down(0, e, g_w)
            sp.wait_ge(s_yout, 16 * NPAIR)
            with if_crowded(sp):
                sp.wait_ge(g_yout, 16 * NE * NWIN)
            for t in range(NT):
                sp.dma_start(gy[:, t], y_rows[:, :].rearrange("(k t p) d -> t p k d", k=TOPK, p=P)[t]
                             ).then_inc(s_gy[t], 16)
            for t in range(NT):
                sp.wait_ge(s_out, t + 1)
                sp.dma_start(out[0, tokens(t), :], outrow[:, t, :]).then_inc(s_stored, 16)
            sp.wait_ge(s_stored, 16 * NT)

        @block.scalar
        def _(act):
            small = [0]

            def load(dst, src, slow=False):
                act.dma_start(dst, src, allow_slow_non_contiguous=slow).then_inc(s_small, 16)
                small[0] += 16

            act.dma_start(const[:], A["constants"]).then_inc(s_const, 16)
            load(gmix[:], A["norm_mix_gain"].rearrange("a (k p) -> p (a k)", p=P), slow=True)
            act.dma_start(wsraw[:], A["sgu_w"].rearrange("a g i j -> i (a g) j")).then_inc(s_sgw, 16)
            load(pos_i[:], A["positions"].rearrange("a (t p) -> p (a t)", p=P), slow=True)
            load(bsgu[:], A["sgu_b"].rearrange("a g i -> i (a g)"), slow=True)
            load(sg_row[:], A["sgu_norm_gain"][0].partition_broadcast(P))
            load(gn_row[:], A["ret_gn_gain"][0].partition_broadcast(P))
            load(gffn[:], A["norm_ffn_gain"].rearrange("a (k p) -> p (a k)", p=P), slow=True)
            load(gffn_s[:], A["norm_ffn_gain"].rearrange("a (p k) -> p (a k)", p=P))
            load(brt[:, NE:], A["b_router_group"][0].partition_broadcast(P))
            load(brt[:, :NE], A["b_router_expert"][0].rearrange("g e -> (g e)").partition_broadcast(P))
            load(wrt[:, :, NE:], A["w_router_group"][0].rearrange("(k p) g -> p k g", p=P), slow=True)
            for g in range(G):
                load(wrt[:, :, g * EPG:(g + 1) * EPG],
                     A["w_router_expert"][0, g].rearrange("(k p) e -> p k e", p=P), slow=True)
            load(consth[:], A["constants_half"])
            act.dma_start(gain_row[:], A["final_norm_gain"].partition_broadcast(P)).then_inc(s_gain, 16)

            def sum_squares(t, kind, scratch):
                if kind + t:
                    act.wait_ge(s_ss, NT * (kind // 2) + t)
                act.activation(scratch, x[:, t, :], ACT.Square,
                               accum_out=stat[:, 3 * kind, t:t + 1]).then_inc(s_ss, 1)

            def half_squares(t, half):
                if NT * half + t:
                    act.wait_ge(s_hss, NT * half + t)
                act.activation(wide[:], x[:, t, half * R:(half + 1) * R], ACT.Square,
                               accum_out=half_ss[:, half, t:t + 1]).then_inc(s_hss, 1)

            def deviation(kind, t, squares, bias):
                act.activation(stat[:, 3 * kind + 1, t], squares, ACT.Sqrt, scale=1.0 / D, bias=bias
                               ).then_inc(s_sd, 1)

            eps = const[:, C_EPS:C_EPS + 1]

            def w_high(g):
                b, k = STEPS[g]
                act.wait_ge(s_raw[g % RAW], 16 * (g // RAW + 1))
                if g >= RAW:
                    wait_step(act, g - RAW)
                    act.wait_ge(s_wlo, g - RAW + 1)
                act.activation(w_hi[:, g % RAW, :], w_raw[:, g % RAW, :], ACT.Copy,
                               scale=gmix[:, k:k + 1] if b < NB_IN else 1.0).then_inc(s_whi, 1)

            def read_aux(item, dst):
                aux.wait_full(act, item)
                act.activation(dst, heads(aux.bank(item)), ACT.Copy).then_inc(aux.done(item), 1)

            def transposed_high(name, dst, t, half):
                item = (name, t, half)
                aux.wait_full(act, item)
                act.activation(dst[:, half_rows(half), tokens(t)], heads(aux.bank(item)),
                               ACT.Copy).then_inc(s_thi, 1)

            def rows(b, dst, func):
                for t in range(NT):
                    main.wait_full(act, (b, t))
                    act.activation(dst[:, t, :], main.bank((b, t))[:, :], func
                                   ).then_inc(main.done((b, t)), 1)

            for t in range(NT):
                act.wait_ge(s_x[t], 16)
                sum_squares(t, 0, junk[:])
            act.wait_ge(s_const, 16)
            act.wait_ge(s_ss, NT)
            deviation(0, slice(0, NT), stat[:, 0, :], eps)
            act.wait_ge(s_small, small[0])
            w_high(0)
            w_high(1)
            for t in range(NT):
                for half in range(2):
                    transposed_high("hT", hT_hi, t, half)
            act.wait_ge(s_ang, 1)
            act.activation(trig[:], ang[:, 0], ACT.Sin).then_inc(s_trig, 1)

            for g in range(2, NSTEP):
                w_high(g)
                if 16 <= g < 16 + NT:
                    read_aux(("kT", g - 16), kT[:, :, tokens(g - 16)])
                if 24 <= g < 24 + NT:
                    read_aux(("qT", g - 24), qT[:, :, tokens(g - 24)])
                if g == 27:
                    rows(VB, vrow[:].rearrange("p t h d -> p t (h d)"), ACT.Copy)
                if g >= 34 and (g - 34) % 3 == 0 and (g - 34) // 3 < NT:
                    n = (g - 34) // 3
                    read_aux(("o", n), orow[:, n])
                if g == 35:
                    rows(VSB, vsrow, ACT.Gelu)
                if g == 38:
                    act.wait_ge(s_vss, 1)
                    act.activation(vss[:, 1], vss[:, 0], ACT.Sqrt, scale=1.0 / P,
                                   bias=const[:, C_EPS:C_EPS + 1]).then_inc(s_vsd, 1)
                if g == 43:
                    rows(UB, urow, ACT.Gelu)
                if g == 46:
                    act.wait_ge(s_gnv, 1)
                    act.activation(gnrs[:, 0], gnaggr[:, :, :, 1], ACT.Sqrt,
                                   bias=const[:, C_EPS:C_EPS + 1]).then_inc(s_gnd, 1)
                if g == 51:
                    for t in range(NT):
                        transposed_high("mT", mT_hi, t, 1)
                    rows(GB, grow, ACT.Silu)
                if g == 52:
                    for t in range(NT):
                        transposed_high("mT", mT_hi, t, 0)
                if g == 61:
                    for t in range(NT):
                        main.wait_read(act, (NB - 2, t))
                        half_squares(t, 0)
                if g in (62, 63):
                    read_aux(("xT", g - 62, 0), xT[:, half_rows(0), tokens(g - 62)])

            for t in (2, 3):
                read_aux(("xT", t, 0), xT[:, half_rows(0), tokens(t)])
            act.wait_ge(s_hbias, 1)
            for t in range(NT):
                main.wait_read(act, (NB - 1, t))
                half_squares(t, 1)
                read_aux(("xT", t, 1), xT[:, half_rows(1), tokens(t)])
                act.wait_ge(s_hss, NT + t + 1)
                deviation(1, slice(t, t + 1), half_ss[:, 1, t:t + 1], half_ss[:, 2, t:t + 1])
            act.wait_ge(s_rstd, 1)
            main.wait_full(act, (NB - 1, NT - 1))
            for t in range(NT):
                act.activation(hx[:, t, :], x[:, t, :], ACT.Copy, scale=stat[:, 5, t:t + 1]
                               ).then_inc(s_hx, 1)
            act.wait_ge(s_arg, 1)
            act.activation(gexp[:], gsub[:], ACT.Exp).then_inc(s_exp, 1)
            act.wait_ge(s_arg, 2)
            act.activation(e2[:], esub[:], ACT.Exp).then_inc(s_exp, 1)

            def silu(r, q):
                at_least(act, s_gu, r, GP, q + 1)
                act.activation(silu_g[:], gate_up_bank[:, 0:FF], ACT.Silu).then_inc(s_silu, 1)

            def y_left(r, q):
                at_least(act, s_down, r, GP, q + 1)
                at_least(act, s_yout, r, 16 * GP, 16 * q)
                act.activation(ysb[:, 0:R], down_bank[0][:, :], ACT.Copy).then_inc(s_yl, 1)

            def group(r, pairs):
                for q in range(pairs):
                    silu(r, q)
                    y_left(r, q)

            group_loop(act, group)
            with if_crowded(act):
                act.wait_ge(s_yout, 16 * NPAIR)
                with act.Fori(0, NE * NWIN) as n:
                    act.wait_ge(g_gu, n + 1)
                    act.activation(silu_g[0:WIN, :], gate_up_bank[0:WIN, 0:FF], ACT.Silu
                                   ).then_inc(g_silu, 1)
                    act.wait_ge(g_down, n + 1)
                    act.activation(ysb[0:WIN, 0:R], down_bank[0][0:WIN, :], ACT.Copy
                                   ).then_inc(g_yl, 1)
                    act.wait_ge(g_yout, n * 16 + 16)

            for t in range(NT):
                act.wait_ge(s_x2, t + 1)
                sum_squares(t, 2, junk2[:])
                act.wait_ge(s_ss, NT + t + 1)
                deviation(2, slice(t, t + 1), stat[:, 6, t:t + 1], eps)

        @block.gpsimd
        def _(pool):
            own = Chain(pool, c_pool)
            pool.wait_ge(s_const, 16)
            pool.wait_ge(s_small, SMALL)
            for n in range(2 * NT):
                b, t = divmod(n, NT)
                dst, decay = ((krow, C_KD), (qrow, C_QD))[b]
                main.wait_read(pool, (b, t))
                own(pool.tensor_tensor(rot[:, n % 2, 0], rot[:, n % 2, 0], rot[:, n % 2, 1], ALU.add))
                own.settle()
                pool.tensor_tensor(dst[:, t], rot[:, n % 2, 0], spread(const[:, decay:decay + H], DH),
                                   ALU.mult).then_inc(s_rot, 1)
            for t in range(NT):
                main.wait_read(pool, (VSB, t))
                pool.tensor_tensor(vsq[:, t], vsrow4[:, t], vsrow4[:, t], ALU.mult).then_inc(s_vsq, 1)
            for t in range(NT):
                pool.wait_ge(s_vn, t + 1)
                pool.tensor_tensor(vsrow[:, t, :], vsrow[:, t, :], sg_row[:], ALU.mult
                                   ).then_inc(s_vg, 1)
            for n in range(NT):
                pool.wait_ge(s_on, n + 1)
                pool.tensor_tensor(orow_flat[:, n, :], orow_flat[:, n, :], gn_row[:], ALU.mult
                                   ).then_inc(s_og, 1)
            main.wait_full(pool, (NB - 1, NT - 1))
            own(pool.memset(xs[:], 0.0))

            def gather(dst, rows, sem):
                pool.indirect_dma_start(
                    out=dst, out_offset=None, in_=hx_rows[:, :],
                    in_offset=bass.IndirectOffsetOnAxis(ap=rows, axis=0),
                    bounds_check=S - 1, oob_is_err=False).then_inc(sem, 16)

            def scatter(src, rows, sem):
                pool.indirect_dma_start(
                    out=y_rows[:, :], out_offset=bass.IndirectOffsetOnAxis(ap=rows, axis=0),
                    in_=src, in_offset=None,
                    bounds_check=TOPK * S - 1, oob_is_err=False).then_inc(sem, 16)

            def gather_pair(r, q):
                at_least(pool, s_rowof, r, GP, q + 1)
                at_least(pool, s_tr, r, 2 * GP, 2 * q)
                pool.sem_inc(s_turn, 1)
                gather(xs[:], row_of[:, q % GP, 0:1], s_xs)

            def scatter_pair(r, q):
                at_least(pool, s_yl, r, GP, q + 1)
                at_least(pool, s_yr, r, GP, q + 1)
                pool.sem_inc(s_turn, 1)
                scatter(ysb[:], row_of[:, q % GP, 1:2], s_yout)

            pool.wait_ge(s_hxout, 16 * NT)
            own.settle()
            gather_pair(0, 0)
            gather_pair(0, 1)

            def group(r, pairs):
                for q in range(pairs):
                    if comes(r, q + 2):
                        gather_pair(r, q + 2)
                    scatter_pair(r, q)

            group_loop(pool, group)
            with if_crowded(pool):
                pool.wait_ge(s_yout, 16 * NPAIR)
                with pool.Fori(0, NE * NWIN) as n:
                    pool.wait_ge(g_rowof, n + 1)
                    pool.sem_inc(s_turn, 1)
                    gather(xs[0:WIN, :], row_of[0:WIN, 0, 0:1], g_xs)
                    pool.wait_ge(g_yl, n + 1)
                    pool.wait_ge(g_yr, n + 1)
                    pool.sem_inc(s_turn, 1)
                    scatter(ysb[0:WIN, :], row_of[0:WIN, 0, 1:2], g_yout)
                    pool.wait_ge(g_yout, n * 16 + 16)

        @block.vector
        def _(dve):
            own = Chain(dve, c_dve)

            def rstd(kind, t, sds):
                dve.wait_ge(s_sd, sds)
                return dve.reciprocal(stat[:, 3 * kind + 2, t], stat[:, 3 * kind + 1, t])

            def rstd_of(kind, t):
                return stat[:, 3 * kind + 2, t:t + 1]

            def w_low(g):
                b, k = STEPS[g]
                dve.wait_ge(s_whi, g + 1)
                dst, raw, high = w_lo[:, g % RAW, :], w_raw[:, g % RAW, :], w_hi[:, g % RAW, :]
                if b < NB_IN:
                    ins = dve.scalar_tensor_tensor(dst, raw, gmix[:, k:k + 1], high.bitcast(F32),
                                                   ALU.mult, ALU.subtract)
                else:
                    ins = dve.tensor_tensor(dst, raw, high.bitcast(F32), ALU.subtract)
                ins.then_inc(s_wlo, 1)

            made = [0]

            def transposed_low(name, hi, lo, t, half):
                item = (name, t, half)
                made[0] += 1
                dve.wait_ge(s_thi, made[0])
                at = (slice(None), half_rows(half), tokens(t))
                dve.tensor_tensor(lo[at], heads(aux.bank(item)), hi[at].bitcast(F32), ALU.subtract
                                  ).then_inc(aux.done(item), 1)

            def normalise(t):
                dve.tensor_scalar(hrow[:, t % 2, :], x[:, t, :], rstd_of(0, t), None, ALU.mult
                                  ).then_inc(s_h, 1)

            dve.wait_ge(s_small, SMALL)
            own(rstd(0, slice(0, NT), 1))
            own.settle()
            normalise(0)
            normalise(1)
            w_low(0)
            w_low(1)
            for t in range(NT):
                for half in range(2):
                    transposed_low("hT", hT_hi, hT_lo, t, half)
                if t + 2 < NT:
                    normalise(t + 2)

            own(dve.tensor_copy(pos_f[:], pos_i[:]))
            own.settle()
            for c in range(2):
                for t in range(NT):
                    own(dve.tensor_scalar(ang[:, 0, c, t, :], const[:, C_FREQ:C_FREQ + HALF],
                                          pos_f[:, t:t + 1], None, ALU.mult))
            own.settle()
            for c in range(2):
                own(dve.tensor_scalar(ang[:, 1, c], ang[:, 0, c], 1 / (2 * np.pi), 0.25 * c,
                                      ALU.mult, ALU.add))
            own.settle()
            own(dve.tensor_scalar(ang[:, 1], ang[:, 1], MAGIC, MAGIC, ALU.add, ALU.subtract))
            for part in TWO_PI:
                own.settle()
                own(dve.scalar_tensor_tensor(flat(ang[:, 0]), flat(ang[:, 1]), -part, flat(ang[:, 0]),
                                             ALU.mult, ALU.add))
            own.settle()
            own(dve.tensor_scalar(ang[:, 0, 1], ang[:, 0, 1], np.pi / 2, None, ALU.add))
            own.settle()
            dve.tensor_scalar(ang[:, 0], ang[:, 0], PI_BELOW, -PI_BELOW, ALU.min, ALU.max
                              ).then_inc(s_ang, 1)

            dve.tensor_tensor(wrt[:], wrt[:], spread(gffn[:], NE + G), ALU.mult).then_inc(s_wrt, 1)
            own(dve.memset(logit[:, :, NE + G:], NEG))

            def rotate(b, t):
                n = NT * b + t
                main.wait_full(dve, (b, t))
                if n >= 2:
                    dve.wait_ge(s_rot, n - 1)
                ps = main.bank((b, t))[:, :].rearrange("p (x c) -> p x c", c=HALF)
                row = main.bank((b, t))[:, :].rearrange("p (h two c) -> p h two c", two=2, c=HALF)
                a = rot[:, n % 2, 0].rearrange("p h (two c) -> p (h two) c", two=2)
                z = rot[:, n % 2, 1].rearrange("p h (two c) -> p h two c", two=2)
                sin, cos = trig[:, 0, t, :], trig[:, 1, t, :]
                dve.tensor_tensor(a, ps, along(cos, 2 * H), ALU.mult)
                dve.scalar_tensor_tensor(z[:, :, 0, :], row[:, :, 1, :], -1.0, along(sin, H),
                                         ALU.mult, ALU.mult)
                dve.tensor_tensor(z[:, :, 1, :], row[:, :, 0, :], along(sin, H), ALU.mult
                                  ).then_inc(main.done((b, t)), 1)

            def mask(n):
                aux.wait_full(dve, ("scores", n))
                dve.tensor_tensor(scT[:, n % 2], heads(aux.bank(("scores", n))), along(causal, H),
                                  ALU.mult).then_inc(aux.done(("scores", n)), 1)

            def next_state(n):
                aux.wait_full(dve, ("kv", n))
                kv, decay = heads(aux.bank(("kv", n))), spread(const[:, C_CD:C_CD + H], DH)
                if n:
                    own(dve.tensor_tensor(kvt[:], kv, state[:, n % 2], ALU.add))
                    own.settle()
                    kv = kvt[:]
                dve.tensor_tensor(state[:, (n + 1) % 2], kv, decay, ALU.mult
                                  ).then_inc(aux.done(("kv", n)), 1)

            def variance(n):
                aux.wait_read(dve, ("o", n))
                for h in range(H):
                    own(dve.bn_stats(gnstat[:, n, h, :], orow[:, n, h, :]))
                own.settle()
                for h in range(H):
                    ins = dve.bn_aggr(gnaggr[:, n, h, :], gnstat[:, n, h, :])
                    if n == NT - 1 and h == H - 1:
                        ins.then_inc(s_gnv, 1)

            def gate_tokens(t):
                item = ("gating", t)
                aux.wait_full(dve, item)
                main.wait_read(dve, (UB, t))
                for g in range(G):
                    u = urow[:, t, g * P:(g + 1) * P]
                    ins = dve.scalar_tensor_tensor(u, aux.bank(item)[:, g * P:(g + 1) * P],
                                                   bsgu[:, g:g + 1], u, ALU.add, ALU.mult)
                ins.then_inc(aux.done(item), 1)

            def residual(c):
                for t in range(NT):
                    item = (NB_IN + c, t)
                    main.wait_full(dve, item)
                    part = x[:, t, c * R:(c + 1) * R]
                    dve.tensor_tensor(part, main.bank(item)[:, :], part, ALU.add
                                      ).then_inc(main.done(item), 1)

            for g in range(2, NSTEP):
                w_low(g)
                if g == 6:
                    aux.wait_full(dve, ("wT",))
                    dve.tensor_tensor(wT[:], heads(aux.bank(("wT",))), along(causal, G), ALU.mult
                                      ).then_inc(aux.done(("wT",)), 1)
                if g in (11, 12, 19, 20):
                    if g == 11:
                        dve.wait_ge(s_trig, 1)
                    b, first = (g - 11) // 8, 2 * ((g - 11) % 8)
                    rotate(b, first)
                    rotate(b, first + 1)
                for n in range(NT):
                    if g == 32 + 3 * n:
                        mask(n)
                        if n < NT - 1:
                            next_state(n)
                    if g == 35 + 3 * n:
                        variance(n)
                if g == 37:
                    dve.wait_ge(s_vsq, NT)
                    dve.tensor_reduce(vss[:, 0], vsq[:], AX, ALU.add).then_inc(s_vss, 1)
                if g == 39:
                    dve.wait_ge(s_vsd, 1)
                    own(dve.reciprocal(vss[:, 2], vss[:, 1]))
                    own.settle()
                    for t in range(NT):
                        dve.tensor_tensor(vsrow4[:, t], vsrow4[:, t], spread(vss[:, 2, t, :], P),
                                          ALU.mult).then_inc(s_vn, 1)
                for t, step in enumerate((45, 46, 47, 48)):
                    if g == step:
                        gate_tokens(t)
                if g == 49:
                    dve.wait_ge(s_gnd, 1)
                    own(dve.reciprocal(gnrs[:, 1], gnrs[:, 0]))
                    own.settle()
                    for n in range(NT):
                        for h in range(H):
                            row = orow[:, n, h, :]
                            ins = dve.tensor_scalar(row, row, gnaggr[:, n, h, 0:1],
                                                    gnrs[:, 1, n, h:h + 1], ALU.subtract, ALU.mult)
                        ins.then_inc(s_on, 1)
                if g == 51:
                    for t in range(NT):
                        transposed_low("mT", mT_hi, mT_lo, t, 1)
                    for t in range(NT):
                        main.wait_read(dve, (GB, t))
                        dve.wait_ge(s_og, t + 1)
                        dve.tensor_tensor(grow[:, t, :], grow[:, t, :], orow_flat[:, t, :], ALU.mult
                                          ).then_inc(s_mix, 1)
                if g == 52:
                    for t in range(NT):
                        transposed_low("mT", mT_hi, mT_lo, t, 0)
                if g == 59:
                    residual(0)
            dve.wait_ge(s_hss, NT)
            dve.tensor_scalar(half_ss[:, 2], half_ss[:, 0], 1.0 / D, EPS, ALU.mult, ALU.add
                              ).then_inc(s_hbias, 1)
            residual(1)
            rstd(1, slice(0, NT), 1 + NT).then_inc(s_rstd, 1)

            dve.wait_ge(s_rstd, 1)
            main.wait_full(dve, ("logits",))
            raw = main.bank(("logits",))[:, 0:NT * (NE + G)].rearrange("p (t c) -> p t c", t=NT)
            for t in range(NT):
                own(dve.scalar_tensor_tensor(logit[:, t, 0:NE + G], raw[:, t], rstd_of(1, t), brt[:],
                                             ALU.mult, ALU.add))
            own.settle()
            glog, elog = logit[:, :, NE:], logit[:, :, 0:NE].rearrange("p t (g e) -> p t g e", g=G)
            for t in range(NT):
                own(dve.max(gtop[:, t, :], glog[:, t, :]))
            own.settle()
            for t in range(NT):
                own(dve.max_index(gidx[:, t, :], gtop[:, t, :], glog[:, t, :]))
            own.settle()
            own(dve.tensor_tensor(gsel[:], along(const[:, C_I32:C_I32 + G], NT),
                                  spread(gidx[:, :, 0], G), ALU.is_equal))
            own.settle()
            own(dve.tensor_tensor(emul[:], elog, spread(gsel[:], EPG), ALU.mult))
            own.settle()
            own(dve.tensor_reduce(slog[:], emul[:].rearrange("p t g e -> p t e g"), AX, ALU.add))
            own.settle()
            for t in range(NT):
                own(dve.max(etop[:, t, :], slog[:, t, :]))
            own.settle()
            for t in range(NT):
                own(dve.max_index(eidx[:, t, :], etop[:, t, :], slog[:, t, :]))
            own.settle()
            own(dve.scalar_tensor_tensor(eid[:], spread(gidx[:, :, 0], TOPK), float(EPG),
                                         eidx[:, :, 0:TOPK], ALU.mult, ALU.add))
            own.settle()
            own(dve.tensor_tensor(pairs[:].rearrange("p t k e -> p (t k) e"),
                                  along(const[:, C_I32:C_I32 + NE], NT * TOPK),
                                  spread(eid[:].rearrange("p t k -> p (t k)"), NE), ALU.is_equal))
            own.settle()
            dve.tensor_tensor(picked[:], pairs[:, :, 0], pairs[:, :, 1], ALU.add
                              ).then_inc(s_pick, 1)
            dve.tensor_tensor(gsub[:], glog[:, :, 0:G], spread(gtop[:, :, 0], G), ALU.subtract
                              ).then_inc(s_arg, 1)
            dve.tensor_tensor(esub[:], etop[:, :, 1], etop[:, :, 0], ALU.subtract).then_inc(s_arg, 1)

            ranks = ("ranks",)
            main.wait_full(dve, ranks)
            rank = main.bank(ranks)[:, 0:NT * NE].rearrange("p (t e) -> p t e", t=NT)
            total = main.bank(ranks)[:, NT * NE:(NT + 1) * NE]
            own(dve.tensor_tensor(spick[:], pairs[:], rank.unsqueeze(2).broadcast_to([P, NT, TOPK, NE]),
                                  ALU.mult))
            own.settle()
            own(dve.tensor_reduce(place_of[:], spick[:], AX, ALU.add))
            own.settle()

            def one_hots(width, src, sem):
                for t in range(NT):
                    for pick in range(TOPK):
                        ins = dve.tensor_scalar(onehot[:, pick, t, 0:width],
                                                consth[:, H_PLACE:H_PLACE + width],
                                                src[:, t, pick:pick + 1], None, ALU.is_equal)
                ins.then_inc(sem, 1)

            def hot(r, q):
                first = isinstance(r, int) and GP * r + q == 0
                at_least(dve, s_moved, r, GP, q)
                at_least(dve, s_ids, r, GP, q)
                src = place_of if first else place_on
                one_hots(P, src, s_hot)
                at_least(dve, s_hot, r, GP, q + 1)
                dve.tensor_scalar(place_on[:], src[:], -2.0 * RANKS, None, ALU.add
                                  ).then_inc(s_moved, 1)

            def row_numbers(r, q):
                at_least(dve, s_ids, r, GP, q + 1)
                at_least(dve, s_yout, r, 16 * GP, 16 * (q - GP + 1))
                dve.tensor_scalar(row_of[:, q % GP, :], ids_bank[:, 0:2], float(UNUSED), None, ALU.add
                                  ).then_inc(s_rowof, 1)

            hot(0, 0)
            row_numbers(0, 0)
            hot(0, 1)
            row_numbers(0, 1)

            own(dve.tensor_reduce(most[:], total, AX, ALU.max))
            own.settle()
            dve.tensor_scalar(crowded[:], most[:], float(WIN), None, ALU.is_gt).then_inc(s_crowd, 1)

            dve.wait_ge(s_exp, 2)
            own(dve.tensor_reduce(gden[:], gexp[:], AX, ALU.add))
            own(dve.tensor_scalar(eden[:], e2[:], 1.0, None, ALU.add))
            own.settle()
            own(dve.tensor_tensor(eden[:], eden[:], gden[:], ALU.mult))
            own.settle()
            own(dve.reciprocal(gates[:, 0, :], eden[:]))
            own.settle()
            own(dve.tensor_tensor(gates[:, 1, :], gates[:, 0, :], e2[:], ALU.mult))


            def gained(half, width, sem):
                ps = half_bank[half][:, 0:4 * P].rearrange("p (k w) -> p k w", k=4)[:, :, 0:width]
                dve.tensor_tensor(xsT[:, half_rows(half), 0:width], ps,
                                  spread(gffn_s[:, half_rows(half)], width), ALU.mult).then_inc(sem, 1)

            def gained_pair(r, q):
                at_least(dve, s_gu, r, GP, q)
                for half in range(2):
                    at_least(dve, s_tr, r, 2 * GP, 2 * q + half + 1)
                    gained(half, P, s_xsT)

            def multiply(r, q):
                at_least(dve, s_silu, r, GP, q + 1)
                dve.tensor_tensor(acts[:], silu_g[:], gate_up_bank[:, FF:2 * FF], ALU.mult
                                  ).then_inc(s_act, 1)

            def transposed_acts(r, q):
                at_least(dve, s_at, r, GP, q + 1)
                dve.tensor_copy(actT[:], act_bank[:, 0:NF * P].rearrange("p (j w) -> p j w", j=NF)
                                ).then_inc(s_actT, 1)

            def y_right(r, q):
                at_least(dve, s_down, r, GP, q + 1)
                at_least(dve, s_yout, r, 16 * GP, 16 * q)
                dve.tensor_copy(ysb[:, R:D], down_bank[1][:, :]).then_inc(s_yr, 1)

            def group(r, pairs):
                for q in range(pairs):
                    if comes(r, q + 2):
                        hot(r, q + 2)
                    multiply(r, q)
                    transposed_acts(r, q)
                    if comes(r, q + 1):
                        gained_pair(r, q + 1)
                    if comes(r, q + 2):
                        row_numbers(r, q + 2)
                    y_right(r, q)

            gained_pair(0, 0)
            group_loop(dve, group)
            with if_crowded(dve):
                dve.wait_ge(s_yout, 16 * NPAIR)
                dve.tensor_copy(place_on[:], place_of[:]).then_inc(g_moved, 1)
                with dve.Fori(0, NE * NWIN) as n:
                    dve.wait_ge(g_moved, n + 1)
                    one_hots(WIN, place_on, g_hot)
                    dve.wait_ge(g_hot, n + 1)
                    dve.tensor_scalar(place_on[:], place_on[:], -float(WIN), None, ALU.add
                                      ).then_inc(g_moved, 1)
                    dve.wait_ge(g_ids, n + 1)
                    dve.tensor_scalar(row_of[0:WIN, 0, :], ids_bank[0:WIN, 0:2], float(UNUSED), None,
                                      ALU.add).then_inc(g_rowof, 1)
                    for half in range(2):
                        dve.wait_ge(g_tr, n * 2 + (half + 1))
                        gained(half, WIN, g_xsT)
                    dve.wait_ge(g_silu, n + 1)
                    dve.tensor_tensor(acts[0:WIN, :], silu_g[0:WIN, :], gate_up_bank[0:WIN, FF:2 * FF],
                                      ALU.mult).then_inc(g_act, 1)
                    dve.wait_ge(g_at, n + 1)
                    dve.tensor_copy(actT[:], act_bank[:, 0:NF * P].rearrange("p (j w) -> p j w", j=NF)
                                    ).then_inc(g_actT, 1)
                    dve.wait_ge(g_down, n + 1)
                    dve.tensor_copy(ysb[0:WIN, R:D], down_bank[1][0:WIN, :]).then_inc(g_yr, 1)
                    dve.wait_ge(g_yout, n * 16 + 16)

            dve.wait_ge(s_gain, 16)

            def finish(t):
                own(rstd(2, slice(t, t + 1), 2 + NT + t))
                own.settle()
                dve.scalar_tensor_tensor(outrow[:, t, :], x[:, t, :], rstd_of(2, t), gain_row[:],
                                         ALU.mult, ALU.mult).then_inc(s_out, 1)

            for t in range(NT):
                dve.wait_ge(s_gy[t], 16)
                own(dve.scalar_tensor_tensor(x[:, t, :], gy[:, t, 0, :], gates[:, 0, t:t + 1],
                                             x[:, t, :], ALU.mult, ALU.add))
                own.settle()
                dve.scalar_tensor_tensor(x[:, t, :], gy[:, t, 1, :], gates[:, 1, t:t + 1], x[:, t, :],
                                         ALU.mult, ALU.add).then_inc(s_x2, 1)
                if t:
                    finish(t - 1)
            finish(NT - 1)

        @block.tensor
        def _(pe):
            def transposes(item, chunks, last=None):
                for i, chunk in enumerate(chunks):
                    ins = pe.transpose(aux.bank(item)[:, i * P:(i + 1) * P], chunk, ident)
                ins.then_inc(aux.filled(item), 1)

            def every_kth(row, half):
                cols = row[:].rearrange("p (q k) -> p k q", k=ND)
                return [cols[:, 4 * half + i, :] for i in range(4)]

            def head_products(item, left, right):
                for h in range(H):
                    ins = pe.matmul(aux.bank(item)[:, h * P:(h + 1) * P], left(h), right(h),
                                    start=True, stop=True)
                ins.then_inc(aux.filled(item), 1)

            def do(item):
                name, *at = item
                if name not in ("logits", "ranks"):
                    aux.wait_free(pe, item)
                if name == "hT":
                    t, half = at
                    pe.wait_ge(s_h, t + 1)
                    transposes(item, [hrow[:, t % 2, (4 * half + i) * P:(4 * half + i + 1) * P]
                                      for i in range(4)])
                elif name == "wT":
                    pe.wait_ge(s_sgw, 16)
                    transposes(item, [wsraw[:, g, :] for g in range(G)])
                elif name in ("kT", "qT"):
                    t, = at
                    src, b = (krow, 0) if name == "kT" else (qrow, 1)
                    pe.wait_ge(s_rot, NT * b + t + 1)
                    transposes(item, [src[:, t, h, :] for h in range(H)])
                elif name == "scores":
                    n, = at
                    aux.wait_read(pe, ("kT", n))
                    aux.wait_read(pe, ("qT", n))
                    head_products(item, lambda h: kT[:, h, tokens(n)], lambda h: qT[:, h, tokens(n)])
                elif name == "kv":
                    n, = at
                    main.wait_read(pe, (VB, n))
                    head_products(item, lambda h: krow[:, n, h, :], lambda h: vrow[:, n, h, :])
                elif name == "o":
                    n, = at
                    main.wait_read(pe, (VB, n))
                    aux.wait_read(pe, ("scores", n))
                    if n:
                        aux.wait_read(pe, ("kv", n - 1))
                    for h in range(H):
                        dst = aux.bank(item)[:, h * P:(h + 1) * P]
                        ins = pe.matmul(dst, scT[:, n % 2, h, :], vrow[:, n, h, :],
                                        start=True, stop=(n == 0))
                        if n:
                            ins = pe.matmul(dst, qT[:, h, tokens(n)], state[:, n % 2, h, :],
                                            start=False, stop=True)
                    ins.then_inc(aux.filled(item), 1)
                elif name == "gating":
                    t, = at
                    aux.wait_read(pe, ("wT",))
                    pe.wait_ge(s_vg, t + 1)
                    head_products(item, lambda g: wT[:, g, :],
                                  lambda g: vsrow[:, t, g * P:(g + 1) * P])
                elif name == "mT":
                    t, half = at
                    if half:
                        aux.wait_read(pe, ("gating", t))
                    else:
                        pe.wait_ge(s_mix, t + 1)
                    src = urow if half else grow
                    transposes(item, [src[:, t, i * P:(i + 1) * P] for i in range(4)])
                elif name == "xT":
                    t, half = at
                    main.wait_read(pe, (NB - 2 + half, t))
                    transposes(item, [x[:, t, (4 * half + i) * P:(4 * half + i + 1) * P]
                                      for i in range(4)])
                elif name == "logits":
                    t, = at
                    if t == 0:
                        main.wait_free(pe, ("logits",))
                        pe.wait_ge(s_wrt, 1)
                    aux.wait_read(pe, ("xT", t, 0))
                    aux.wait_read(pe, ("xT", t, 1))
                    dst = main.bank(("logits",))[:, t * (NE + G):(t + 1) * (NE + G)]
                    for k in range(ND):
                        ins = pe.matmul(dst, xT[:, k, tokens(t)], wrt[:, k, :],
                                        start=(k == 0), stop=(k == ND - 1))
                    if t == NT - 1:
                        ins.then_inc(main.filled(("logits",)), 1)
                elif name == "ranks":
                    main.wait_free(pe, item)
                    pe.wait_ge(s_pick, 1)
                    for t in range(NT):
                        dst = main.bank(item)[:, t * NE:(t + 1) * NE]
                        pe.matmul(dst, ones, consth[:, H_BASE:H_BASE + NE], start=True, stop=False)
                        for c in range(t + 1):
                            pe.matmul(dst, before if c == t else ones, picked[:, c, :],
                                      start=False, stop=(c == t))
                    for c in range(NT):
                        ins = pe.matmul(main.bank(item)[:, NT * NE:(NT + 1) * NE], ones,
                                        picked[:, c, :], start=(c == 0), stop=(c == NT - 1))
                    ins.then_inc(main.filled(item), 1)

            def step(g):
                b, k = STEPS[g]
                high, low = (hT_hi, hT_lo) if b < NB_IN else (mT_hi, mT_lo)
                first, last = g % ND == 0, g % ND == ND - 1
                pe.wait_ge(s_wlo, g + 1)
                for t in range(NT):
                    if g == NB_IN * ND or g == NB_IN * ND + 4:
                        aux.wait_read(pe, ("mT", t, int(g == NB_IN * ND)))
                    if first:
                        main.wait_free(pe, (b, t))
                    dst = main.bank((b, t))[:, :]
                    slot = g % RAW
                    pe.matmul(dst, high[:, k, tokens(t)], w_hi[:, slot, :], start=first, stop=False)
                    pe.matmul(dst, high[:, k, tokens(t)], w_lo[:, slot, :], start=False, stop=False)
                    ins = pe.matmul(dst, low[:, k, tokens(t)], w_hi[:, slot, :],
                                    start=False, stop=last)
                    if last:
                        ins.then_inc(main.filled((b, t)), 1)
                    elif t == NT - 1:
                        ins.then_inc(s_step, 1)

            pe.wait_ge(s_const, 16)
            todo = list(beside)
            for g in range(-1, NSTEP + 1):
                if g == 0:
                    aux.wait_read(pe, ("hT", NT - 1, 0))
                    aux.wait_read(pe, ("hT", NT - 1, 1))
                if 0 <= g < NSTEP:
                    step(g)
                while todo and todo[0][0] == g:
                    do(todo.pop(0)[1])

            def row_sums(width, sem):
                for pick in range(TOPK):
                    for t in range(NT):
                        c = H_ROW + 2 * (NT * pick + t)
                        ins = pe.matmul(ids_bank[0:width, 0:2], onehot[:, pick, t, 0:width],
                                        consth[:, c:c + 2], start=(pick + t == 0),
                                        stop=(pick == TOPK - 1 and t == NT - 1))
                ins.then_inc(sem, 1)

            def window_halves(sem):
                for half in range(2):
                    for i, cols in enumerate(every_kth(xs, half)):
                        ins = pe.transpose(half_bank[half][:, i * P:(i + 1) * P], cols, ident)
                    ins.then_inc(sem, 1)

            def gate_up(slots):
                for k in range(ND):
                    for i, slot in enumerate(slots):
                        half = slice(i * WIN, (i + 1) * WIN)
                        ins = pe.matmul(gate_up_bank[half, :], xsT[:, k, half],
                                        wgu[slot][:, k].rearrange("p w f -> p (w f)"),
                                        start=(k == 0), stop=(k == ND - 1))
                return ins

            def transposed_acts(sem):
                cols = acts[:].rearrange("p (q j) -> p j q", j=NF)
                for j in range(NF):
                    ins = pe.transpose(act_bank[:, j * P:(j + 1) * P], cols[:, j, :], ident)
                ins.then_inc(sem, 1)

            def down(slots):
                for c in range(2):
                    for f in range(NF):
                        for i, slot in enumerate(slots):
                            half = slice(i * WIN, (i + 1) * WIN)
                            ins = pe.matmul(down_bank[c][half, :], actT[:, f, half],
                                            wd[slot][:, f, c * R:(c + 1) * R],
                                            start=(f == 0), stop=(f == NF - 1))
                return ins

            def pair_rows(r, q):
                at_least(pe, s_hot, r, GP, q + 1)
                at_least(pe, s_rowof, r, GP, q)
                row_sums(P, s_ids)

            def pair_halves(r, q):
                at_least(pe, s_xs, r, 16 * GP, 16 * (q + 1))
                at_least(pe, s_xsT, r, 2 * GP, 2 * q)
                window_halves(s_tr)

            def pair_gate_up(r, q):
                at_least(pe, s_xsT, r, 2 * GP, 2 * q + 2)
                at_least(pe, s_act, r, GP, q)
                at_least(pe, s_wgu[q % GP], r, 64, 64 * (q // GP + 1))
                gate_up((2 * q % RING, 2 * q % RING + 1)).then_inc(s_gu, 1)

            def pair_down(r, q):
                at_least(pe, s_act, r, GP, q + 1)
                transposed_acts(s_at)
                at_least(pe, s_wd[q % GP], r, 32, 32 * (q // GP + 1))
                at_least(pe, s_actT, r, GP, q + 1)
                at_least(pe, s_yl, r, GP, q)
                at_least(pe, s_yr, r, GP, q)
                down((2 * q % RING, 2 * q % RING + 1)).then_inc(s_down, 1)

            def group(r, pairs):
                for q in range(pairs):
                    pair_gate_up(r, q)
                    if comes(r, q + 1):
                        pair_halves(r, q + 1)
                    if comes(r, q + 2):
                        pair_rows(r, q + 2)
                    pair_down(r, q)

            pair_rows(0, 0)
            pair_rows(0, 1)
            pair_halves(0, 0)
            pe.wait_ge(s_crowd, 1)
            group_loop(pe, group)
            with if_crowded(pe):
                pe.wait_ge(s_yl, NPAIR)
                pe.wait_ge(s_yr, NPAIR)
                with pe.Fori(0, NE) as e:
                    with pe.Fori(0, NWIN) as w:
                        n = e * NWIN + w
                        pe.wait_ge(g_hot, n + 1)
                        row_sums(WIN, g_ids)
                        pe.wait_ge(g_xs, n * 16 + 16)
                        window_halves(g_tr)
                        pe.wait_ge(g_xsT, n * 2 + 2)
                        pe.wait_ge(g_w, e * 48 + 48)
                        gate_up((0,)).then_inc(g_gu, 1)
                        pe.wait_ge(g_act, n + 1)
                        transposed_acts(g_at)
                        pe.wait_ge(g_actT, n + 1)
                        down((0,)).then_inc(g_down, 1)
                        pe.wait_ge(g_yl, n + 1)
                        pe.wait_ge(g_yr, n + 1)


def kernel(**inputs):
    from concourse import bacc
    from concourse.bass_utils import run_bass_kernel_spmd

    nc = bacc.Bacc("TRN2", target_bir_lowering=False, num_devices=1)
    wide, half = constants()
    arrays = {"in_" + n: np.ascontiguousarray(inputs[n]) for n in INPUTS}
    arrays["in_constants"], arrays["in_constants_half"] = wide, half
    A = {n[3:]: nc.dram_tensor(n, a.shape, mybir.dt.from_np(a.dtype), kind="ExternalInput").ap()
         for n, a in arrays.items()}
    out = nc.dram_tensor("out", (1, S, D), F32, kind="ExternalOutput").ap()
    build(nc, A, out)
    r = run_bass_kernel_spmd(nc, [arrays], core_ids=[0])
    return r.results[0]["out"]
```

```python
from contextlib import ExitStack

import numpy as np

import concourse.bass as bass
from concourse import mybir

P = 128
F32 = mybir.dt.float32
F32R = mybir.dt.float32r
F16 = mybir.dt.float16
I32 = mybir.dt.int32
U32 = mybir.dt.uint32
ALU = mybir.AluOpType
ACT = mybir.ActivationFunctionType
AX = mybir.AxisListType.X

D = 1024
S = 512
NT = S // P
ND = D // P
H = 4
DH = 128
HALF = DH // 2
R = H * DH
NB_IN = 6
NB = NB_IN + 2
G = 4
EPG = 8
NE = G * EPG
FF = 256
NF = FF // P
TOPK = 2
WIN = 64
RANKS = S
NWIN = RANKS // WIN
UNUSED = 2048
NPAIR = NE // 2
GATE_STEP = 2.0 ** 11
SUMS = 2 * NT
EARLY_SUMS = 6
EPS = 1e-6
ROPE_BASE = 10000.0
NEG = -3.0e38
MAGIC = 1.5 * 2.0 ** 23
PI_BELOW = 3.1415925
TWO_PI = (6.28125, 4059 * 2.0 ** -21, 2 * np.pi - 6.28125 - 4059 * 2.0 ** -21)

RAW = 4
RING = 6
GP = RING // 2
NGROUP = NPAIR // GP
LAST = NPAIR - GP * (NGROUP - 1)
SMALL = 16 * 14

BLOCK_COL = [1, 0, 2, 5, 4, 3]
KB, QB, VB, VSB, UB, GB = range(6)
STEPS = [(b, k) for b in range(NB_IN) for k in range(ND)] + \
        [(NB_IN + c, k) for c in range(2) for k in (4, 5, 6, 7, 0, 1, 2, 3)]
NSTEP = len(STEPS)

C_ID, C_CAUSAL = 0, 128
C_QD, C_KD, C_CD, C_FREQ, C_I32, C_EPS = 256, 260, 264, 268, 332, 364
C_N = 368
H_BEFORE, H_ONES, H_PLACE, H_BASE, H_TOKEN, H_NUMBER = 0, 128, 256, 384, 416, 420
H_N = H_NUMBER + S


def constants():
    c = np.zeros((P, C_N), np.float32)
    i = np.arange(P, dtype=np.float64)
    c[:, C_ID:C_ID + P] = np.eye(P)
    c[:, C_CAUSAL:C_CAUSAL + P] = i[:, None] <= i[None, :]
    gamma = 1.0 - 2.0 ** (-5.0 - np.arange(H))
    c[:, C_QD:C_QD + H] = gamma[None, :] ** (i[:, None] + 1)
    c[:, C_KD:C_KD + H] = gamma[None, :] ** -(i[:, None] + 1) * DH ** -0.5
    c[:, C_CD:C_CD + H] = gamma[None, :] ** P
    c[:, C_FREQ:C_FREQ + HALF] = ROPE_BASE ** (-np.arange(HALF) * 2.0 / DH)
    c[:, C_I32:C_I32 + NE] = np.arange(NE)
    c[:, C_EPS] = EPS
    h = np.zeros((P, H_N), np.float16)
    h[:, H_BEFORE:H_BEFORE + P] = i[:, None] < i[None, :]
    h[:, H_ONES:H_ONES + P] = 1.0
    h[:, H_PLACE:H_PLACE + P] = np.arange(P) % WIN + RANKS * (np.arange(P) // WIN)
    h[:, H_BASE:H_BASE + NE] = np.arange(NE) * (RANKS // P)
    h[:, H_TOKEN:H_TOKEN + NT] = i[:, None] + P * np.arange(NT) - UNUSED
    h[:, H_NUMBER:H_NUMBER + S] = np.arange(S)
    return c, h



class Banks:

    def __init__(self, banks, full, read):
        self.banks, self.full, self.read, self.order = banks, full, read, {}

    def add(self, item):
        self.order[item] = len(self.order)

    def turn(self, item):
        return self.order[item] % len(self.banks), self.order[item] // len(self.banks)

    def bank(self, item):
        return self.banks[self.turn(item)[0]]

    def filled(self, item):
        return self.full[self.turn(item)[0]]

    def done(self, item):
        return self.read[self.turn(item)[0]]

    def wait_free(self, eng, item):
        i, before = self.turn(item)
        if before:
            eng.wait_ge(self.read[i], before)

    def wait_full(self, eng, item):
        i, before = self.turn(item)
        eng.wait_ge(self.full[i], before + 1)

    def wait_read(self, eng, item):
        i, before = self.turn(item)
        eng.wait_ge(self.read[i], before + 1)


class Chain:

    def __init__(self, eng, sem):
        self.eng, self.sem, self.n = eng, sem, 0

    def __call__(self, ins):
        ins.then_inc(self.sem, 1)
        self.n += 1

    def settle(self):
        self.eng.wait_ge(self.sem, self.n)


INPUTS = ["x", "positions", "norm_mix_gain", "w_in", "ret_gn_gain", "sgu_norm_gain", "sgu_w", "sgu_b",
          "w_out", "norm_ffn_gain", "w_router_group", "b_router_group", "w_router_expert",
          "b_router_expert", "w_expert_gate_up", "w_expert_up", "w_expert_down", "final_norm_gain"]


def flat(ap):
    return ap.rearrange("p a b c -> p (a b c)")


def build(nc, A, out):
    ctx = ExitStack()
    with ctx:
        at = {"next": 0}
        base = (nc.sbuf_base + 63) // 64 * 64

        def place(name, shape, dt, offset):
            return nc.alloc_sbuf_tensor_at("sb_" + name, list(shape), dt, offset=base + offset)

        def sb(name, shape, dt=F32):
            size = int(np.prod(shape[1:])) * (2 if dt == F16 else 4)
            t = place(name, shape, dt, at["next"])
            at["next"] += (size + 31) // 32 * 32
            return t

        def psum(name):
            return ctx.enter_context(nc.psum_tensor("ps_" + name, [P, 512], F32))

        def sem(name):
            return ctx.enter_context(nc.semaphore(name))

        KiB = 1024
        const = sb("const", [P, C_N])
        consth = sb("consth", [P, H_N], F16)
        gmix = sb("gmix", [P, ND])
        gffn = sb("gffn", [P, ND])
        gffn_s = sb("gffn_s", [P, ND])
        bsgu = sb("bsgu", [P, G])
        brt = sb("brt", [P, NE + G])
        wrt = sb("wrt", [P, ND, NE + G])
        pos_i = sb("pos_i", [P, NT], I32)
        pos_f = sb("pos_f", [P, NT])
        stat = sb("stat", [P, 3 * 3, NT])
        half_ss = sb("half_ss", [P, 6, NT])
        gnstat = sb("gnstat", [P, NT, H, 6])
        gnaggr = sb("gnaggr", [P, NT, H, 2])
        gnrs = sb("gnrs", [P, 2, NT, H])
        vss = sb("vss", [P, 3, NT, G])
        actT = sb("actT", [P, NF, P])
        silu_g = sb("silu_g", [P, FF])
        acts = sb("acts", [P, FF])
        crowded = sb("crowded", [P, 1], I32)
        most = sb("most", [P, 1])
        gsub = sb("gsub", [P, NT, G])
        esub = sb("esub", [P, NT])
        e2 = sb("e2", [P, NT])
        gden = sb("gden", [P, NT])
        eden = sb("eden", [P, NT])
        gates = sb("gates", [P, TOPK, NT])
        gain_row = sb("gain_row", [P, D])
        logit = sb("logit", [P, NT, NE + 8])
        gtop = sb("gtop", [P, NT, 8])
        gidx = sb("gidx", [P, NT, 8], U32)
        gsel = sb("gsel", [P, NT, G])
        emul = sb("emul", [P, NT, G, EPG])
        slog = sb("slog", [P, NT, EPG])
        etop = sb("etop", [P, NT, 8])
        eidx = sb("eidx", [P, NT, 8], U32)
        gexp = sb("gexp", [P, NT, G])
        eid = sb("eid", [P, NT, TOPK])
        pairs = sb("pairs", [P, NT, TOPK, NE], F16)
        picked = sb("picked", [P, NT, NE], F16)
        spick = sb("spick", [P, NT, TOPK, NE])
        place_of = sb("place_of", [P, NT, TOPK])
        place_on = sb("place_on", [P, NT, TOPK])
        onehot = sb("onehot", [P, TOPK, NT, P], F16)
        values = sb("values", [P, TOPK, NT, 4], F16)
        rest = sb("rest", [P, TOPK, NT])
        scaled = sb("scaled", [P, 2, TOPK, NT])
        row_of = sb("row_of", [P, GP, 1], I32)
        summed = sb("summed", [P, GP, 4])
        token_of = sb("token_of", [P, 1])
        gate_rest = sb("gate_rest", [P, 1])
        gate_of = sb("gate_of", [P, 1])
        used = sb("used", [P, NT, TOPK])
        spread_to = place("spread_to", [P, S], F32R, at["next"])
        at["next"] += 2 * KiB
        root_loaded = sb("root_loaded", [P, 1])
        root_again = sb("root_again", [P, 1])
        wide = sb("wide", [P, R])
        x = sb("x", [P, NT, D])

        arena = at["next"]
        w_raw = place("w_raw", [P, RAW, R], F32, arena)
        w_hi = place("w_hi", [P, RAW, R], F32R, arena + 8 * KiB)
        w_lo = place("w_lo", [P, RAW, R], F32R, arena + 16 * KiB)
        xs = [place(f"xs{i}", [P, D], F32, arena + at_kib * KiB) for i, at_kib in enumerate((0, 20, 16))]
        hx = place("hx", [P, NT, D], F32, arena + 4 * KiB)
        xsT = place("xsT", [P, ND, P], F32, arena + 4 * KiB)
        y_hi = place("y_hi", [P, D], F32R, arena + 8 * KiB)
        y_lo = place("y_lo", [P, D], F32R, arena + 12 * KiB)
        at["next"] = arena + 24 * KiB
        ring = at["next"]
        slot_size = 24 * KiB
        wgu = [place(f"wgu{i}", [P, ND, 2, FF], F32, ring + slot_size * i) for i in range(RING)]
        wd = [place(f"wd{i}", [P, NF, D], F32, ring + slot_size * i + 16 * KiB) for i in range(RING)]
        rows = ring + slot_size
        krow = place("krow", [P, NT, H, DH], F32, rows)
        vrow = place("vrow", [P, NT, H, DH], F32, rows + 8 * KiB)
        kT = place("kT", [P, H, S], F32, rows + 16 * KiB)
        qT = place("qT", [P, H, S], F32, rows + 24 * KiB)
        orow = place("orow", [P, NT, H, DH], F32, rows + 32 * KiB)
        grow = place("grow", [P, NT, R], F32, rows + 40 * KiB)
        urow = place("urow", [P, NT, R], F32, rows + 48 * KiB)
        vsrow = place("vsrow", [P, NT, R], F32, rows + 56 * KiB)
        state = place("state", [P, 2, H, DH], F32, rows + 64 * KiB)
        scT = place("scT", [P, 2, H, DH], F32, rows + 68 * KiB)
        hrow = place("hrow", [P, 2, D], F32, rows + 32 * KiB)
        qk_row = place("qk_row", [P, NT, R], F32, rows + 32 * KiB)
        rot = place("rot", [P, 2, 2, H, DH], F32, rows + 40 * KiB)
        qrow = place("qrow", [P, NT, H, DH], F32, rows + 48 * KiB)
        vsq = place("vsq", [P, NT, G, P], F32, rows + 48 * KiB)
        junk = place("junk", [P, D], F32, rows + 56 * KiB)
        wsraw = place("wsraw", [P, G, P], F32, rows + 60 * KiB)
        ang = place("ang", [P, 2, 2, NT, HALF], F32, rows)
        xT = place("xT", [P, ND, S], F32, rows + 104 * KiB)
        hT_hi = place("hT_hi", [P, ND, S], F32R, rows + 72 * KiB)
        hT_lo = place("hT_lo", [P, ND, S], F32R, rows + 88 * KiB)
        mT_hi = place("mT_hi", [P, ND, S], F32R, rows + 72 * KiB)
        mT_lo = place("mT_lo", [P, ND, S], F32R, rows + 88 * KiB)
        trig = place("trig", [P, 2, NT, HALF], F32, rows + 104 * KiB)
        sg_row = place("sg_row", [P, R], F32, rows + 106 * KiB)
        gn_row = place("gn_row", [P, R], F32, rows + 108 * KiB)
        wT = place("wT", [P, G, P], F32, rows + 110 * KiB)
        kvt = place("kvt", [P, H, DH], F32, rows + 112 * KiB)
        outrow = place("outrow", [P, NT, D], F32, ring)
        junk2 = place("junk2", [P, D], F32, ring + 16 * KiB)
        at["next"] = ring + RING * slot_size
        assert base + at["next"] <= nc.sbuf_usable_end, (base + at["next"], nc.sbuf_usable_end)

        orow_flat = orow[:].rearrange("p t h d -> p t (h d)")
        vsrow4 = vsrow[:].rearrange("p t (g c) -> p t g c", g=G)
        bk = [psum(f"bank{i}") for i in range(8)]

        hx_rows = nc.dram_tensor("hx_rows", [S, D], F32).ap()

        s_x = [sem(f"x_loaded{t}") for t in range(NT)]
        s_const = sem("constants_loaded")
        s_gmix = sem("mix_gain_loaded")
        s_small = sem("small_inputs_loaded")
        s_sgw = sem("sgu_w_loaded")
        s_gain = sem("row_gain_loaded")
        s_raw = [sem(f"w_raw_loaded{i}") for i in range(RAW)]
        s_whi = sem("w_high_made")
        s_wlo = sem("w_low_made")
        s_step = sem("dense_step_done")
        s_ss = sem("squares_summed")
        s_sd = sem("deviation_made")
        s_h = sem("normalised_rows_made")
        s_thi = sem("transposed_high_made")
        s_ang = sem("angles_reduced")
        s_trig = sem("sin_cos_made")
        s_turned = sem("rotation_parts_made")
        s_rot = sem("rotated_rows_made")
        s_vsq = sem("gating_squares_made")
        s_vss = sem("gating_sums_made")
        s_vsd = sem("gating_deviation_made")
        s_vn = sem("gating_v_scaled")
        s_vg = sem("gating_v_normalised")
        s_gnv = sem("retention_variance_made")
        s_gnd = sem("retention_deviation_made")
        s_on = sem("retention_normalised")
        s_og = sem("retention_gained")
        s_mix = sem("retention_mix_made")
        s_wrt = sem("router_weights_scaled")
        s_hss = sem("half_squares_summed")
        s_hbias = sem("first_half_squares_biased")
        s_rstd = sem("ffn_scale_made")
        s_hx = sem("scaled_rows_made")
        s_hxout = sem("scaled_rows_stored")
        s_arg = sem("softmax_arguments_made")
        s_exp = sem("softmax_exponentials_made")
        s_gates = sem("gates_made")
        s_values = sem("gate_parts_made")
        s_pick = sem("pairs_picked")
        s_crowd = sem("crowding_known")
        s_hot = sem("place_one_hots_made")
        s_moved = sem("places_moved_on")
        s_ids = sem("row_numbers_summed")
        s_rowof = sem("row_numbers_made")
        s_xs = [sem(f"window_rows_gathered{q}") for q in range(GP)]
        s_tr = sem("window_halves_transposed")
        s_xsT = sem("window_halves_ready")
        s_auxf = [sem(f"aux_bank_full{i}") for i in range(2)]
        s_auxr = [sem(f"aux_bank_read{i}") for i in range(2)]
        s_earlyf = [sem(f"early_bank_full{i}") for i in range(4)]
        s_earlyr = [sem(f"early_bank_read{i}") for i in range(4)]
        s_mainf = [sem(f"main_bank_full{i}") for i in range(6)]
        s_mainr = [sem(f"main_bank_read{i}") for i in range(6)]
        s_wgu = [sem(f"gate_up_weights_loaded{q}") for q in range(GP)]
        s_wd = [sem(f"down_weights_loaded{q}") for q in range(GP)]
        s_gu = sem("gate_up_done")
        s_silu = sem("silu_made")
        s_act = sem("activation_made")
        s_at = sem("activation_transposed")
        s_actT = sem("transposed_activation_ready")
        s_down = sem("down_done")
        s_summed = sem("place_values_read")
        s_gpart = sem("place_gate_rests_made")
        s_slotv = sem("place_gates_made")
        s_yhi = sem("gated_high_made")
        s_ylo = sem("gated_low_made")
        s_spread = sem("spreading_one_hots_made")
        s_sum = sem("token_sums_done")
        s_added = sem("token_sums_added")
        g_w = sem("general_weights_loaded")
        g_hot = sem("general_one_hots_made")
        g_moved = sem("general_places_moved_on")
        g_ids = sem("general_row_numbers_summed")
        g_rowof = sem("general_row_numbers_made")
        g_xs = sem("general_rows_gathered")
        g_tr = sem("general_halves_transposed")
        g_xsT = sem("general_halves_ready")
        g_gu = sem("general_gate_up_done")
        g_silu = sem("general_silu_made")
        g_act = sem("general_activation_made")
        g_at = sem("general_activation_transposed")
        g_actT = sem("general_transposed_activation_ready")
        g_down = sem("general_down_done")
        g_summed = sem("general_place_values_read")
        g_gpart = sem("general_place_gate_rests_made")
        g_slotv = sem("general_place_gates_made")
        g_yhi = sem("general_gated_high_made")
        g_ylo = sem("general_gated_low_made")
        g_spread = sem("general_spreading_one_hots_made")
        g_sum = sem("general_token_sums_done")
        g_added = sem("general_token_sums_added")
        g_prep = sem("general_preparation_steps")
        s_rstd2 = sem("final_scale_made")
        s_out = sem("rows_finished")
        s_turn = sem("indirect_queue_turn")
        s_stored = sem("output_stored")
        c_act = sem("scalar_own_results")
        c_dve = sem("vector_own_results")
        c_pool = sem("pool_own_results")

        main = Banks(bk[:6], s_mainf, s_mainr)
        for b in range(NB):
            for t in range(NT):
                main.add((b, t))
        for t in range(NT):
            main.add(("logits", t))
        main.add(("ranks",))
        beside = [(-1, ("hT", t, half)) for t in range(NT) for half in range(2)]
        beside += [(2, ("wT",))]
        beside += [(12 + t, ("kT", t)) for t in range(NT)]
        beside += [(20 + t, ("qT", t)) for t in range(NT)]
        for n in range(NT):
            beside += [(28 + 3 * n, ("scores", n)), (30 + 3 * n, ("o", n))]
            if n < NT - 1:
                beside += [(28 + 3 * n, ("kv", n))]
        beside += [(41 + t, ("gating", t)) for t in range(NT)]
        beside += [(46 + t // 2, ("mT", t, 1)) for t in range(NT)]
        beside += [(49 + t // 2, ("mT", t, 0)) for t in range(NT)]
        beside += [(58 + t, ("xT", t, 0)) for t in range(NT)]
        beside += [(NSTEP - 1, ("logits", t, 0)) for t in range(2)]
        beside += [(NSTEP, ("xT", t, 1)) for t in range(2)]
        beside += [(NSTEP, ("logits", 0, 1)), (NSTEP, ("xT", 2, 1)), (NSTEP, ("logits", 1, 1)),
                   (NSTEP, ("xT", 3, 1))]
        beside += [(NSTEP, ("logits", t, half)) for t in (2, 3) for half in range(2)]
        beside += [(NSTEP, ("ranks",))]
        beside.sort(key=lambda entry: entry[0])
        aux = Banks(bk[6:], s_auxf, s_auxr)
        early = Banks(bk[2:6], s_earlyf, s_earlyr)
        for _, item in beside:
            if item[0] == "hT":
                early.add(item)
            elif item[0] not in ("logits", "ranks"):
                aux.add(item)

        def banks_of(item):
            return early if item[0] == "hT" else aux

        def heads(bank):
            return bank[:, :].rearrange("p (h d) -> p h d", h=H)

        ident = const[:, C_ID:C_ID + P]
        causal = const[:, C_CAUSAL:C_CAUSAL + P]
        before = consth[:, H_BEFORE:H_BEFORE + P]
        ones = consth[:, H_ONES:H_ONES + P]

        def along(ap, n):
            return ap.unsqueeze(1).broadcast_to([P, n, ap.shape[1]])

        def spread(ap, n):
            return ap.unsqueeze(len(ap.shape)).broadcast_to([*ap.shape, n])

        w_gate = A["w_expert_gate_up"].rearrange("l g e (p k) f -> (l g e) p k f", p=P)
        w_up = A["w_expert_up"].rearrange("l g e (p k) f -> (l g e) p k f", p=P)
        w_down = A["w_expert_down"].rearrange("l g e (p j) n -> (l g e) p j n", p=P)

        def one(ap, e):
            return ap[bass.ds(e, 1)].squeeze(0) if not isinstance(e, int) else ap[e]

        block = ctx.enter_context(nc.Block())

        def at_least(eng, sem, i, mul, add):
            if isinstance(i, int):
                if mul * i + add > 0:
                    eng.wait_ge(sem, mul * i + add)
            else:
                eng.wait_ge(sem, i * mul + add)

        def group_loop(eng, group):
            group(0, GP)
            with eng.Fori(1, NGROUP - 1) as r:
                group(r, GP)
            group(NGROUP - 1, LAST)

        def comes(r, q):
            return not isinstance(r, int) or GP * r + q < NPAIR

        def if_crowded(eng):
            eng.wait_ge(s_crowd, 1)
            return eng.If(eng.value_load(crowded[0:1, 0:1], min_val=0, max_val=1) >= 1)

        gate_up_bank, act_bank = bk[0], bk[1]
        down_bank = [bk[2], bk[3]]
        ids_bank = bk[1]
        NUMBERS = NF * P
        sum_bank = [bk[4], bk[5]]
        last_sum_bank = [bk[4], bk[5], bk[6], bk[7]]
        half_bank = [bk[6], bk[7]]

        def wait_step(eng, g):
            if g % ND == ND - 1:
                main.wait_full(eng, (STEPS[g][0], NT - 1))
            else:
                eng.wait_ge(s_step, g + 1 - g // ND)

        def tokens(t):
            return slice(t * P, (t + 1) * P)

        def half_rows(half):
            return slice(4 * half, 4 * half + 4)

        @block.sync
        def _(sp):
            for t in range(NT):
                sp.dma_start(x[:, t, :], A["x"][0, tokens(t), :]).then_inc(s_x[t], 16)

            def gate(slot, e, sem):
                sp.dma_start(wgu[slot][:, :, 0, :], one(w_gate, e)).then_inc(sem, 16)

            def up(slot, e, sem):
                sp.dma_start(wgu[slot][:, :, 1, :], one(w_up, e)).then_inc(sem, 16)

            def gate_up(slot, e, sem):
                gate(slot, e, sem)
                up(slot, e, sem)

            def down(slot, e, sem):
                sp.dma_start(wd[slot][:], one(w_down, e)).then_inc(sem, 16)

            for g, (b, k) in enumerate(STEPS):
                if g >= RAW:
                    sp.wait_ge(s_whi, g - RAW + 1)
                    sp.wait_ge(s_wlo, g - RAW + 1)
                if b < NB_IN:
                    src = A["w_in"][0, tokens(k), BLOCK_COL[b] * R:(BLOCK_COL[b] + 1) * R]
                else:
                    src = A["w_out"][0, tokens(k), (b - NB_IN) * R:(b - NB_IN + 1) * R]
                sp.dma_start(w_raw[:, g % RAW, :], src).then_inc(s_raw[g % RAW], 16)
                if g == 8:
                    gate_up(0, 0, s_wgu[0])
                    down(0, 0, s_wd[0])
                if g == 57:
                    aux.wait_read(sp, ("mT", NT - 2, 0))
                    aux.wait_read(sp, ("mT", NT - 1, 0))
                    gate(1, 1, s_wgu[0])
                if g == 58:
                    up(1, 1, s_wgu[0])
                if g == 59:
                    down(1, 1, s_wd[0])
                if g == 60:
                    gate(2, 2, s_wgu[1])
                if g == 61:
                    up(2, 2, s_wgu[1])
            down(2, 2, s_wd[1])
            gate_up(3, 3, s_wgu[1])
            down(3, 3, s_wd[1])
            main.wait_full(sp, (NB - 1, NT - 1))
            gate_up(4, 4, s_wgu[2])
            down(4, 4, s_wd[2])
            for t in range(NT):
                sp.wait_ge(s_hx, t + 1)
                sp.dma_start(hx_rows[tokens(t), :], hx[:, t, :]).then_inc(s_hxout, 16)
            sp.wait_ge(s_xs[0], 16)
            main.wait_full(sp, ("logits", NT - 1))
            gate_up(5, 5, s_wgu[2])
            down(5, 5, s_wd[2])

            def group(r, pairs):
                for q in range(pairs):
                    e = r * RING + (2 * q + RING)
                    at_least(sp, s_gu, r, GP, q + 1)
                    for i in range(2):
                        gate_up(2 * q + i, e + i, s_wgu[q])
                    at_least(sp, s_down, r, 2 * GP, 2 * q + 2)
                    for i in range(2):
                        down(2 * q + i, e + i, s_wd[q])

            group(0, GP)
            with sp.Fori(1, NGROUP - 1) as r:
                group(r, GP)
            group(NGROUP - 1, LAST - GP)
            sp.wait_ge(s_down, 2 * NPAIR)
            with if_crowded(sp):
                gate_up(0, 0, g_w)
                down(0, 0, g_w)
                with sp.Fori(1, NE) as e:
                    sp.wait_ge(g_down, e * (2 * NWIN))
                    gate_up(0, e, g_w)
                    down(0, e, g_w)
            for t in range(NT):
                sp.wait_ge(s_out, t + 1)
                sp.dma_start(out[0, tokens(t), :], outrow[:, t, :]).then_inc(s_stored, 16)
            sp.wait_ge(s_stored, 16 * NT)

        @block.scalar
        def _(act):
            act.dma_start(const[:], A["constants"]).then_inc(s_const, 16)
            act.dma_start(gmix[:], A["norm_mix_gain"].rearrange("a (k p) -> p (a k)", p=P),
                          allow_slow_non_contiguous=True).then_inc(s_gmix, 16)

            def sum_squares(t, kind, scratch):
                if kind + t:
                    act.wait_ge(s_ss, NT * (kind // 2) + t)
                act.activation(scratch, x[:, t, :], ACT.Square,
                               accum_out=stat[:, 3 * kind, t:t + 1]).then_inc(s_ss, 1)

            def half_squares(t, half, norm=0):
                before = NT * (2 * norm + half) + t
                if before:
                    act.wait_ge(s_hss, before)
                act.activation(wide[:], x[:, t, half * R:(half + 1) * R], ACT.Square,
                               accum_out=half_ss[:, 3 * norm + half, t:t + 1]).then_inc(s_hss, 1)

            def deviation(kind, t, squares, bias):
                act.activation(stat[:, 3 * kind + 1, t], squares, ACT.Sqrt, scale=1.0 / D, bias=bias
                               ).then_inc(s_sd, 1)

            eps = const[:, C_EPS:C_EPS + 1]

            def w_high(g):
                b, k = STEPS[g]
                act.wait_ge(s_raw[g % RAW], 16 * (g // RAW + 1))
                if g >= RAW:
                    wait_step(act, g - RAW)
                    act.wait_ge(s_wlo, g - RAW + 1)
                act.activation(w_hi[:, g % RAW, :], w_raw[:, g % RAW, :], ACT.Copy,
                               scale=gmix[:, k:k + 1] if b < NB_IN else 1.0).then_inc(s_whi, 1)

            def read_aux(item, dst):
                aux.wait_full(act, item)
                act.activation(dst, heads(aux.bank(item)), ACT.Copy).then_inc(aux.done(item), 1)

            def transposed_high(name, dst, t, half):
                item = (name, t, half)
                banks_of(item).wait_full(act, item)
                act.activation(dst[:, half_rows(half), tokens(t)], heads(banks_of(item).bank(item)),
                               ACT.Copy).then_inc(s_thi, 1)

            def rows(b, dst, func):
                for t in range(NT):
                    main.wait_full(act, (b, t))
                    act.activation(dst[:, t, :], main.bank((b, t))[:, :], func
                                   ).then_inc(main.done((b, t)), 1)

            for t in range(NT):
                act.wait_ge(s_x[t], 16)
                sum_squares(t, 0, junk[:])
                act.wait_ge(s_const, 16)
                act.wait_ge(s_ss, t + 1)
                deviation(0, slice(t, t + 1), stat[:, 0, t:t + 1], eps)
                if t:
                    for half in range(2):
                        transposed_high("hT", hT_hi, t - 1, half)
            act.wait_ge(s_gmix, 16)
            w_high(0)
            w_high(1)
            for half in range(2):
                transposed_high("hT", hT_hi, NT - 1, half)
            for g in range(2, NSTEP):
                w_high(g)
                if g == 6:
                    act.wait_ge(s_ang, 1)
                    act.activation(trig[:], ang[:, 0], ACT.Sin).then_inc(s_trig, 1)
                if g in (11, 19):
                    if g == 19:
                        act.wait_ge(s_turned, NT)
                    rows(KB if g == 11 else QB, qk_row, ACT.Copy)
                if 16 <= g < 16 + NT:
                    read_aux(("kT", g - 16), kT[:, :, tokens(g - 16)])
                if 24 <= g < 24 + NT:
                    read_aux(("qT", g - 24), qT[:, :, tokens(g - 24)])
                if g == 27:
                    rows(VB, vrow[:].rearrange("p t h d -> p t (h d)"), ACT.Copy)
                if g >= 34 and (g - 34) % 3 == 0 and (g - 34) // 3 < NT:
                    n = (g - 34) // 3
                    read_aux(("o", n), orow[:, n])
                if g == 35:
                    rows(VSB, vsrow, ACT.Gelu)
                if g == 38:
                    act.wait_ge(s_vss, 1)
                    act.activation(vss[:, 1], vss[:, 0], ACT.Sqrt, scale=1.0 / P,
                                   bias=const[:, C_EPS:C_EPS + 1]).then_inc(s_vsd, 1)
                if g == 43:
                    rows(UB, urow, ACT.Gelu)
                if g == 46:
                    act.wait_ge(s_gnv, 1)
                    act.activation(gnrs[:, 0], gnaggr[:, :, :, 1], ACT.Sqrt,
                                   bias=const[:, C_EPS:C_EPS + 1]).then_inc(s_gnd, 1)
                if g == 51:
                    for t in range(NT):
                        transposed_high("mT", mT_hi, t, 1)
                    rows(GB, grow, ACT.Silu)
                if g == 52:
                    for t in range(NT):
                        transposed_high("mT", mT_hi, t, 0)
                if g == 61:
                    for t in range(NT):
                        main.wait_read(act, (NB - 2, t))
                        half_squares(t, 0)
                    act.activation(root_loaded[:], eps, ACT.Sqrt)
                if g in (62, 63):
                    read_aux(("xT", g - 62, 0), xT[:, half_rows(0), tokens(g - 62)])

            for t in (2, 3):
                read_aux(("xT", t, 0), xT[:, half_rows(0), tokens(t)])
            act.wait_ge(s_hbias, 1)
            for t in range(NT):
                main.wait_read(act, (NB - 1, t))
                half_squares(t, 1)
                read_aux(("xT", t, 1), xT[:, half_rows(1), tokens(t)])
                act.wait_ge(s_hss, NT + t + 1)
                deviation(1, slice(t, t + 1), half_ss[:, 1, t:t + 1], half_ss[:, 2, t:t + 1])
            act.wait_ge(s_rstd, 1)
            main.wait_full(act, (NB - 1, NT - 1))
            for t in range(NT):
                act.activation(hx[:, t, :], x[:, t, :], ACT.Copy, scale=stat[:, 5, t:t + 1]
                               ).then_inc(s_hx, 1)
            act.wait_ge(s_arg, 1)
            act.activation(gexp[:], gsub[:], ACT.Exp).then_inc(s_exp, 1)
            act.wait_ge(s_arg, 2)
            act.activation(e2[:], esub[:], ACT.Exp).then_inc(s_exp, 1)

            def silu(r, q):
                at_least(act, s_gu, r, GP, q + 1)
                act.activation(silu_g[:], gate_up_bank[:, 0:FF], ACT.Silu).then_inc(s_silu, 1)

            def gated_high(r, q):
                for c in range(2):
                    at_least(act, s_down, r, 2 * GP, 2 * q + c + 1)
                    act.activation(y_hi[:, c * R:(c + 1) * R], down_bank[c][:, :], ACT.Copy,
                                   scale=gate_of[:, 0:1]).then_inc(s_yhi, 1)

            def group(r, pairs):
                for q in range(pairs):
                    silu(r, q)
                    at_least(act, s_slotv, r, GP, q + 1)
                    gated_high(r, q)

            group_loop(act, group)
            with if_crowded(act):
                with act.Fori(0, NE * NWIN) as n:
                    act.wait_ge(g_gu, n + 1)
                    act.activation(silu_g[0:WIN, :], gate_up_bank[0:WIN, 0:FF], ACT.Silu
                                   ).then_inc(g_silu, 1)
                    for c in range(2):
                        act.wait_ge(g_down, n * 2 + (c + 1))
                        act.activation(y_hi[0:WIN, c * R:(c + 1) * R], down_bank[c][0:WIN, :], ACT.Copy,
                                       scale=gate_of[0:WIN, 0:1]).then_inc(g_yhi, 1)
                act.wait_ge(g_added, SUMS * NE * NWIN)

            for t in range(NT):
                act.wait_ge(s_added, SUMS * (NPAIR - 1) + t + 1)
                half_squares(t, 0, 1)
            act.activation(root_again[:], eps, ACT.Sqrt)
            for t in range(NT):
                act.wait_ge(s_added, SUMS * (NPAIR - 1) + NT + t + 1)
                half_squares(t, 1, 1)
                act.wait_ge(s_hbias, 2)
                act.wait_ge(s_hss, 3 * NT + t + 1)
                deviation(2, slice(t, t + 1), half_ss[:, 4, t:t + 1], half_ss[:, 5, t:t + 1])

        @block.gpsimd
        def _(pool):
            own = Chain(pool, c_pool)

            def load(dst, src, slow=False):
                pool.dma_start(dst, src, allow_slow_non_contiguous=slow).then_inc(s_small, 16)

            pool.dma_start(wsraw[:], A["sgu_w"].rearrange("a g i j -> i (a g) j")).then_inc(s_sgw, 16)
            load(pos_i[:], A["positions"].rearrange("a (t p) -> p (a t)", p=P), slow=True)
            load(bsgu[:], A["sgu_b"].rearrange("a g i -> i (a g)"), slow=True)
            load(sg_row[:], A["sgu_norm_gain"][0].partition_broadcast(P))
            load(gn_row[:], A["ret_gn_gain"][0].partition_broadcast(P))
            load(gffn[:], A["norm_ffn_gain"].rearrange("a (k p) -> p (a k)", p=P), slow=True)
            load(gffn_s[:], A["norm_ffn_gain"].rearrange("a (p k) -> p (a k)", p=P))
            load(brt[:, NE:], A["b_router_group"][0].partition_broadcast(P))
            load(brt[:, :NE], A["b_router_expert"][0].rearrange("g e -> (g e)").partition_broadcast(P))
            load(wrt[:, :, NE:], A["w_router_group"][0].rearrange("(k p) g -> p k g", p=P), slow=True)
            for g in range(G):
                load(wrt[:, :, g * EPG:(g + 1) * EPG],
                     A["w_router_expert"][0, g].rearrange("(k p) e -> p k e", p=P), slow=True)
            load(consth[:], A["constants_half"])
            pool.dma_start(gain_row[:], A["final_norm_gain"].partition_broadcast(P)).then_inc(s_gain, 16)
            pool.wait_ge(s_const, 16)
            pool.wait_ge(s_small, SMALL)
            for n in range(2 * NT):
                b, t = divmod(n, NT)
                dst, decay = ((krow, C_KD), (qrow, C_QD))[b]
                pool.wait_ge(s_turned, n + 1)
                own(pool.tensor_tensor(rot[:, n % 2, 0], rot[:, n % 2, 0], rot[:, n % 2, 1], ALU.add))
                own.settle()
                pool.tensor_tensor(dst[:, t], rot[:, n % 2, 0], spread(const[:, decay:decay + H], DH),
                                   ALU.mult).then_inc(s_rot, 1)
            for t in range(NT):
                main.wait_read(pool, (VSB, t))
                pool.tensor_tensor(vsq[:, t], vsrow4[:, t], vsrow4[:, t], ALU.mult).then_inc(s_vsq, 1)
            for t in range(NT):
                pool.wait_ge(s_vn, t + 1)
                pool.tensor_tensor(vsrow[:, t, :], vsrow[:, t, :], sg_row[:], ALU.mult
                                   ).then_inc(s_vg, 1)
            for n in range(NT):
                pool.wait_ge(s_on, n + 1)
                pool.tensor_tensor(orow_flat[:, n, :], orow_flat[:, n, :], gn_row[:], ALU.mult
                                   ).then_inc(s_og, 1)
            main.wait_full(pool, (NB - 1, NT - 1))
            own(pool.memset(xs[0][:], 0.0))
            own(pool.memset(xs[1][:], 0.0))

            pool.wait_ge(s_gates, 1)
            own(pool.tensor_copy(values[:, :, :, 1], gates[:]))
            own.settle()
            own(pool.tensor_tensor(rest[:], gates[:], values[:, :, :, 1], ALU.subtract))
            own.settle()
            own(pool.tensor_scalar(scaled[:, 0], rest[:], GATE_STEP, None, ALU.mult))
            own.settle()
            own(pool.tensor_copy(values[:, :, :, 2], scaled[:, 0]))
            own.settle()
            own(pool.tensor_tensor(scaled[:, 1], scaled[:, 0], values[:, :, :, 2], ALU.subtract))
            own.settle()
            pool.tensor_scalar(values[:, :, :, 3], scaled[:, 1], GATE_STEP, None, ALU.mult
                               ).then_inc(s_values, 1)

            def gather(dst, rows, sem):
                pool.indirect_dma_start(
                    out=dst, out_offset=None, in_=hx_rows[:, :],
                    in_offset=bass.IndirectOffsetOnAxis(ap=rows, axis=0),
                    bounds_check=S - 1, oob_is_err=False).then_inc(sem, 16)

            def gather_pair(r, q):
                at_least(pool, s_rowof, r, GP, q + 1)
                at_least(pool, s_tr, r, 2 * GP, 2 * (q - GP + 1))
                pool.sem_inc(s_turn, 1)
                gather(xs[q % GP][:], row_of[:, q % GP, :], s_xs[q % GP])

            pool.wait_ge(s_hxout, 16 * NT)
            own.settle()
            gather_pair(0, 0)
            gather_pair(0, 1)
            own(pool.memset(xs[2][:], 0.0))
            own.settle()
            gather_pair(0, 2)

            def group(r, pairs):
                for q in range(pairs):
                    if comes(r, q + 3):
                        gather_pair(r, q + 3)

            group_loop(pool, group)
            with if_crowded(pool):
                pool.wait_ge(s_added, SUMS * NPAIR)
                with pool.Fori(0, NE * NWIN) as n:
                    pool.wait_ge(g_rowof, n + 1)
                    pool.sem_inc(s_turn, 1)
                    gather(xs[0][0:WIN, :], row_of[0:WIN, 0, :], g_xs)
                pool.wait_ge(g_xs, 16 * NE * NWIN)

        @block.vector
        def _(dve):
            own = Chain(dve, c_dve)

            def rstd(kind, t, sds):
                dve.wait_ge(s_sd, sds)
                return dve.reciprocal(stat[:, 3 * kind + 2, t], stat[:, 3 * kind + 1, t])

            def rstd_of(kind, t):
                return stat[:, 3 * kind + 2, t:t + 1]

            def w_low(g):
                b, k = STEPS[g]
                dve.wait_ge(s_whi, g + 1)
                dst, raw, high = w_lo[:, g % RAW, :], w_raw[:, g % RAW, :], w_hi[:, g % RAW, :]
                if b < NB_IN:
                    ins = dve.scalar_tensor_tensor(dst, raw, gmix[:, k:k + 1], high.bitcast(F32),
                                                   ALU.mult, ALU.subtract)
                else:
                    ins = dve.tensor_tensor(dst, raw, high.bitcast(F32), ALU.subtract)
                ins.then_inc(s_wlo, 1)

            made = [0]

            def transposed_low(name, hi, lo, t, half):
                item = (name, t, half)
                made[0] += 1
                dve.wait_ge(s_thi, made[0])
                at = (slice(None), half_rows(half), tokens(t))
                dve.tensor_tensor(lo[at], heads(banks_of(item).bank(item)), hi[at].bitcast(F32),
                                  ALU.subtract).then_inc(banks_of(item).done(item), 1)

            def normalise(t):
                own(rstd(0, slice(t, t + 1), t + 1))
                own.settle()
                dve.tensor_scalar(hrow[:, t % 2, :], x[:, t, :], rstd_of(0, t), None, ALU.mult
                                  ).then_inc(s_h, 1)

            normalise(0)
            normalise(1)
            for t in range(NT):
                if t == NT - 1:
                    dve.wait_ge(s_gmix, 16)
                    w_low(0)
                    w_low(1)
                for half in range(2):
                    transposed_low("hT", hT_hi, hT_lo, t, half)
                if t + 2 < NT:
                    normalise(t + 2)

            w_low(2)
            w_low(3)

            dve.wait_ge(s_small, SMALL)
            own(dve.tensor_copy(pos_f[:], pos_i[:]))
            own.settle()
            for c in range(2):
                for t in range(NT):
                    own(dve.tensor_scalar(ang[:, 0, c, t, :], const[:, C_FREQ:C_FREQ + HALF],
                                          pos_f[:, t:t + 1], None, ALU.mult))
            own.settle()
            for c in range(2):
                own(dve.tensor_scalar(ang[:, 1, c], ang[:, 0, c], 1 / (2 * np.pi), 0.25 * c,
                                      ALU.mult, ALU.add))
            own.settle()
            own(dve.tensor_scalar(ang[:, 1], ang[:, 1], MAGIC, MAGIC, ALU.add, ALU.subtract))
            for part in TWO_PI:
                own.settle()
                own(dve.scalar_tensor_tensor(flat(ang[:, 0]), flat(ang[:, 1]), -part, flat(ang[:, 0]),
                                             ALU.mult, ALU.add))
            own.settle()
            own(dve.tensor_scalar(ang[:, 0, 1], ang[:, 0, 1], np.pi / 2, None, ALU.add))
            own.settle()
            dve.tensor_scalar(ang[:, 0], ang[:, 0], PI_BELOW, -PI_BELOW, ALU.min, ALU.max
                              ).then_inc(s_ang, 1)

            dve.tensor_tensor(wrt[:], wrt[:], spread(gffn[:], NE + G), ALU.mult).then_inc(s_wrt, 1)
            own(dve.memset(logit[:, :, NE + G:], NEG))
            for pick in range(TOPK):
                own(dve.tensor_copy(values[:, pick, :, 0], consth[:, H_TOKEN:H_TOKEN + NT]))

            def rotate(b, t):
                n = NT * b + t
                main.wait_read(dve, (b, t))
                if n >= 2:
                    dve.wait_ge(s_rot, n - 1)
                whole = qk_row[:, t, :].rearrange("p (x c) -> p x c", c=HALF)
                row = qk_row[:, t, :].rearrange("p (h two c) -> p h two c", two=2, c=HALF)
                a = rot[:, n % 2, 0].rearrange("p h (two c) -> p (h two) c", two=2)
                z = rot[:, n % 2, 1].rearrange("p h (two c) -> p h two c", two=2)
                sin, cos = trig[:, 0, t, :], trig[:, 1, t, :]
                dve.tensor_tensor(a, whole, along(cos, 2 * H), ALU.mult)
                dve.scalar_tensor_tensor(z[:, :, 0, :], row[:, :, 1, :], -1.0, along(sin, H),
                                         ALU.mult, ALU.mult)
                dve.tensor_tensor(z[:, :, 1, :], row[:, :, 0, :], along(sin, H), ALU.mult
                                  ).then_inc(s_turned, 1)

            def mask(n):
                aux.wait_full(dve, ("scores", n))
                dve.tensor_tensor(scT[:, n % 2], heads(aux.bank(("scores", n))), along(causal, H),
                                  ALU.mult).then_inc(aux.done(("scores", n)), 1)

            def next_state(n):
                aux.wait_full(dve, ("kv", n))
                kv, decay = heads(aux.bank(("kv", n))), spread(const[:, C_CD:C_CD + H], DH)
                if n:
                    own(dve.tensor_tensor(kvt[:], kv, state[:, n % 2], ALU.add))
                    own.settle()
                    kv = kvt[:]
                dve.tensor_tensor(state[:, (n + 1) % 2], kv, decay, ALU.mult
                                  ).then_inc(aux.done(("kv", n)), 1)

            def variance(n):
                aux.wait_read(dve, ("o", n))
                for h in range(H):
                    own(dve.bn_stats(gnstat[:, n, h, :], orow[:, n, h, :]))
                own.settle()
                for h in range(H):
                    ins = dve.bn_aggr(gnaggr[:, n, h, :], gnstat[:, n, h, :])
                    if n == NT - 1 and h == H - 1:
                        ins.then_inc(s_gnv, 1)

            def gate_tokens(t):
                item = ("gating", t)
                aux.wait_full(dve, item)
                main.wait_read(dve, (UB, t))
                for g in range(G):
                    u = urow[:, t, g * P:(g + 1) * P]
                    ins = dve.scalar_tensor_tensor(u, aux.bank(item)[:, g * P:(g + 1) * P],
                                                   bsgu[:, g:g + 1], u, ALU.add, ALU.mult)
                ins.then_inc(aux.done(item), 1)

            def residual(c):
                for t in range(NT):
                    item = (NB_IN + c, t)
                    main.wait_full(dve, item)
                    part = x[:, t, c * R:(c + 1) * R]
                    dve.tensor_tensor(part, main.bank(item)[:, :], part, ALU.add
                                      ).then_inc(main.done(item), 1)

            for g in range(4, NSTEP):
                w_low(g)
                if g == 6:
                    aux.wait_full(dve, ("wT",))
                    dve.tensor_tensor(wT[:], heads(aux.bank(("wT",))), along(causal, G), ALU.mult
                                      ).then_inc(aux.done(("wT",)), 1)
                if g == 11:
                    dve.wait_ge(s_trig, 1)
                if 11 <= g < 11 + NT or 19 <= g < 19 + NT:
                    rotate((g - 11) // ND, (g - 11) % ND)
                for n in range(NT):
                    if g == 32 + 3 * n:
                        mask(n)
                        if n < NT - 1:
                            next_state(n)
                    if g == 35 + 3 * n:
                        variance(n)
                if g == 37:
                    dve.wait_ge(s_vsq, NT)
                    dve.tensor_reduce(vss[:, 0], vsq[:], AX, ALU.add).then_inc(s_vss, 1)
                if g == 39:
                    dve.wait_ge(s_vsd, 1)
                    own(dve.reciprocal(vss[:, 2], vss[:, 1]))
                    own.settle()
                    for t in range(NT):
                        dve.tensor_tensor(vsrow4[:, t], vsrow4[:, t], spread(vss[:, 2, t, :], P),
                                          ALU.mult).then_inc(s_vn, 1)
                for t, step in enumerate((45, 46, 47, 48)):
                    if g == step:
                        gate_tokens(t)
                if g == 49:
                    dve.wait_ge(s_gnd, 1)
                    own(dve.reciprocal(gnrs[:, 1], gnrs[:, 0]))
                    own.settle()
                    for n in range(NT):
                        for h in range(H):
                            row = orow[:, n, h, :]
                            ins = dve.tensor_scalar(row, row, gnaggr[:, n, h, 0:1],
                                                    gnrs[:, 1, n, h:h + 1], ALU.subtract, ALU.mult)
                        ins.then_inc(s_on, 1)
                if g == 51:
                    for t in range(NT):
                        transposed_low("mT", mT_hi, mT_lo, t, 1)
                    for t in range(NT):
                        main.wait_read(dve, (GB, t))
                        dve.wait_ge(s_og, t + 1)
                        dve.tensor_tensor(grow[:, t, :], grow[:, t, :], orow_flat[:, t, :], ALU.mult
                                          ).then_inc(s_mix, 1)
                if g == 52:
                    for t in range(NT):
                        transposed_low("mT", mT_hi, mT_lo, t, 0)
                if g == 59:
                    residual(0)
            dve.wait_ge(s_hss, NT)
            dve.tensor_scalar(half_ss[:, 2], half_ss[:, 0], 1.0 / D, EPS, ALU.mult, ALU.add
                              ).then_inc(s_hbias, 1)
            residual(1)
            rstd(1, slice(0, NT), 2 * NT).then_inc(s_rstd, 1)

            dve.wait_ge(s_rstd, 1)
            for t in range(NT):
                main.wait_full(dve, ("logits", t))
                own(dve.scalar_tensor_tensor(logit[:, t, 0:NE + G],
                                             main.bank(("logits", t))[:, 0:NE + G], rstd_of(1, t),
                                             brt[:], ALU.mult, ALU.add))
            own.settle()
            glog, elog = logit[:, :, NE:], logit[:, :, 0:NE].rearrange("p t (g e) -> p t g e", g=G)
            for t in range(NT):
                own(dve.max(gtop[:, t, :], glog[:, t, :]))
            own.settle()
            for t in range(NT):
                own(dve.max_index(gidx[:, t, :], gtop[:, t, :], glog[:, t, :]))
            own.settle()
            own(dve.tensor_tensor(gsel[:], along(const[:, C_I32:C_I32 + G], NT),
                                  spread(gidx[:, :, 0], G), ALU.is_equal))
            own.settle()
            own(dve.tensor_tensor(emul[:], elog, spread(gsel[:], EPG), ALU.mult))
            own.settle()
            own(dve.tensor_reduce(slog[:], emul[:].rearrange("p t g e -> p t e g"), AX, ALU.add))
            own.settle()
            for t in range(NT):
                own(dve.max(etop[:, t, :], slog[:, t, :]))
            own.settle()
            for t in range(NT):
                own(dve.max_index(eidx[:, t, :], etop[:, t, :], slog[:, t, :]))
            own.settle()
            own(dve.scalar_tensor_tensor(eid[:], spread(gidx[:, :, 0], TOPK), float(EPG),
                                         eidx[:, :, 0:TOPK], ALU.mult, ALU.add))
            own.settle()
            own(dve.tensor_tensor(pairs[:].rearrange("p t k e -> p (t k) e"),
                                  along(const[:, C_I32:C_I32 + NE], NT * TOPK),
                                  spread(eid[:].rearrange("p t k -> p (t k)"), NE), ALU.is_equal))
            own.settle()
            dve.tensor_tensor(picked[:], pairs[:, :, 0], pairs[:, :, 1], ALU.add
                              ).then_inc(s_pick, 1)
            dve.tensor_tensor(gsub[:], glog[:, :, 0:G], spread(gtop[:, :, 0], G), ALU.subtract
                              ).then_inc(s_arg, 1)
            dve.tensor_tensor(esub[:], etop[:, :, 1], etop[:, :, 0], ALU.subtract).then_inc(s_arg, 1)

            dve.wait_ge(s_exp, 2)
            own(dve.tensor_reduce(gden[:], gexp[:], AX, ALU.add))
            own(dve.tensor_scalar(eden[:], e2[:], 1.0, None, ALU.add))
            own.settle()
            own(dve.tensor_tensor(eden[:], eden[:], gden[:], ALU.mult))
            own.settle()
            own(dve.reciprocal(gates[:, 0, :], eden[:]))
            own.settle()
            dve.tensor_tensor(gates[:, 1, :], gates[:, 0, :], e2[:], ALU.mult).then_inc(s_gates, 1)

            ranks = ("ranks",)
            main.wait_full(dve, ranks)
            rank = main.bank(ranks)[:, 0:NT * NE].rearrange("p (t e) -> p t e", t=NT)
            total = main.bank(ranks)[:, NT * NE:(NT + 1) * NE]
            own(dve.tensor_tensor(spick[:], pairs[:], rank.unsqueeze(2).broadcast_to([P, NT, TOPK, NE]),
                                  ALU.mult))
            own.settle()
            own(dve.tensor_reduce(place_of[:], spick[:], AX, ALU.add))
            own.settle()

            def one_hots(width, src, sem):
                for t in range(NT):
                    for pick in range(TOPK):
                        ins = dve.tensor_scalar(onehot[:, pick, t, 0:width],
                                                consth[:, H_PLACE:H_PLACE + width],
                                                src[:, t, pick:pick + 1], None, ALU.is_equal)
                ins.then_inc(sem, 1)

            def hot(r, q):
                first = isinstance(r, int) and GP * r + q == 0
                at_least(dve, s_moved, r, GP, q)
                at_least(dve, s_ids, r, GP, q)
                src = place_of if first else place_on
                one_hots(P, src, s_hot)
                at_least(dve, s_hot, r, GP, q + 1)
                dve.tensor_scalar(place_on[:], src[:], -2.0 * RANKS, None, ALU.add
                                  ).then_inc(s_moved, 1)

            def numbers(i, width, row, read):
                got = ids_bank[0:width, NUMBERS:NUMBERS + 4]
                dve.tensor_scalar(row_of[0:width, i, :], got[:, 0:1], float(UNUSED), None, ALU.add
                                  ).then_inc(row, 1)
                dve.tensor_copy(summed[0:width, i, :], got).then_inc(read, 1)

            def current(i, wait, width, part, gate):
                dve.tensor_scalar(token_of[0:width, :], summed[0:width, i, 0:1], float(UNUSED),
                                  None, ALU.add)
                dve.scalar_tensor_tensor(gate_rest[0:width, :], summed[0:width, i, 3:4],
                                         1 / GATE_STEP, summed[0:width, i, 2:3], ALU.mult, ALU.add
                                         ).then_inc(part, 1)
                wait(part)
                dve.scalar_tensor_tensor(gate_of[0:width, :], gate_rest[0:width, :],
                                         1 / GATE_STEP, summed[0:width, i, 1:2], ALU.mult, ALU.add
                                         ).then_inc(gate, 1)

            def pair_numbers(r, q):
                at_least(dve, s_ids, r, GP, q + 1)
                at_least(dve, s_slotv, r, GP, q - GP + 1)
                at_least(dve, s_tr, r, 2 * GP, 2 * (q - GP + 1))
                numbers(q % GP, P, s_rowof, s_summed)

            def pair_current(r, q):
                at_least(dve, s_ylo, r, 2 * GP, 2 * q)
                at_least(dve, s_summed, r, GP, q + 1)
                current(q % GP, lambda sem: at_least(dve, sem, r, GP, q + 1), P, s_gpart, s_slotv)

            hot(0, 0)
            pair_numbers(0, 0)
            own(dve.tensor_reduce(most[:], total, AX, ALU.max))
            own.settle()
            dve.tensor_scalar(crowded[:], most[:], float(WIN), None, ALU.is_gt).then_inc(s_crowd, 1)
            hot(0, 1)
            pair_numbers(0, 1)

            def gained(half, width, sem):
                ps = half_bank[half][:, 0:4 * P].rearrange("p (k w) -> p k w", k=4)[:, :, 0:width]
                dve.tensor_tensor(xsT[:, half_rows(half), 0:width], ps,
                                  spread(gffn_s[:, half_rows(half)], width), ALU.mult).then_inc(sem, 1)

            def gained_pair(r, q):
                at_least(dve, s_gu, r, GP, q)
                for half in range(2):
                    at_least(dve, s_tr, r, 2 * GP, 2 * q + half + 1)
                    gained(half, P, s_xsT)

            def multiply(r, q):
                at_least(dve, s_silu, r, GP, q + 1)
                dve.tensor_tensor(acts[:], silu_g[:], gate_up_bank[:, FF:2 * FF], ALU.mult
                                  ).then_inc(s_act, 1)

            def transposed_acts(r, q):
                at_least(dve, s_at, r, GP, q + 1)
                dve.tensor_copy(actT[:], act_bank[:, 0:NF * P].rearrange("p (j w) -> p j w", j=NF)
                                ).then_inc(s_actT, 1)

            def spreading(width, sem):
                dve.tensor_scalar(spread_to[0:width, :], consth[0:width, H_NUMBER:H_NUMBER + S],
                                  token_of[0:width, 0:1], None, ALU.is_equal).then_inc(sem, 1)

            def gated_low(c, width, sem):
                half = slice(c * R, (c + 1) * R)
                dve.scalar_tensor_tensor(y_lo[0:width, half], down_bank[c][0:width, :],
                                         gate_of[0:width, 0:1], y_hi[0:width, half].bitcast(F32),
                                         ALU.mult, ALU.subtract).then_inc(sem, 1)

            def gate_pair(r, q):
                at_least(dve, s_sum, r, SUMS * GP, SUMS * q)
                spreading(P, s_spread)
                for c in range(2):
                    at_least(dve, s_yhi, r, 2 * GP, 2 * q + c + 1)
                    gated_low(c, P, s_ylo)

            def add(i, sem, banks=sum_bank):
                c, t = divmod(i, NT)
                to = x[:, t, c * R:(c + 1) * R]
                dve.tensor_tensor(to, banks[i % len(banks)][:, :], to, ALU.add).then_inc(sem, 1)

            def add_pair(r, q, first=0, last=SUMS, banks=sum_bank):
                for i in range(first, last):
                    at_least(dve, s_sum, r, SUMS * GP, SUMS * q + i + 1)
                    add(i, s_added, banks)

            def group(r, pairs):
                for q in range(pairs):
                    pair_current(r, q)
                    if comes(r, q + 3):
                        pair_numbers(r, q + 3)
                    if not isinstance(r, int) or r + q:
                        add_pair(r, q - 1, 0, EARLY_SUMS)
                    multiply(r, q)
                    if not isinstance(r, int) or r + q:
                        add_pair(r, q - 1, EARLY_SUMS, SUMS)
                    transposed_acts(r, q)
                    if comes(r, q + 1):
                        gained_pair(r, q + 1)
                    if comes(r, q + 4):
                        hot(r, q + 4)
                    gate_pair(r, q)

            gained_pair(0, 0)
            hot(0, 2)
            pair_numbers(0, 2)
            hot(0, 3)
            group_loop(dve, group)
            add_pair(NGROUP - 1, LAST - 1, banks=last_sum_bank)
            with if_crowded(dve):
                prep = Chain(dve, g_prep)
                dve.wait_ge(s_added, SUMS * NPAIR)
                prep(dve.scalar_tensor_tensor(used[:], eid[:], -float(RANKS), place_of[:],
                                              ALU.mult, ALU.add))
                prep.settle()
                prep(dve.tensor_scalar(used[:], used[:], float(WIN), None, ALU.is_ge))
                prep(dve.tensor_scalar(place_on[:], place_of[:], 1.0, None, ALU.add))
                prep.settle()
                prep(dve.tensor_tensor(place_on[:], place_on[:], used[:], ALU.mult))
                prep.settle()
                dve.tensor_scalar(place_on[:], place_on[:], -1.0, None, ALU.add).then_inc(g_moved, 1)
                with dve.Fori(0, NE * NWIN) as n:
                    dve.wait_ge(g_moved, n + 1)
                    one_hots(WIN, place_on, g_hot)
                    dve.wait_ge(g_hot, n + 1)
                    dve.tensor_scalar(place_on[:], place_on[:], -float(WIN), None, ALU.add
                                      ).then_inc(g_moved, 1)
                    dve.wait_ge(g_ids, n + 1)
                    numbers(0, WIN, g_rowof, g_summed)
                    dve.wait_ge(g_summed, n + 1)
                    current(0, lambda sem: dve.wait_ge(sem, n + 1), WIN, g_gpart, g_slotv)
                    spreading(WIN, g_spread)
                    for half in range(2):
                        dve.wait_ge(g_tr, n * 2 + (half + 1))
                        gained(half, WIN, g_xsT)
                    dve.wait_ge(g_silu, n + 1)
                    dve.tensor_tensor(acts[0:WIN, :], silu_g[0:WIN, :], gate_up_bank[0:WIN, FF:2 * FF],
                                      ALU.mult).then_inc(g_act, 1)
                    dve.wait_ge(g_at, n + 1)
                    dve.tensor_copy(actT[:], act_bank[:, 0:NF * P].rearrange("p (j w) -> p j w", j=NF)
                                    ).then_inc(g_actT, 1)
                    for c in range(2):
                        dve.wait_ge(g_yhi, n * 2 + (c + 1))
                        gated_low(c, WIN, g_ylo)
                    for i in range(SUMS):
                        dve.wait_ge(g_sum, n * SUMS + (i + 1))
                        add(i, g_added)

            dve.wait_ge(s_gain, 16)

            dve.wait_ge(s_hss, 3 * NT)
            dve.tensor_scalar(half_ss[:, 5], half_ss[:, 3], 1.0 / D, EPS, ALU.mult, ALU.add
                              ).then_inc(s_hbias, 1)
            for t in range(NT):
                rstd(2, slice(t, t + 1), 2 * NT + t + 1).then_inc(s_rstd2, 1)
                dve.wait_ge(s_rstd2, t + 1)
                dve.scalar_tensor_tensor(outrow[:, t, :], x[:, t, :], rstd_of(2, t), gain_row[:],
                                         ALU.mult, ALU.mult).then_inc(s_out, 1)

        @block.tensor
        def _(pe):
            def transposes(item, chunks, last=None):
                for i, chunk in enumerate(chunks):
                    ins = pe.transpose(banks_of(item).bank(item)[:, i * P:(i + 1) * P], chunk, ident)
                ins.then_inc(banks_of(item).filled(item), 1)

            def every_kth(row, half):
                cols = row[:].rearrange("p (q k) -> p k q", k=ND)
                return [cols[:, 4 * half + i, :] for i in range(4)]

            def head_products(item, left, right):
                for h in range(H):
                    ins = pe.matmul(aux.bank(item)[:, h * P:(h + 1) * P], left(h), right(h),
                                    start=True, stop=True)
                ins.then_inc(aux.filled(item), 1)

            def do(item):
                name, *at = item
                if name not in ("logits", "ranks"):
                    banks_of(item).wait_free(pe, item)
                if name == "hT":
                    t, half = at
                    pe.wait_ge(s_h, t + 1)
                    transposes(item, [hrow[:, t % 2, (4 * half + i) * P:(4 * half + i + 1) * P]
                                      for i in range(4)])
                elif name == "wT":
                    pe.wait_ge(s_sgw, 16)
                    transposes(item, [wsraw[:, g, :] for g in range(G)])
                elif name in ("kT", "qT"):
                    t, = at
                    src, b = (krow, 0) if name == "kT" else (qrow, 1)
                    pe.wait_ge(s_rot, NT * b + t + 1)
                    transposes(item, [src[:, t, h, :] for h in range(H)])
                elif name == "scores":
                    n, = at
                    aux.wait_read(pe, ("kT", n))
                    aux.wait_read(pe, ("qT", n))
                    head_products(item, lambda h: kT[:, h, tokens(n)], lambda h: qT[:, h, tokens(n)])
                elif name == "kv":
                    n, = at
                    main.wait_read(pe, (VB, n))
                    head_products(item, lambda h: krow[:, n, h, :], lambda h: vrow[:, n, h, :])
                elif name == "o":
                    n, = at
                    main.wait_read(pe, (VB, n))
                    aux.wait_read(pe, ("scores", n))
                    if n:
                        aux.wait_read(pe, ("kv", n - 1))
                    for h in range(H):
                        dst = aux.bank(item)[:, h * P:(h + 1) * P]
                        ins = pe.matmul(dst, scT[:, n % 2, h, :], vrow[:, n, h, :],
                                        start=True, stop=(n == 0))
                        if n:
                            ins = pe.matmul(dst, qT[:, h, tokens(n)], state[:, n % 2, h, :],
                                            start=False, stop=True)
                    ins.then_inc(aux.filled(item), 1)
                elif name == "gating":
                    t, = at
                    aux.wait_read(pe, ("wT",))
                    pe.wait_ge(s_vg, t + 1)
                    head_products(item, lambda g: wT[:, g, :],
                                  lambda g: vsrow[:, t, g * P:(g + 1) * P])
                elif name == "mT":
                    t, half = at
                    if half:
                        aux.wait_read(pe, ("gating", t))
                    else:
                        pe.wait_ge(s_mix, t + 1)
                    src = urow if half else grow
                    transposes(item, [src[:, t, i * P:(i + 1) * P] for i in range(4)])
                elif name == "xT":
                    t, half = at
                    main.wait_read(pe, (NB - 2 + half, t))
                    transposes(item, [x[:, t, (4 * half + i) * P:(4 * half + i + 1) * P]
                                      for i in range(4)])
                elif name == "logits":
                    t, half = at
                    if half == 0:
                        main.wait_free(pe, ("logits", t))
                        pe.wait_ge(s_wrt, 1)
                    aux.wait_read(pe, ("xT", t, half))
                    dst = main.bank(("logits", t))[:, 0:NE + G]
                    for k in range(4 * half, 4 * half + 4):
                        ins = pe.matmul(dst, xT[:, k, tokens(t)], wrt[:, k, :],
                                        start=(k == 0), stop=(k == ND - 1))
                    if half:
                        ins.then_inc(main.filled(("logits", t)), 1)
                elif name == "ranks":
                    main.wait_free(pe, item)
                    pe.wait_ge(s_pick, 1)
                    for t in range(NT):
                        dst = main.bank(item)[:, t * NE:(t + 1) * NE]
                        pe.matmul(dst, ones, consth[:, H_BASE:H_BASE + NE], start=True, stop=False)
                        for c in range(t + 1):
                            pe.matmul(dst, before if c == t else ones, picked[:, c, :],
                                      start=False, stop=(c == t))
                    for c in range(NT):
                        ins = pe.matmul(main.bank(item)[:, NT * NE:(NT + 1) * NE], ones,
                                        picked[:, c, :], start=(c == 0), stop=(c == NT - 1))
                    ins.then_inc(main.filled(item), 1)

            def step(g, chunks=range(NT)):
                b, k = STEPS[g]
                high, low = (hT_hi, hT_lo) if b < NB_IN else (mT_hi, mT_lo)
                first, last = g % ND == 0, g % ND == ND - 1
                pe.wait_ge(s_wlo, g + 1)
                for t in chunks:
                    if g == NB_IN * ND or g == NB_IN * ND + 4:
                        aux.wait_read(pe, ("mT", t, int(g == NB_IN * ND)))
                    if first:
                        main.wait_free(pe, (b, t))
                    dst = main.bank((b, t))[:, :]
                    slot = g % RAW
                    pe.matmul(dst, high[:, k, tokens(t)], w_hi[:, slot, :], start=first, stop=False)
                    pe.matmul(dst, high[:, k, tokens(t)], w_lo[:, slot, :], start=False, stop=False)
                    ins = pe.matmul(dst, low[:, k, tokens(t)], w_hi[:, slot, :],
                                    start=False, stop=last)
                    if last:
                        ins.then_inc(main.filled((b, t)), 1)
                    elif t == NT - 1:
                        ins.then_inc(s_step, 1)

            pe.wait_ge(s_const, 16)
            todo = list(beside)
            for g in range(-1, NSTEP + 1):
                if g == 0:
                    for t in range(NT - 2, NT):
                        for half in range(2):
                            early.wait_read(pe, ("hT", t, half))
                if 0 <= g < NSTEP and g % ND == 0:
                    for chunks in (range(0, 2), range(2, NT)):
                        step(g, chunks)
                        step(g + 1, chunks)
                elif 0 <= g < NSTEP and g % ND > 1:
                    step(g)
                while todo and todo[0][0] == g:
                    do(todo.pop(0)[1])

            def row_sums(width, sem):
                for pick in range(TOPK):
                    for t in range(NT):
                        ins = pe.matmul(ids_bank[0:width, NUMBERS:NUMBERS + 4],
                                        onehot[:, pick, t, 0:width], values[:, pick, t, :],
                                        start=(pick + t == 0),
                                        stop=(pick == TOPK - 1 and t == NT - 1))
                ins.then_inc(sem, 1)

            def window_half(xs, half, sem):
                for i, cols in enumerate(every_kth(xs, half)):
                    ins = pe.transpose(half_bank[half][:, i * P:(i + 1) * P], cols, ident)
                ins.then_inc(sem, 1)

            def gate_up(slots, between=lambda k: None):
                for k in range(ND):
                    for i, slot in enumerate(slots):
                        half = slice(i * WIN, (i + 1) * WIN)
                        ins = pe.matmul(gate_up_bank[half, :], xsT[:, k, half],
                                        wgu[slot][:, k].rearrange("p w f -> p (w f)"),
                                        start=(k == 0), stop=(k == ND - 1))
                    if k < ND - 1:
                        between(k)
                return ins

            def token_sums(i, width, sem, banks=sum_bank):
                c, t = divmod(i, NT)
                for y in (y_hi, y_lo):
                    ins = pe.matmul(banks[i % len(banks)][:, :], spread_to[0:width, tokens(t)],
                                    y[0:width, c * R:(c + 1) * R], start=(y is y_hi),
                                    stop=(y is y_lo))
                ins.then_inc(sem, 1)

            def transposed_acts(sem):
                cols = acts[:].rearrange("p (q j) -> p j q", j=NF)
                for j in range(NF):
                    ins = pe.transpose(act_bank[:, j * P:(j + 1) * P], cols[:, j, :], ident)
                ins.then_inc(sem, 1)

            def down(slots, sem):
                for c in range(2):
                    for f in range(NF):
                        for i, slot in enumerate(slots):
                            half = slice(i * WIN, (i + 1) * WIN)
                            ins = pe.matmul(down_bank[c][half, :], actT[:, f, half],
                                            wd[slot][:, f, c * R:(c + 1) * R],
                                            start=(f == 0), stop=(f == NF - 1))
                    ins.then_inc(sem, 1)

            def pair_rows(r, q):
                at_least(pe, s_hot, r, GP, q + 1)
                at_least(pe, s_summed, r, GP, q)
                if isinstance(r, int) and r + q == 0:
                    pe.wait_ge(s_values, 1)
                row_sums(P, s_ids)

            def pair_sum(r, q, i, banks=sum_bank):
                at_least(pe, s_spread, r, GP, q + 1)
                at_least(pe, s_ylo, r, 2 * GP, 2 * q + i // NT + 1)
                before = i - 1 if banks is sum_bank else max(i - len(banks) + 1, 0)
                at_least(pe, s_added, r, SUMS * GP, SUMS * q + before)
                token_sums(i, P, s_sum, banks)

            def pair_half(r, q, half):
                at_least(pe, s_xs[q % GP], r, 16, 16 * (q // GP + 1))
                at_least(pe, s_xsT, r, 2 * GP, 2 * q - 1 + half)
                window_half(xs[q % GP], half, s_tr)

            def pair_gate_up(r, q):
                at_least(pe, s_xsT, r, 2 * GP, 2 * q + 2)
                at_least(pe, s_act, r, GP, q)
                at_least(pe, s_wgu[q % GP], r, 64, 64 * (q // GP + 1))

                def between(k):
                    if k == 1 and comes(r, q + 3) and (not isinstance(r, int) or r + q):
                        pair_rows(r, q + 3)
                    if 3 <= k < 3 + EARLY_SUMS // 2 and (not isinstance(r, int) or r + q):
                        for i in (2 * (k - 3), 2 * (k - 3) + 1):
                            pair_sum(r, q - 1, i)

                gate_up((2 * q % RING, 2 * q % RING + 1), between).then_inc(s_gu, 1)
                if isinstance(r, int) and r + q == 0:
                    pair_rows(0, 2)
                    pair_rows(0, 3)

            def pair_down(r, q):
                if not isinstance(r, int) or r + q:
                    for i in range(EARLY_SUMS, SUMS):
                        pair_sum(r, q - 1, i)
                at_least(pe, s_act, r, GP, q + 1)
                transposed_acts(s_at)
                if comes(r, q + 1):
                    pair_half(r, q + 1, 0)
                    pair_half(r, q + 1, 1)
                at_least(pe, s_wd[q % GP], r, 32, 32 * (q // GP + 1))
                at_least(pe, s_actT, r, GP, q + 1)
                at_least(pe, s_ylo, r, 2 * GP, 2 * q)
                down((2 * q % RING, 2 * q % RING + 1), s_down)

            def group(r, pairs):
                for q in range(pairs):
                    pair_gate_up(r, q)
                    pair_down(r, q)

            pair_rows(0, 0)
            pair_rows(0, 1)
            pair_half(0, 0, 0)
            pair_half(0, 0, 1)
            pe.wait_ge(s_crowd, 1)
            group_loop(pe, group)
            for i in range(SUMS):
                pair_sum(NGROUP - 1, LAST - 1, i, last_sum_bank)
            with if_crowded(pe):
                pe.wait_ge(s_added, SUMS * NPAIR)
                with pe.Fori(0, NE) as e:
                    with pe.Fori(0, NWIN) as w:
                        n = e * NWIN + w
                        pe.wait_ge(g_hot, n + 1)
                        row_sums(WIN, g_ids)
                        pe.wait_ge(g_xs, n * 16 + 16)
                        window_half(xs[0], 0, g_tr)
                        window_half(xs[0], 1, g_tr)
                        pe.wait_ge(g_xsT, n * 2 + 2)
                        pe.wait_ge(g_w, e * 48 + 48)
                        gate_up((0,)).then_inc(g_gu, 1)
                        pe.wait_ge(g_act, n + 1)
                        transposed_acts(g_at)
                        pe.wait_ge(g_actT, n + 1)
                        down((0,), g_down)
                        pe.wait_ge(g_spread, n + 1)
                        pe.wait_ge(g_ylo, n * 2 + 2)
                        for i in range(SUMS):
                            if i >= 2:
                                pe.wait_ge(g_added, n * SUMS + (i - 1))
                            token_sums(i, WIN, g_sum)
                        pe.wait_ge(g_added, n * SUMS + SUMS)


def kernel(**inputs):
    from concourse import bacc
    from concourse.bass_utils import run_bass_kernel_spmd

    nc = bacc.Bacc("TRN2", target_bir_lowering=False, num_devices=1)
    wide, half = constants()
    arrays = {"in_" + n: np.ascontiguousarray(inputs[n]) for n in INPUTS}
    arrays["in_constants"], arrays["in_constants_half"] = wide, half
    A = {n[3:]: nc.dram_tensor(n, a.shape, mybir.dt.from_np(a.dtype), kind="ExternalInput").ap()
         for n, a in arrays.items()}
    out = nc.dram_tensor("out", (1, S, D), F32, kind="ExternalOutput").ap()
    build(nc, A, out)
    r = run_bass_kernel_spmd(nc, [arrays], core_ids=[0])
    return r.results[0]["out"]
```
